# Optimizing a Trainium2 kernel written in Bass

```python
import jax, jax.numpy as jnp
from jax import lax
import numpy as np
import math

D_MODEL = 2048
BATCH = 1
SEQ = 256
DEPTH = 1

CONV_CH = 1024
CONV_K = 31
N_HEADS = 8
QK_NOPE = 128
QK_ROPE = 64
V_HEAD = 128
QK_HEAD = QK_NOPE + QK_ROPE
Q_LORA = 768
KV_LORA = 512
ATTN_CH = N_HEADS * V_HEAD
MIX_WIDTH = CONV_CH + ATTN_CH
IN_COLS = 2 * CONV_CH + Q_LORA + KV_LORA + QK_ROPE
ROPE_THETA = 10000.0
Q_BLOCK = 128
D_FF = ((8 * D_MODEL // 3 + 255) // 256) * 256
EPS = 1e-6


def rmsnorm(x, g):
    xf = x.astype(jnp.float32)
    y = xf * lax.rsqrt(jnp.mean(xf * xf, axis=-1, keepdims=True) + EPS)
    return (y * g.astype(jnp.float32)).astype(x.dtype)

def layernorm(x, g, b):
    xf = x.astype(jnp.float32)
    mu = jnp.mean(xf, axis=-1, keepdims=True)
    var = jnp.mean(jnp.square(xf - mu), axis=-1, keepdims=True)
    y = (xf - mu) * lax.rsqrt(var + EPS)
    return (y * g.astype(jnp.float32) + b.astype(jnp.float32)).astype(x.dtype)

def rope_tables(positions, dtype):
    inv_freq = ROPE_THETA ** (-jnp.arange(0, QK_ROPE, 2, dtype=jnp.float32) / QK_ROPE)
    ang = positions.astype(jnp.float32)[..., None] * inv_freq
    return jnp.cos(ang).astype(dtype), jnp.sin(ang).astype(dtype)

def apply_rope(x, cos, sin):
    x1, x2 = jnp.split(x, 2, axis=-1)
    return jnp.concatenate([x1 * cos - x2 * sin, x2 * cos + x1 * sin], axis=-1)

def causal_depthwise_conv(u, w, b):
    y = lax.conv_general_dilated(
        u, w[:, None, :], window_strides=(1,), padding=[(CONV_K - 1, 0)],
        dimension_numbers=("NWC", "WIO", "NWC"), feature_group_count=u.shape[-1])
    return y + b

def causal_attention(q, k, v):
    B, S, H, Dq = q.shape
    nblk = S // Q_BLOCK
    qb = q.reshape(B, nblk, Q_BLOCK, H, Dq).transpose(1, 0, 2, 3, 4)
    kpos = jnp.arange(S)
    scale = Dq ** -0.5
    neg = jnp.finfo(jnp.float32).min

    def one_block(args):
        i, qi = args
        s = jnp.einsum('bqhd,bkhd->bhqk', qi, k).astype(jnp.float32) * scale
        qpos = i * Q_BLOCK + jnp.arange(Q_BLOCK)
        s = jnp.where(kpos[None, :] <= qpos[:, None], s, neg)
        p = jax.nn.softmax(s, axis=-1).astype(v.dtype)
        return jnp.einsum('bhqk,bkhd->bqhd', p, v)

    out = lax.map(one_block, (jnp.arange(nblk), qb))
    return out.transpose(1, 0, 2, 3, 4).reshape(B, S, H * v.shape[-1])

def first_inputs(seed: int = 0) -> dict:
    key = jax.random.key(seed)
    ks = jax.random.split(key, 24)
    f = jnp.float32
    L = DEPTH

    def w(k, shape, fan_in):
        return jax.random.normal(k, shape, f) * (fan_in ** -0.5)

    def gain(k, n):
        return jnp.ones((L, n), f) + 0.05 * jax.random.normal(k, (L, n), f)

    x = jax.random.normal(ks[0], (BATCH, SEQ, D_MODEL), f)
    offset = jax.random.randint(ks[1], (BATCH, 1), 0, 1024, dtype=jnp.int32)
    positions = offset + jnp.arange(SEQ, dtype=jnp.int32)[None, :]
    return {
        "x": x,
        "positions": positions,
        "pre_mix_norm": gain(ks[2], D_MODEL),
        "w_in": w(ks[3], (L, D_MODEL, IN_COLS), D_MODEL),
        "q_norm": gain(ks[4], Q_LORA),
        "w_uq": w(ks[5], (L, Q_LORA, N_HEADS * QK_HEAD), Q_LORA),
        "kv_norm": gain(ks[6], KV_LORA),
        "w_ukv": w(ks[7], (L, KV_LORA, N_HEADS * (QK_NOPE + V_HEAD)), KV_LORA),
        "conv_w": w(ks[8], (L, CONV_K, CONV_CH), CONV_K),
        "conv_b": 0.02 * jax.random.normal(ks[9], (L, CONV_CH), f),
        "conv_ln_g": gain(ks[10], CONV_CH),
        "conv_ln_b": 0.02 * jax.random.normal(ks[11], (L, CONV_CH), f),
        "conv_out_norm": gain(ks[12], CONV_CH),
        "attn_out_norm": gain(ks[13], ATTN_CH),
        "w_out": w(ks[14], (L, MIX_WIDTH, D_MODEL), MIX_WIDTH),
        "post_mix_norm": gain(ks[15], D_MODEL),
        "pre_ffn_norm": gain(ks[16], D_MODEL),
        "w_gate": w(ks[17], (L, D_MODEL, D_FF), D_MODEL),
        "w_up": w(ks[18], (L, D_MODEL, D_FF), D_MODEL),
        "w_down": w(ks[19], (L, D_FF, D_MODEL), D_FF),
        "post_ffn_norm": gain(ks[20], D_MODEL),
    }

def first_block(x, positions, pre_mix_norm, w_in, q_norm, w_uq, kv_norm, w_ukv,
              conv_w, conv_b, conv_ln_g, conv_ln_b, conv_out_norm, attn_out_norm,
              w_out, post_mix_norm, pre_ffn_norm, w_gate, w_up, w_down, post_ffn_norm):
    B, S, _ = x.shape
    cos, sin = rope_tables(positions, x.dtype)
    c1 = 2 * CONV_CH
    c2 = c1 + Q_LORA
    c3 = c2 + KV_LORA
    for l in range(DEPTH):
        h = rmsnorm(x, pre_mix_norm[l])
        z = h @ w_in[l]
        conv_in, q_lat, kv_lat, k_rope = z[..., :c1], z[..., c1:c2], z[..., c2:c3], z[..., c3:]

        a, g = jnp.split(conv_in, 2, axis=-1)
        u = a * jax.nn.sigmoid(g)
        u = causal_depthwise_conv(u, conv_w[l], conv_b[l])
        u = jax.nn.silu(layernorm(u, conv_ln_g[l], conv_ln_b[l]))

        q = (rmsnorm(q_lat, q_norm[l]) @ w_uq[l]).reshape(B, S, N_HEADS, QK_HEAD)
        q_nope, q_pe = q[..., :QK_NOPE], q[..., QK_NOPE:]
        q_pe = apply_rope(q_pe, cos[:, :, None, :], sin[:, :, None, :])
        kv = (rmsnorm(kv_lat, kv_norm[l]) @ w_ukv[l]).reshape(B, S, N_HEADS, QK_NOPE + V_HEAD)
        k_nope, v = kv[..., :QK_NOPE], kv[..., QK_NOPE:]
        k_pe = apply_rope(k_rope, cos, sin)
        k_pe = jnp.broadcast_to(k_pe[:, :, None, :], (B, S, N_HEADS, QK_ROPE))
        q_full = jnp.concatenate([q_nope, q_pe], axis=-1)
        k_full = jnp.concatenate([k_nope, k_pe], axis=-1)
        attn = causal_attention(q_full, k_full, v)

        mix = jnp.concatenate([rmsnorm(u, conv_out_norm[l]),
                               rmsnorm(attn, attn_out_norm[l])], axis=-1) @ w_out[l]
        x = x + rmsnorm(mix, post_mix_norm[l])

        hf = rmsnorm(x, pre_ffn_norm[l])
        ff = (jax.nn.silu(hf @ w_gate[l]) * (hf @ w_up[l])) @ w_down[l]
        x = x + rmsnorm(ff, post_ffn_norm[l])
    return x


MIX_WIDTH_2 = D_MODEL
HEAD_DIM = 128
ATTN_WIDTH = MIX_WIDTH_2 // 2
ATTN_HEADS = ATTN_WIDTH // HEAD_DIM
KV_HEADS = 2
GQA_GROUP = ATTN_HEADS // KV_HEADS
WINDOW = 128
ATTN_BLOCK = 128

GLA_WIDTH = MIX_WIDTH_2 - ATTN_WIDTH
GLA_HEADS = 4
GLA_KEY_WIDTH = GLA_WIDTH // 2
GLA_DK = GLA_KEY_WIDTH // GLA_HEADS
GLA_DV = GLA_WIDTH // GLA_HEADS
GLA_DECAY_RANK = 16
GLA_GATE_NORMALIZER = 16.0
GLA_CHUNK = 64

D_FF_2 = 5632
CONV_WIDTH = 3
NORM_EPS = 1e-6

IN_WIDTHS = (ATTN_WIDTH,
             KV_HEADS * HEAD_DIM,
             KV_HEADS * HEAD_DIM,
             GLA_KEY_WIDTH,
             GLA_KEY_WIDTH,
             GLA_WIDTH,
             GLA_WIDTH,
             GLA_DECAY_RANK,
             GLA_DECAY_RANK)
IN_TOTAL = sum(IN_WIDTHS)


def rms_norm(x, g):
    xf = x.astype(jnp.float32)
    y = xf * lax.rsqrt(jnp.mean(xf * xf, axis=-1, keepdims=True) + NORM_EPS)
    return (y * g.astype(jnp.float32)).astype(x.dtype)

def rope(x, pos):
    half = x.shape[-1] // 2
    inv = 1.0 / (ROPE_THETA ** (jnp.arange(half, dtype=jnp.float32) / half))
    ang = pos.astype(jnp.float32)[:, None] * inv[None, :]
    cos = jnp.cos(ang)[:, None, :]
    sin = jnp.sin(ang)[:, None, :]
    xf = x.astype(jnp.float32)
    x1, x2 = xf[..., :half], xf[..., half:]
    return jnp.concatenate([x1 * cos - x2 * sin, x2 * cos + x1 * sin], axis=-1).astype(x.dtype)

def window_attention(q, k, v, sink):
    B, T, HQ, D = q.shape
    nb = T // ATTN_BLOCK
    qb = q.reshape(B, nb, ATTN_BLOCK, KV_HEADS, GQA_GROUP, D)
    pad = ((0, 0), (ATTN_BLOCK, ATTN_BLOCK), (0, 0), (0, 0))
    kb = jnp.pad(k, pad).reshape(B, nb + 2, ATTN_BLOCK, KV_HEADS, D)
    vb = jnp.pad(v, pad).reshape(B, nb + 2, ATTN_BLOCK, KV_HEADS, D)
    kw = jnp.concatenate([kb[:, :-2], kb[:, 1:-1], kb[:, 2:]], axis=2)
    vw = jnp.concatenate([vb[:, :-2], vb[:, 1:-1], vb[:, 2:]], axis=2)
    s = jnp.einsum('bnqhgd,bnshd->bhgnqs', qb, kw).astype(jnp.float32) * (D ** -0.5)
    qi = jnp.arange(ATTN_BLOCK)[:, None]
    sj = jnp.arange(3 * ATTN_BLOCK)[None, :]
    rel = sj - ATTN_BLOCK - qi
    kpos = jnp.arange(nb)[:, None, None] * ATTN_BLOCK - ATTN_BLOCK + sj[None]
    mask = (jnp.abs(rel) <= WINDOW)[None] & (kpos >= 0) & (kpos < T)
    s = jnp.where(mask, s, -jnp.inf)
    sk = sink.astype(jnp.float32).reshape(KV_HEADS, GQA_GROUP)[None, :, :, None, None, None]
    m = jnp.maximum(jnp.max(s, axis=-1, keepdims=True), sk)
    p = jnp.exp(s - m)
    p = p / (jnp.sum(p, axis=-1, keepdims=True) + jnp.exp(sk - m))
    o = jnp.einsum('bhgnqs,bnshd->bnqhgd', p.astype(v.dtype), vw)
    return o.reshape(B, T, HQ * D)

def gla_chunked(q, k, v, g, strict):
    B, H, T, DK = q.shape
    DV = v.shape[-1]
    C = GLA_CHUNK
    n = T // C
    q = q.reshape(B, H, n, C, DK)
    k = k.reshape(B, H, n, C, DK)
    g = g.reshape(B, H, n, C, DK)
    v = v.reshape(B, H, n, C, DV)
    b = jnp.cumsum(g, axis=3)
    b_last = b[:, :, :, -1:, :]
    b_ref = b[:, :, :, C // 2:C // 2 + 1, :]
    a = jnp.einsum('bhnid,bhnjd->bhnij', q * jnp.exp(b - b_ref), k * jnp.exp(b_ref - b))
    mask = jnp.tril(jnp.ones((C, C), dtype=bool), -1 if strict else 0)
    a = jnp.where(mask, a, 0.0)
    o_intra = jnp.einsum('bhnij,bhnje->bhnie', a, v)
    q_in = q * jnp.exp(b)
    k_out = k * jnp.exp(b_last - b)
    chunk_decay = jnp.exp(b_last[:, :, :, 0, :])

    def step(state, inp):
        qc, kc, vc, dc = inp
        o = jnp.einsum('bhid,bhde->bhie', qc, state)
        state = state * dc[..., None] + jnp.einsum('bhjd,bhje->bhde', kc, vc)
        return state, o

    s0 = jnp.zeros((B, H, DK, DV), jnp.float32)
    xs = (jnp.moveaxis(q_in, 2, 0), jnp.moveaxis(k_out, 2, 0),
          jnp.moveaxis(v, 2, 0), jnp.moveaxis(chunk_decay, 2, 0))
    _, o_inter = lax.scan(step, s0, xs)
    o_inter = jnp.moveaxis(o_inter, 0, 2)
    return (o_intra + o_inter).reshape(B, H, T, DV)

def bidirectional_gla(q, k, v, lr_f, lr_b, wa2_f, ba_f, wa2_b, ba_b, gate, out_norm_g):
    B, T, _ = q.shape
    f32 = jnp.float32

    def heads(t, d):
        return jnp.transpose(t.astype(f32).reshape(B, T, GLA_HEADS, d), (0, 2, 1, 3))

    qh = heads(q, GLA_DK) * (GLA_DK ** -0.5)
    kh = heads(k, GLA_DK)
    vh = heads(v, GLA_DV)
    g_f = jax.nn.log_sigmoid((lr_f @ wa2_f + ba_f).astype(f32)) / GLA_GATE_NORMALIZER
    g_b = jax.nn.log_sigmoid((lr_b @ wa2_b + ba_b).astype(f32)) / GLA_GATE_NORMALIZER
    gf = heads(g_f, GLA_DK)
    gb = heads(g_b, GLA_DK)
    o_fwd = gla_chunked(qh, kh, vh, gf, strict=False)
    flip = lambda t: jnp.flip(t, axis=2)
    o_bwd = flip(gla_chunked(flip(qh), flip(kh), flip(vh), flip(gb), strict=True))
    o = jnp.transpose(o_fwd + o_bwd, (0, 2, 1, 3)).astype(v.dtype)
    o = rms_norm(o, out_norm_g)
    o = o * jax.nn.silu(gate.reshape(B, T, GLA_HEADS, GLA_DV))
    return o.reshape(B, T, GLA_WIDTH)

def conv_gated_ffn(h, w_up, conv_w, conv_b, w_down):
    u = h @ w_up
    up_ = jnp.pad(u, ((0, 0), (1, 1), (0, 0)))
    u = up_[:, :-2] * conv_w[0] + up_[:, 1:-1] * conv_w[1] + up_[:, 2:] * conv_w[2] + conv_b
    gate, val = jnp.split(u, 2, axis=-1)
    return (jax.nn.silu(gate) * val) @ w_down

def hybrid_layer(x, norm1_g, w_in, q_norm_g, k_norm_g, sink, wa2_f, ba_f, wa2_b, ba_b,
                 gla_out_norm_g, w_out, norm2_g, w_up, conv_w, conv_b, w_down):
    B, T, _ = x.shape
    pos = jnp.arange(T, dtype=jnp.int32)
    h = rms_norm(x, norm1_g)
    proj = h @ w_in
    offsets = []
    acc = 0
    for w in IN_WIDTHS[:-1]:
        acc += w
        offsets.append(acc)
    q_a, k_a, v_a, q_g, k_g, v_g, gate_g, lr_f, lr_b = jnp.split(proj, offsets, axis=-1)
    qa = rope(rms_norm(q_a.reshape(B, T, ATTN_HEADS, HEAD_DIM), q_norm_g), pos)
    ka = rope(rms_norm(k_a.reshape(B, T, KV_HEADS, HEAD_DIM), k_norm_g), pos)
    va = v_a.reshape(B, T, KV_HEADS, HEAD_DIM)
    o_attn = window_attention(qa, ka, va, sink)
    o_gla = bidirectional_gla(q_g, k_g, v_g, lr_f, lr_b, wa2_f, ba_f, wa2_b, ba_b,
                              gate_g, gla_out_norm_g)
    x = x + jnp.concatenate([o_attn, o_gla], axis=-1) @ w_out
    x = x + conv_gated_ffn(rms_norm(x, norm2_g), w_up, conv_w, conv_b, w_down)
    return x

def second_inputs(seed: int = 0) -> dict:
    key = jax.random.key(seed)
    ks = jax.random.split(key, 20)
    f32 = jnp.float32
    L = DEPTH

    def nrm(k, shape, scale):
        return jax.random.normal(k, shape, f32) * scale

    return {
        "x": nrm(ks[0], (BATCH, SEQ, D_MODEL), 1.0),
        "norm1_g": 1.0 + nrm(ks[1], (L, D_MODEL), 0.02),
        "w_in": nrm(ks[2], (L, D_MODEL, IN_TOTAL), D_MODEL ** -0.5),
        "attn_q_norm_g": 1.0 + nrm(ks[3], (L, HEAD_DIM), 0.02),
        "attn_k_norm_g": 1.0 + nrm(ks[4], (L, HEAD_DIM), 0.02),
        "attn_sink": nrm(ks[5], (L, ATTN_HEADS), 0.5),
        "gla_wa2_fwd": nrm(ks[6], (L, GLA_DECAY_RANK, GLA_KEY_WIDTH), GLA_DECAY_RANK ** -0.5),
        "gla_ba_fwd": nrm(ks[7], (L, GLA_KEY_WIDTH), 0.1),
        "gla_wa2_bwd": nrm(ks[8], (L, GLA_DECAY_RANK, GLA_KEY_WIDTH), GLA_DECAY_RANK ** -0.5),
        "gla_ba_bwd": nrm(ks[9], (L, GLA_KEY_WIDTH), 0.1),
        "gla_out_norm_g": 1.0 + nrm(ks[10], (L, GLA_DV), 0.02),
        "w_out": nrm(ks[11], (L, MIX_WIDTH_2, D_MODEL), MIX_WIDTH_2 ** -0.5),
        "norm2_g": 1.0 + nrm(ks[12], (L, D_MODEL), 0.02),
        "w_up": nrm(ks[13], (L, D_MODEL, 2 * D_FF_2), D_MODEL ** -0.5),
        "conv_w": nrm(ks[14], (L, CONV_WIDTH, 2 * D_FF_2), CONV_WIDTH ** -0.5),
        "conv_b": nrm(ks[15], (L, 2 * D_FF_2), 0.02),
        "w_down": nrm(ks[16], (L, D_FF_2, D_MODEL), D_FF_2 ** -0.5),
    }

def second_block(x, norm1_g, w_in, attn_q_norm_g, attn_k_norm_g, attn_sink, gla_wa2_fwd,
              gla_ba_fwd, gla_wa2_bwd, gla_ba_bwd, gla_out_norm_g, w_out, norm2_g,
              w_up, conv_w, conv_b, w_down):
    for l in range(DEPTH):
        x = hybrid_layer(x, norm1_g[l], w_in[l], attn_q_norm_g[l], attn_k_norm_g[l],
                         attn_sink[l], gla_wa2_fwd[l], gla_ba_fwd[l], gla_wa2_bwd[l],
                         gla_ba_bwd[l], gla_out_norm_g[l], w_out[l], norm2_g[l],
                         w_up[l], conv_w[l], conv_b[l], w_down[l])
    return x


def setup_inputs(seed=0):
    out = dict(first_inputs(seed))
    for name, value in second_inputs(seed + 1).items():
        if name != "x":
            out[name + "_2"] = value
    return out


def reference(
    x, positions, pre_mix_norm, w_in, q_norm, w_uq, kv_norm, w_ukv, conv_w, conv_b, conv_ln_g,
    conv_ln_b, conv_out_norm, attn_out_norm, w_out, post_mix_norm, pre_ffn_norm, w_gate, w_up,
    w_down, post_ffn_norm, norm1_g_2, w_in_2, attn_q_norm_g_2, attn_k_norm_g_2, attn_sink_2,
    gla_wa2_fwd_2, gla_ba_fwd_2, gla_wa2_bwd_2, gla_ba_bwd_2, gla_out_norm_g_2, w_out_2,
    norm2_g_2, w_up_2, conv_w_2, conv_b_2, w_down_2,
):
    x = first_block(
        x, positions, pre_mix_norm, w_in, q_norm, w_uq, kv_norm, w_ukv, conv_w, conv_b,
        conv_ln_g, conv_ln_b, conv_out_norm, attn_out_norm, w_out, post_mix_norm, pre_ffn_norm,
        w_gate, w_up, w_down, post_ffn_norm,
    )
    return second_block(
        x, norm1_g_2, w_in_2, attn_q_norm_g_2, attn_k_norm_g_2, attn_sink_2, gla_wa2_fwd_2,
        gla_ba_fwd_2, gla_wa2_bwd_2, gla_ba_bwd_2, gla_out_norm_g_2, w_out_2, norm2_g_2, w_up_2,
        conv_w_2, conv_b_2, w_down_2,
    )


_drawn_inputs = setup_inputs


def setup_inputs(seed=0):
    import zlib

    import numpy as np

    out = dict(_drawn_inputs(seed))
    spreads = {}
    factors = {'conv_ln_b': 3.958,
     'norm1_g_2': 5.277,
     'attn_q_norm_g_2': 8.0,
     'attn_k_norm_g_2': 8.0,
     'attn_sink_2': 8.0,
     'gla_ba_fwd_2': 7.547,
     'gla_ba_bwd_2': 7.451,
     'gla_out_norm_g_2': 8.0,
     'norm2_g_2': 5.915,
     'conv_b_2': 6.333}
    for name, (base, spread) in spreads.items():
        noise = np.random.default_rng([zlib.crc32(name.encode()), seed]).standard_normal(out[name].shape)
        drawn = base * np.exp(spread * noise) if base else spread * noise
        out[name] = __import__('jax').numpy.asarray(drawn.astype(out[name].dtype))
    for name, factor in factors.items():
        out[name] = (out[name] * factor).astype(out[name].dtype)
    return out
```

```python
from contextlib import ExitStack

import numpy as np

import concourse.bass as bass
from concourse import mybir

F32 = mybir.dt.float32
F32R = mybir.dt.float32r
I32 = mybir.dt.int32
ALU = mybir.AluOpType
ACT = mybir.ActivationFunctionType
X = mybir.AxisListType.X

P = 128
SEQ = 256
TOK = SEQ // P
DM = 2048
KD = DM // P
NB = 512
EPS = 1e-6
RING = 4
MASKED = -3.0e38

CONV = 1024
CC = CONV // P
TAPS = 31
HEADS = 8
NOPE, ROPE, VD = 128, 64, 128
QKH = NOPE + ROPE
QL, KVL = 768, 512
QC, KVC = QL // P, KVL // P
Z1 = QL + KVL + ROPE
DFF = 5632
FC = DFF // P
FB = DFF // NB
THETA = 10000.0

HD = 128
KVH = 2
GH, DK, DV, RANK, CHUNK = 4, 128, 256, 16, 64
NCH = SEQ // CHUNK
Z2 = 4640
W2 = Z2 // 10
QA, KA, VA, QG, KG, VG, GG, LR = 0, 1024, 1280, 1536, 2048, 2560, 3584, 4608
B2_ORDER = [9, 3, 4, 5, 6, 7, 0, 1, 2, 8]

SHAPES = []


def _phase(blocks, tiles, width):
    start = len(SHAPES)
    SHAPES.extend([(kc, width(b)) for b in range(blocks) for kc in tiles])
    return start


IN1_COLS = [(0, 512), (1024, 512), (512, 512), (1536, 512), (2048, 448), (2496, 448), (2944, 448)]
T_IN1 = _phase(7, [2] * 8, lambda b: IN1_COLS[b][1])
T_UQ = _phase(3, [2] * 3, lambda b: NB)
T_UKV = _phase(4, [2] * 2, lambda b: NB)
T_OUT1 = _phase(4, [2] * 8, lambda b: NB)
T_FF1 = _phase(2 * FB, [2] * 8, lambda b: NB)
DN_TILES = [2] * 20 + [1] * 4
T_DN1 = _phase(4, DN_TILES, lambda b: NB)
T_IN2 = _phase(10, [2] * 8, lambda b: W2)
T_OUT2 = _phase(4, [2] * 8, lambda b: NB)
T_FF2 = _phase(2 * FB, [2] * 8, lambda b: NB)
T_DN2 = _phase(4, DN_TILES, lambda b: NB)
T_END = len(SHAPES)

G_FF1 = 7
G_IN2 = G_FF1 + FB
G_FF2 = G_IN2 + 5

F_XT1, F_LAT, F_MIX1, F_XT2, F_FF1 = 0, 8, 13, 17, 25
F_XT3 = F_FF1 + 2 * FB
F_MIX2, F_XT4 = F_XT3 + 8, F_XT3 + 16

GAINS = [("pre_mix_norm", KD), ("q_norm", QC), ("kv_norm", KVC), ("conv_b", CC), ("conv_ln_g", CC),
         ("conv_ln_b", CC), ("conv_out_norm", CC), ("attn_out_norm", CC), ("pre_ffn_norm", KD),
         ("norm1_g_2", KD), ("norm2_g_2", KD)]
G_AT, _n = {}, 0
for _name, _k in GAINS:
    G_AT[_name] = _n
    _n += _k
G_ROWS = _n


def build(nc, a, out):
    ctx = ExitStack()
    with ctx:
        def sb(name, shape, dt=F32):
            return ctx.enter_context(nc.sbuf_tensor(name, shape, dt))

        def overlay(tensors, stay=False):
            inner = ExitStack()
            got = [inner.enter_context(nc.sbuf_tensor(n, s, d)) for n, s, d in tensors]
            if stay:
                ctx.push(inner)
            else:
                inner.close()
            return got

        def sem(name):
            return ctx.enter_context(nc.semaphore(name))

        x_sb = sb("x_sb", [P, TOK, DM])
        raw = sb("raw", [P, RING, 2, NB])
        w_hi = sb("w_hi", [P, RING, 2, NB], F32R)
        w_lo = sb("w_lo", [P, RING, 2, NB], F32R)
        ident = sb("ident", [P, P])
        ones = sb("ones", [P, P])
        gains = sb("gains", [P, G_ROWS])
        convw = sb("convw", [P, TAPS * CC])
        conv2 = sb("conv2", [P, 4, 2 * FC])
        masks = sb("masks", [P, 5 * P])
        mask1 = masks[:, 0:3 * P]
        mask2 = masks[:, P:5 * P]
        tri = sb("tri", [P, 2, P])
        gmask = sb("gmask", [P, 2, P], I32)
        posf = sb("posf", [P, 2, TOK])
        trig = sb("trig", [P, TOK, 2, 96])
        invf = sb("invf", [P, 96])
        ss = sb("ss", [P, 64])
        ms = sb("ms", [P, 64])
        rstd = sb("rstd", [P, 64])
        minus_half = sb("minus_half", [P, 20])
        amax = sb("amax", [P, 2, 2, 4])
        asum = sb("asum", [P, 2, 2, 2])
        sinkb = sb("sinkb", [P, HEADS])
        decay = sb("decay", [P, 2, GH * NCH])
        y_dn, _, grow_dn = overlay([("y_dn", [P, TOK * DM], F32), ("under_grow", [P, DM], F32), ("grow_dn", [P, DM], F32)])
        state, ktok, att2_q, att2_s, att2_p, at_sb = overlay([
            ("state", [P, 2, 2, 3, DV], F32), ("ktok", [P, 2, 2, TOK, P], F32),
            ("att2_q", [P, 2, SEQ], F32), ("att2_s", [P, 2, TOK, SEQ], F32), ("att2_p", [P, 2, 4, P], F32),
            ("at_sb", [P, 2, TOK, P], F32)])
        hT_hi = sb("hT_hi", [P, KD, SEQ], F32R)
        hT_lo = sb("hT_lo", [P, KD, SEQ], F32R)
        z1, uT, cv, q1, kv1, attn1, qkT, qpeT, att1_s, att1_p, kpe, kpeT = overlay([
            ("z1", [P, TOK, Z1], F32), ("uT", [P, CC, SEQ + TAPS - 1], F32), ("cv", [P, CC, SEQ], F32),
            ("q1", [P, TOK, HEADS * QKH], F32), ("kv1", [P, TOK, DM], F32), ("attn1", [P, TOK, CONV], F32),
            ("qkT", [P, 2, 2, SEQ], F32), ("qpeT", [ROPE, 2, SEQ], F32), ("att1_s", [P, 2, 3 * P], F32),
            ("att1_p", [P, 2, 3 * P], F32), ("kpe", [P, TOK, ROPE], F32), ("kpeT", [ROPE, SEQ], F32)])
        taken = sum([TOK * Z1, CC * (SEQ + TAPS - 1), CC * SEQ, TOK * HEADS * QKH, TOK * DM, TOK * CONV,
                     4 * SEQ, 2 * SEQ, 6 * P, 6 * P, TOK * ROPE, SEQ])
        _, latT_hi, latT_lo = overlay([("under_lat", [P, taken], F32),
                                       ("latT_hi", [P, QC + KVC, SEQ], F32R), ("latT_lo", [P, QC + KVC, SEQ], F32R)])
        _, lnsq = overlay([("under_ln", [P, taken], F32), ("lnsq", [P, CC, SEQ], F32)])
        y_out, grow_out = overlay([("y_out", [P, TOK * DM], F32), ("grow_out", [P, DM], F32)])
        z2, gb, qT2, kT2, fac, kaT, gqk, gla_g = overlay([
            ("z2", [P, TOK, Z2], F32), ("gb", [P, 2, 2, 2 * NB], F32), ("qT2", [P, GH, SEQ], F32),
            ("kT2", [P, GH, SEQ], F32), ("fac", [P, 2, 4, GH, SEQ], F32), ("kaT", [P, KVH, SEQ], F32),
            ("gqk", [P, 2, HD], F32), ("gla_g", [P, DV], F32)])
        taken = TOK * Z2 + 8 * NB + 2 * GH * SEQ + 6 * GH * SEQ
        _, lrT, wa2 = overlay([("under_lr", [P, taken], F32), ("lrT", [RANK + 1, 2, SEQ], F32),
                               ("wa2", [RANK + 1, 2, NB], F32)])
        rows, = overlay([("rows", [P, 8, P], F32)])
        trig_t, = overlay([("under_trig", [P, 8 * P], F32), ("trig_t", [P, 4, TOK * 96], F32)])[1:]
        aT_hi = sb("aT_hi", [P, FC, SEQ], F32R)
        aT_lo = sb("aT_lo", [P, FC, SEQ], F32R)
        stage = sb("stage", [P, 3, 4, SEQ])
        ps = ctx.enter_context(nc.psum_tensor("ps", [P, 8, NB], F32))

        gate_s = stage[:, 0].rearrange("p c s -> p (c s)").rearrange("p (t n) -> p t n", t=TOK)
        prod_s = stage[:, 1].rearrange("p c s -> p (c s)").rearrange("p (t n) -> p t n", t=TOK)
        raw_s = gate_s
        cg, cval = stage[:, 1], stage[:, 2]
        a_s = attn1[:, :, 0:NB]
        sg_s = attn1[:, :, NB:2 * NB]

        raw_landed = [sem(f"raw_landed{s}") for s in range(RING)]
        hi_ready, lo_ready, tile_used = sem("hi_ready"), sem("lo_ready"), sem("tile_used")
        gemm_free = [sem("gemm_free0"), sem("gemm_free1")]
        tp_ready, tp_hi, tp_free = sem("tp_ready"), sem("tp_hi"), sem("tp_free")
        x_landed, params_landed, late_landed, grow_landed, out_landed = (
            sem("x_landed"), sem("params_landed"), sem("late_landed"), sem("grow_landed"), sem("out_landed"))
        rows_landed = sem("rows_landed")
        ident_ready, consts_ready, masks_ready = sem("ident_ready"), sem("consts_ready"), sem("masks_ready")
        rows_T, gains_ready = sem("rows_T"), sem("gains_ready")
        dve_step, act_step, pool_step = sem("dve_step"), sem("act_step"), sem("pool_step")
        ms_ready, rstd_ready, sq_done = sem("ms_ready"), sem("rstd_ready"), sem("sq_done")
        u_ready, cu_ready, cu_free = sem("u_ready"), sem("cu_ready"), sem("cu_free")
        a_ready = sem("a_ready")
        conv_tap = sem("conv_tap")
        trig_arg, trig_abs, trig_done = sem("trig_arg"), sem("trig_abs"), sem("trig_done")
        at_T, at_qk, at_S, at_max, at_exp, at_PT, at_pT, at_PV, at_out = (
            sem("at_T"), sem("at_qk"), sem("at_S"), sem("at_max"), sem("at_exp"), sem("at_PT"), sem("at_pT"),
            sem("at_PV"), sem("at_out"))
        rope_ready, kpe_ready = sem("rope_ready"), sem("kpe_ready")
        ln_mm, ln_dve, ln_act = sem("ln_mm"), sem("ln_dve"), sem("ln_act")
        attn_scaled, mix_conv = sem("attn_scaled"), sem("mix_conv")
        row_sq, row_y, x_new = sem("row_sq"), sem("row_y"), sem("x_new")
        ct_ready, ct_center, ct_free, cg_silu, prod_ready, aT_hi_ready, aT_ready, conv2_step = (
            sem("ct_ready"), sem("ct_center"), sem("ct_free"), sem("cg_silu"), sem("prod_ready"),
            sem("aT_hi_ready"), sem("aT_ready"), sem("conv2_step"))
        gl_mm, gl_act, gl_dve = sem("gl_mm"), sem("gl_act"), sem("gl_dve")
        fac_exp, fac_ready = sem("fac_exp"), sem("fac_ready")
        g_AT, g_at, g_KT, g_kt, g_SS, g_st, g_O, g_o = (
            sem("g_AT"), sem("g_at"), sem("g_KT"), sem("g_kt"), sem("g_SS"), sem("g_st"), sem("g_O"), sem("g_o"))
        mix2_ready, gate2_ready = sem("mix2_ready"), sem("gate2_ready")

        def chunks(w):
            return w[0].rearrange("(c p) n -> p c n", p=P)

        w_in, w_uq, w_ukv, w_out = chunks(a["w_in"]), chunks(a["w_uq"]), chunks(a["w_ukv"]), chunks(a["w_out"])
        w_gate, w_up, w_down = chunks(a["w_gate"]), chunks(a["w_up"]), chunks(a["w_down"])
        w_in2, w_out2, w_up2, w_down2 = (chunks(a["w_in_2"]), chunks(a["w_out_2"]), chunks(a["w_up_2"]),
                                         chunks(a["w_down_2"]))

        def landed(c0, step):
            return 16 * (c0 // RING + 1) + (16 // RING) * step

        def cols(n, w=NB):
            return bass.ts(n, w)

        def in_sbuf(eng, B, base=0):
            eng.wait_ge(gemm_free[B % 2], base + B // 2 + 1)

        def last_of(b, d):
            return b.rearrange("p h (c s) -> p (h c) s", s=CHUNK)[:, :, CHUNK - 1 if d == 0 else 0]

        def gla_sum(d, c):
            bank, i = {(0, 0): (2, 0), (0, 2): (2, 1), (1, 2): (3, 0), (0, 1): (4, 0), (1, 3): (4, 1), (1, 1): (6, 0)}[d, c]
            return ps[:, bank, i * DV:(i + 1) * DV]

        gb_flat = gb[:].rearrange("p a d n -> p (a d n)")
        ps_flat = ps[:].rearrange("p b n -> p (b n)")
        ss4 = ss[:, 56:64]

        block = ctx.enter_context(nc.Block())

        @block.sync
        def _(sp):
            for t in range(TOK):
                sp.dma_start(x_sb[:, t, :], a["x"][0, t * P:(t + 1) * P, :]).then_inc(x_landed, 16)

            def load(c0, step, w, k0, at):
                kc, width = SHAPES[c0]
                s = c0 % RING
                if c0 >= RING:
                    sp.wait_ge(lo_ready, c0 - RING + 1 + step)
                sp.dma_start(raw[:, s, :kc, :width], w[:, k0:k0 + kc, at]).then_inc(raw_landed[s], 16)

            def load_block(c0, step, w, tiles, at):
                k0 = 0
                for n, kc in enumerate(tiles):
                    load(c0 + n, step, w, k0, at)
                    k0 += kc

            def rows_phase(c0, w, tiles):
                T = len(tiles)
                load_block(c0, 0, w, tiles, cols(0))
                with sp.Fori(1, 4) as n:
                    load_block(c0, n * T, w, tiles, cols(n))

            for b, (n0, width) in enumerate(IN1_COLS):
                load_block(T_IN1 + 8 * b, 0, w_in, [2] * 8, slice(n0, n0 + width))
            for b in range(3):
                load_block(T_UQ + 3 * b, 0, w_uq, [2] * 3, cols(b))
            for b in range(4):
                load_block(T_UKV + 2 * b, 0, w_ukv, [2] * 2, cols(b))
            rows_phase(T_OUT1, w_out, [2] * 8)

            def ff1(j):
                load_block(T_FF1, 16 * j, w_gate, [2] * 8, cols(j))
                load_block(T_FF1 + 8, 16 * j, w_up, [2] * 8, cols(j))
            with sp.Fori(0, FB) as j:
                ff1(j)
            rows_phase(T_DN1, w_down, DN_TILES)
            for b, n in enumerate(B2_ORDER):
                load_block(T_IN2 + 8 * b, 0, w_in2, [2] * 8, slice(n * W2, (n + 1) * W2))
            rows_phase(T_OUT2, w_out2, [2] * 8)
            with sp.Fori(0, FB) as j:
                load_block(T_FF2, 16 * j, w_up2, [2] * 8, cols(j))
                load_block(T_FF2 + 8, 16 * j, w_up2, [2] * 8, cols(j + FB))
            rows_phase(T_DN2, w_down2, DN_TILES)
            for n in range(4):
                sp.wait_ge(row_y, 9 + n)
                sp.dma_start(out[0, :, cols(n)].rearrange("(t p) n -> p t n", p=P), x_sb[:, :, cols(n)])\
                  .then_inc(out_landed, 16)
            sp.wait_ge(out_landed, 16 * 4)

        R = {}
        at = 0
        for name, n in [("x0", 2), ("lat", 4), ("ln", 2), ("conv", 2), ("attn", 2), ("out1", 2), ("x1", 2),
                        ("dn1", 2), ("x2", 2), ("qk", 20), ("gla", 8), ("x3", 2)]:
            R[name] = (at, n)
            at += n
        R_ORDER = ["x0", "lat", "attn", "ln", "conv", "out1", "x1", "dn1", "x2", "qk", "gla", "x3"]

        def r_count(name):
            return R_ORDER.index(name) + 1

        def r_of(tensor, name, lo=0, n=None):
            at, k = R[name]
            return tensor[:, at + lo:at + lo + (k - lo if n is None else n)]

        @block.gpsimd
        def _(pool):
            count = [0]

            def step(ins):
                count[0] += 1
                ins.then_inc(pool_step, 1)
                pool.wait_ge(pool_step, count[0])

            step(pool.memset(ident[:], 0.0))
            pool.affine_select(out=ident[:], in_=ident[:], compare_op=ALU.not_equal, fill=1.0, base=0,
                               pattern=[[-1, P]], channel_multiplier=1).then_inc(ident_ready, 1)
            step(pool.memset(masks[:], 0.0))
            step(pool.memset(tri[:], 1.0))
            for at, sign in ((0, 1), (2 * P, 1), (3 * P, -1)):
                step(pool.affine_select(out=masks[:, at:at + P], in_=masks[:, at:at + P], compare_op=ALU.is_ge,
                                        fill=MASKED, base=0, pattern=[[-sign, P]], channel_multiplier=sign))
            for d, (m, c) in enumerate([(-1, 1), (1, -1)]):
                step(pool.affine_select(out=tri[:, d, :], in_=tri[:, d, :], compare_op=ALU.is_ge, fill=0.0,
                                        base=0, pattern=[[c, P]], channel_multiplier=m))
                step(pool.affine_select(out=tri[:, d, 0:CHUNK], in_=tri[:, d, 0:CHUNK], compare_op=ALU.is_ge,
                                        fill=0.0, base=CHUNK - 1, pattern=[[0, CHUNK]], channel_multiplier=-1))
                step(pool.affine_select(out=tri[:, d, CHUNK:P], in_=tri[:, d, CHUNK:P], compare_op=ALU.is_ge,
                                        fill=0.0, base=-CHUNK, pattern=[[0, CHUNK]], channel_multiplier=1))
            step(pool.tensor_copy(gmask[:], tri[:]))
            step(pool.affine_select(out=gmask[:, 1, :], in_=gmask[:, 1, :], compare_op=ALU.is_gt, fill=0.0,
                                    base=0, pattern=[[-1, P]], channel_multiplier=1))
            pool.iota(posf[:, 1, :], pattern=[[P, TOK]], base=0, channel_multiplier=1,
                      allow_small_or_imprecise_dtypes=True).then_inc(masks_ready, 1)
            pool.wait_ge(consts_ready, 2)
            for n, name in enumerate(R_ORDER):
                pool.wait_ge(ms_ready, n + 1)
                k = R[name][1]
                pool.tensor_tensor(r_of(rstd, name), r_of(ms, name), minus_half[:, 0:k],
                                   ALU.pow).then_inc(rstd_ready, 1)

        @block.tensor
        def _(pe):
            def gemm_tile(c0, step, A, k0, banks, start, stop):
                kc, width = SHAPES[c0]
                s = c0 % RING
                pe.wait_ge(lo_ready, c0 + 1 + step)
                for k in range(kc):
                    for t in range(TOK):
                        o = banks(t, width)
                        first, last = start and k == 0, stop and k == kc - 1
                        xh, xl = A[0][:, k0 + k, t * P:(t + 1) * P], A[1][:, k0 + k, t * P:(t + 1) * P]
                        wh, wl = w_hi[:, s, k, :width], w_lo[:, s, k, :width]
                        pe.matmul(o, xh, wh, start=first, stop=False)
                        pe.matmul(o, xh, wl, start=False, stop=False)
                        mm = pe.matmul(o, xl, wh, start=False, stop=last)
                mm.then_inc(tile_used, 1)

            def pair(p):
                return lambda t, width: ps[:, 2 * p + t, :width]

            H = (hT_hi, hT_lo)

            def fill(F, src, n, wait=None):
                if F >= 4:
                    pe.wait_ge(tp_free, F - 3)
                for k in range(2):
                    for t in range(TOK):
                        mm = pe.transpose(ps[:, 4 + F % 4, k * SEQ + t * P:k * SEQ + (t + 1) * P],
                                          src[:, t, (2 * n + k) * P:(2 * n + k + 1) * P], ident[:])
                mm.then_inc(tp_ready, 1)

            def with_fills(c0, F, src, ready, banks):
                for n in range(4):
                    ready(n)
                    fill(F + n, src, n)
                for n in range(8):
                    pe.wait_ge(tp_free, F + n + 1)
                    gemm_tile(c0 + n, 0, H, 2 * n, banks, n == 0, n == 7)
                    if n < 4:
                        ready(n + 4)
                        fill(F + n + 4, src, n + 4)

            pe.wait_ge(ident_ready, 1)
            pe.wait_ge(consts_ready, 1)
            pe.wait_ge(rows_landed, 16 * len(GAINS))
            mm = pe.transpose(ps[:, 0, 0:G_ROWS], rows[0:G_ROWS, 0, :], ident[0:G_ROWS, 0:G_ROWS])
            mm.then_inc(rows_T, 1)
            pe.wait_ge(x_landed, 16 * TOK)

            def x0_ready(n):
                pass

            for n in range(4):
                fill(F_XT1 + n, x_sb, n)
            pe.wait_ge(params_landed, 16 * 9)
            pe.transpose(ps[:, 2, 0:P], rows[:, 1, :], ident[:])
            pe.transpose(ps[:, 2, P:TAPS * CC], rows[0:TAPS * CC - P, 2, :],
                         ident[0:TAPS * CC - P, 0:TAPS * CC - P]).then_inc(rows_T, 1)
            for n in range(4):
                mm = pe.transpose(ps[:, 3, n * 2 * FC:(n + 1) * 2 * FC], rows[0:2 * FC, 3 + n, :],
                                  ident[0:2 * FC, 0:2 * FC])
            mm.then_inc(rows_T, 1)
            pe.wait_ge(gains_ready, 3)
            for n in range(8):
                pe.wait_ge(tp_free, F_XT1 + n + 1)
                gemm_tile(T_IN1 + n, 0, H, 2 * n, pair(0), n == 0, n == 7)
                if n < 4:
                    fill(F_XT1 + n + 4, x_sb, n + 4)

            def cu_fills(g):
                pe.wait_ge(u_ready, g + 1)
                if g == 0:
                    pe.wait_ge(tp_free, 8)
                for f in range(2):
                    if g > 0:
                        pe.wait_ge(cu_free, 2 * (g - 1) + f + 1)
                    for k in range(2):
                        for t in range(TOK):
                            c = 2 * f + k
                            mm = pe.transpose(ps[:, 6 + f, k * SEQ + t * P:k * SEQ + (t + 1) * P],
                                              a_s[:, t, c * P:(c + 1) * P], ident[:])
                    mm.then_inc(cu_ready, 1)

            def in1_tiles(lo, hi):
                for g in range(lo, hi):
                    b, n = divmod(g, 8)
                    if n == 0 and b >= 2:
                        pe.wait_ge(gemm_free[b % 2], b // 2)
                    gemm_tile(T_IN1 + g, 0, H, 2 * n, pair(b % 2), n == 0, n == 7)

            in1_tiles(8, 20)
            cu_fills(0)
            in1_tiles(20, 36)
            cu_fills(1)
            in1_tiles(36, 52)
            pe.wait_ge(cu_free, 4)
            in_sbuf(pe, 4)
            in_sbuf(pe, 5)
            for n in range(3):
                fill(F_LAT + n, z1, n)
            in1_tiles(52, 56)
            L = (latT_hi, latT_lo)

            def up_tiles(first, lo, hi):
                for g in range(lo, hi):
                    b, n = divmod(g, 3)
                    B = 7 + b
                    if n == 0:
                        pe.wait_ge(gemm_free[B % 2], B // 2)
                    pe.wait_ge(tp_free, F_LAT + n + 1)
                    gemm_tile(T_UQ + g, 0, L, 2 * n, pair(B % 2), n == 0, n == 2)

            up_tiles(0, 0, 3)
            in_sbuf(pe, 6)
            for n in range(2):
                fill(F_LAT + 3 + n, z1, QC // 2 + n)
            up_tiles(0, 3, 9)
            for b in range(4):
                B = 10 + b
                pe.wait_ge(gemm_free[B % 2], B // 2)
                for n in range(2):
                    pe.wait_ge(tp_free, F_LAT + 4 + n)
                    gemm_tile(T_UKV + 2 * b + n, 0, L, QC + 2 * n, pair(B % 2), n == 0, n == 1)

            pe.wait_ge(tp_free, F_LAT + 5)
            pe.wait_ge(gemm_free[0], 7)
            pe.wait_ge(gemm_free[1], 7)
            pe.wait_ge(kpe_ready, 1)
            for t in range(TOK):
                mm = pe.transpose(ps[0:ROPE, 5, t * P:(t + 1) * P], kpe[:, t, :], ident[:])
            mm.then_inc(kpe_ready, 1)
            pe.wait_ge(rope_ready, 1)
            pe.wait_ge(kpe_ready, 3)

            def attn1_T(h):
                b = 4 * (h % 2)
                if h >= 2:
                    pe.wait_ge(at_qk, h - 1)
                for t in range(TOK):
                    pe.transpose(ps[:, b, t * P:(t + 1) * P], q1[:, t, h * QKH:h * QKH + NOPE], ident[:])
                    pe.transpose(ps[:, b, SEQ + t * P:SEQ + (t + 1) * P], kv1[:, t, h * 2 * VD:h * 2 * VD + NOPE],
                                 ident[:])
                    mm = pe.transpose(ps[0:ROPE, b + 1, t * P:(t + 1) * P],
                                      z1[:, t, h * ROPE:(h + 1) * ROPE], ident[:])
                mm.then_inc(at_T, 1)

            def attn1_S(h):
                b, e = 4 * (h % 2), h % 2
                pe.wait_ge(at_qk, h + 1)
                if h >= 2:
                    pe.wait_ge(at_max, h - 1)
                for t in range(TOK):
                    n = (t + 1) * P
                    o = ps[:, b + 2, t * P:t * P + n]
                    pe.matmul(o, qkT[:, e, 0, t * P:(t + 1) * P], qkT[:, e, 1, 0:n], start=True, stop=False)
                    mm = pe.matmul(o, qpeT[:, e, t * P:(t + 1) * P], kpeT[:, 0:n], start=False, stop=True)
                mm.then_inc(at_S, 1)

            def attn_PT(h, h0, n, src):
                b, e = 4 * (h % 2), h % 2
                pe.wait_ge(at_exp, h0 + h + 1)
                if h >= 2:
                    pe.wait_ge(at_out, h0 + h - 1)
                for k in range(n):
                    mm = pe.transpose(ps[:, b + 3, k * P:(k + 1) * P], src(e, k), ident[:])
                mm.then_inc(at_PT, 1)

            def attn1_PV(h):
                b, e = 4 * (h % 2), h % 2
                pe.wait_ge(at_pT, h + 1)
                v = [kv1[:, t, h * 2 * VD + NOPE:(h + 1) * 2 * VD] for t in range(TOK)]
                pT = [att1_p[:, e, k * P:(k + 1) * P] for k in range(3)]
                pe.matmul(ps[:, b + 3, 0:VD], pT[0], v[0], start=True, stop=True)
                pe.matmul(ps[:, b + 3, VD:2 * VD], pT[1], v[0], start=True, stop=False)
                pe.matmul(ps[:, b + 3, VD:2 * VD], pT[2], v[1], start=False, stop=True).then_inc(at_PV, 1)

            def src1(e, k):
                return att1_s[:, e, k * P:(k + 1) * P]

            attn1_T(0)
            for h in range(HEADS + 1):
                if h + 1 < HEADS:
                    attn1_T(h + 1)
                if h < HEADS:
                    attn1_S(h)
                if h >= 1:
                    attn_PT(h - 1, 0, 3, src1)
                    attn1_PV(h - 1)

            pe.wait_ge(conv_tap, TAPS * CC)
            pe.wait_ge(at_out, HEADS)
            for c in range(CC):
                mm = pe.matmul(ps[:, 0, 0:SEQ], ones[:], cv[:, c, :], start=(c == 0), stop=(c == CC - 1))
            mm.then_inc(ln_mm, 1)

            def column_sums(bank, done):
                for t in range(TOK):
                    for c in range(CC):
                        mm = pe.matmul(ps[:, bank, t:t + 1], lnsq[:, c, t * P:(t + 1) * P], ones[:, 0:1],
                                       start=(c == 0), stop=(c == CC - 1))
                mm.then_inc(done, 1)

            pe.wait_ge(ln_act, 1)
            column_sums(1, ln_mm)
            pe.wait_ge(ln_dve, 2)
            for t in range(TOK):
                mm = pe.matmul(ps[:, 0, t * P:(t + 1) * P], ones[:], lnsq[:, 0, t * P:(t + 1) * P],
                               start=True, stop=True)
            mm.then_inc(ln_mm, 1)
            pe.wait_ge(ln_act, 3)
            column_sums(1, ln_mm)
            pe.wait_ge(attn_scaled, 1)
            for n in range(4):
                fill(F_MIX1 + n, attn1, n)

            def rows_tiles(c0, step, A, tiles, lo, hi, banks):
                k0 = sum(tiles[:lo])
                for n in range(lo, hi):
                    gemm_tile(c0 + n, step, A, k0, banks, n == 0, n == len(tiles) - 1)
                    k0 += tiles[n]

            def rows_rest(c0, A, tiles):
                T = len(tiles)
                with pe.Fori(1, 4) as n:
                    rows_tiles(c0, n * T, A, tiles, 0, T, lambda t, width: ps_flat[:, bass.ts(2 * n + t, NB)])

            pe.wait_ge(tp_free, F_MIX1 + 4)
            pe.wait_ge(mix_conv, 1)
            rows_tiles(T_OUT1, 0, H, [2] * 8, 0, 8, pair(0))
            rows_rest(T_OUT1, H, [2] * 8)

            def x_ready(base):
                return lambda n: pe.wait_ge(x_new, base + n // 2 + 1)

            def ff_tiles(c0, step, p, lo, hi):
                for n in range(lo, hi):
                    gemm_tile(c0 + n, step, H, 2 * n, pair(p), n == 0, n == 7)

            def ff1_turn(j):
                pe.wait_ge(gemm_free[1], G_FF1 + 1 + j)
                for f in range(2):
                    pe.wait_ge(tp_free, F_FF1 + f - 1 + 2 * j)
                    for k in range(2):
                        for t in range(TOK):
                            c = 2 * f + k
                            mm = pe.transpose(ps[:, 4 + f, k * SEQ + t * P:k * SEQ + (t + 1) * P],
                                              prod_s[:, t, c * P:(c + 1) * P], ident[:])
                    mm.then_inc(tp_ready, 1)

            with_fills(T_FF1, F_XT2, x_sb, x_ready(0), pair(0))
            ff_tiles(T_FF1 + 8, 0, 1, 0, 8)
            with pe.Fori(1, FB) as j:
                pe.wait_ge(gemm_free[0], G_FF1 + j)
                ff_tiles(T_FF1, 16 * j, 0, 0, 4)
                ff1_turn(j - 1)
                ff_tiles(T_FF1, 16 * j, 0, 4, 8)
                pe.wait_ge(gemm_free[1], G_FF1 + j)
                ff_tiles(T_FF1 + 8, 16 * j, 1, 0, 8)
            A = (aT_hi, aT_lo)
            pe.wait_ge(gemm_free[0], G_FF1 + FB)
            rows_tiles(T_DN1, 0, A, DN_TILES, 0, 4, pair(0))
            ff1_turn(FB - 1)
            rows_tiles(T_DN1, 0, A, DN_TILES, 4, 20, pair(0))
            pe.wait_ge(tp_free, F_XT3)
            rows_tiles(T_DN1, 0, A, DN_TILES, 20, 24, pair(0))
            rows_rest(T_DN1, A, DN_TILES)

            with_fills(T_IN2, F_XT3, x_sb, x_ready(4), pair(0))

            def in2_tiles(lo, hi):
                for g in range(lo, hi):
                    b, n = divmod(g, 8)
                    if n == 0:
                        pe.wait_ge(gemm_free[b % 2], G_IN2 + b // 2)
                    gemm_tile(T_IN2 + g, 0, H, 2 * n, pair(b % 2), n == 0, n == 7)

            in2_tiles(8, 12)
            in_sbuf(pe, 0, G_IN2)
            pe.wait_ge(tp_free, F_XT3 + 8)
            for d in range(2):
                for t in range(TOK):
                    mm = pe.transpose(ps[0:RANK, 4, d * SEQ + t * P:d * SEQ + (t + 1) * P],
                                      z2[:, t, LR + d * RANK:LR + (d + 1) * RANK], ident[:])
            mm.then_inc(gl_mm, 1)
            in2_tiles(12, 16)
            pe.wait_ge(gl_act, 1)
            pe.wait_ge(late_landed, 16 * 7)
            for d in range(2):
                for t in range(TOK):
                    mm = pe.matmul(ps[:, 4 + 2 * d + t, :], lrT[:, d, t * P:(t + 1) * P], wa2[:, d, :],
                                   start=True, stop=True)
            mm.then_inc(gl_mm, 1)
            in2_tiles(16, 28)
            pe.wait_ge(gl_dve, 1)
            for d in range(2):
                for h in range(GH):
                    for t in range(TOK):
                        at = h * SEQ + t * P
                        mm = pe.matmul(ps[:, 4 + 2 * d + at // NB, at % NB:at % NB + P],
                                       gb[:, 0, d, t * NB + h * DK:t * NB + (h + 1) * DK], tri[:, d, :],
                                       start=True, stop=True)
            mm.then_inc(gl_mm, 1)
            in2_tiles(28, 40)
            in_sbuf(pe, 2, G_IN2)
            in_sbuf(pe, 3, G_IN2)
            pe.wait_ge(gl_act, 3)
            for i, c0 in enumerate((QG, KG)):
                for h in range(GH):
                    for t in range(TOK):
                        at = h * SEQ + t * P
                        mm = pe.transpose(ps[:, 4 + 2 * i + at // NB, at % NB:at % NB + P],
                                          z2[:, t, c0 + h * DK:c0 + (h + 1) * DK], ident[:])
            mm.then_inc(gl_mm, 1)
            in2_tiles(40, 80)

            pe.wait_ge(gemm_free[0], G_FF2)
            pe.wait_ge(gemm_free[1], G_FF2)
            pe.wait_ge(gl_act, 4)
            pe.wait_ge(rope_ready, 2)
            for g in range(KVH):
                for t in range(TOK):
                    mm = pe.transpose(ps[:, 4, g * SEQ + t * P:g * SEQ + (t + 1) * P],
                                      z2[:, t, KA + g * HD:KA + (g + 1) * HD], ident[:])
            mm.then_inc(kpe_ready, 1)
            pe.wait_ge(kpe_ready, 5)

            def attn2_T(h):
                b = 4 * (h % 2)
                if h >= 2:
                    pe.wait_ge(at_qk, HEADS + h - 1)
                for t in range(TOK):
                    mm = pe.transpose(ps[:, b, t * P:(t + 1) * P], z2[:, t, h * HD:(h + 1) * HD], ident[:])
                mm.then_inc(at_T, 1)

            def attn2_S(h):
                b, e = 4 * (h % 2), h % 2
                pe.wait_ge(at_qk, HEADS + h + 1)
                if h >= 2:
                    pe.wait_ge(at_max, HEADS + h - 1)
                for t in range(TOK):
                    mm = pe.matmul(ps[:, b + 2, t * SEQ:(t + 1) * SEQ], att2_q[:, e, t * P:(t + 1) * P],
                                   kaT[:, h * KVH // HEADS, :], start=True, stop=True)
                mm.then_inc(at_S, 1)

            def attn2_PV(h):
                b, e = 4 * (h % 2), h % 2
                pe.wait_ge(at_pT, HEADS + h + 1)
                g = h * KVH // HEADS
                for t in range(TOK):
                    for k in range(TOK):
                        mm = pe.matmul(ps[:, b + 3, t * HD:(t + 1) * HD], att2_p[:, e, 2 * t + k, :],
                                       z2[:, k, VA + g * HD:VA + (g + 1) * HD], start=(k == 0), stop=(k == 1))
                mm.then_inc(at_PV, 1)

            def src2(e, k):
                return att2_s[:, e, k // 2, (k % 2) * P:(k % 2 + 1) * P]

            attn2_T(0)
            for h in range(HEADS + 1):
                if h + 1 < HEADS:
                    attn2_T(h + 1)
                if h < HEADS:
                    attn2_S(h)
                if h >= 1:
                    attn_PT(h - 1, HEADS, 4, src2)
                    attn2_PV(h - 1)

            pe.wait_ge(fac_ready, 2)
            pe.wait_ge(at_out, 2 * HEADS)
            QE, KE, QI, KO = range(4)

            def gla_A(h):
                if h >= 1:
                    pe.wait_ge(g_at, h)
                for d in range(2):
                    for t in range(TOK):
                        mm = pe.matmul(ps[:, 0, (2 * d + t) * P:(2 * d + t + 1) * P],
                                       fac[:, d, KE, h, t * P:(t + 1) * P], fac[:, d, QE, h, t * P:(t + 1) * P],
                                       start=True, stop=True)
                mm.then_inc(g_AT, 1)
                if h >= 1:
                    pe.wait_ge(g_kt, h)
                for d in range(2):
                    for t in range(TOK):
                        mm = pe.transpose(ps[:, 1, (2 * d + t) * P:(2 * d + t + 1) * P],
                                          fac[:, d, KO, h, t * P:(t + 1) * P], ident[:])
                mm.then_inc(g_KT, 1)

            def gla_S(h):
                pe.wait_ge(g_kt, h + 1)
                if h >= 1:
                    pe.wait_ge(g_st, h)
                e = h % 2
                for d in range(2):
                    for n in range(3):
                        c = n if d == 0 else 3 - n
                        r = slice(CHUNK * (c % 2), CHUNK * (c % 2) + CHUNK)
                        mm = pe.matmul(gla_sum(d, c),
                                       ktok[r, e, d, c // 2, :], z2[r, c // 2, VG + h * DV:VG + (h + 1) * DV],
                                       start=True, stop=True)
                mm.then_inc(g_SS, 1)

            def gla_O(h):
                e = h % 2
                pe.wait_ge(g_at, h + 1)
                pe.wait_ge(g_st, h + 1)
                if h >= 1:
                    pe.wait_ge(g_o, h)
                for t in range(TOK):
                    o = ps[:, 5, t * DV:(t + 1) * DV]
                    pe.matmul(o, at_sb[:, e, t, :], z2[:, t, VG + h * DV:VG + (h + 1) * DV],
                              start=True, stop=False, skip_group_check=True)
                    parts = []
                    for half in range(2):
                        c = 2 * t + half
                        if c >= 1:
                            parts.append((half, 0, c, c - 1))
                        if c <= 2:
                            parts.append((half, 1, c, 2 - c))
                    for n, (half, d, c, i) in enumerate(parts):
                        mm = pe.matmul(ps[half * CHUNK:(half + 1) * CHUNK, 5, t * DV:(t + 1) * DV],
                                       fac[:, d, QI, h, c * CHUNK:(c + 1) * CHUNK], state[:, e, d, i, :],
                                       start=False, stop=(n == len(parts) - 1), skip_group_check=True)
                mm.then_inc(g_O, 1)

            gla_A(0)
            for h in range(GH):
                gla_S(h)
                if h + 1 < GH:
                    gla_A(h + 1)
                gla_O(h)

            for n in range(8):
                if n == 0:
                    pe.wait_ge(g_o, GH)
                if n == 4:
                    pe.wait_ge(mix2_ready, 1)
                fill(F_MIX2 + n, z2 if n < 4 else z2[:, :, QG:QG + 2 * NB], n % 4)
            for n in range(8):
                pe.wait_ge(tp_free, F_MIX2 + n + 1)
                gemm_tile(T_OUT2 + n, 0, H, 2 * n, pair(0), n == 0, n == 7)
            rows_rest(T_OUT2, H, [2] * 8)

            def ff2_turn(j, half):
                pe.wait_ge(gemm_free[half], G_FF2 + 1 + j)
                for c in range(4):
                    for t in range(TOK):
                        mm = pe.transpose(ps[:, 4 + 2 * half + c // 2, (c % 2) * SEQ + t * P:(c % 2) * SEQ + (t + 1) * P],
                                          raw_s[:, t, c * P:(c + 1) * P], ident[:])
                mm.then_inc(ct_ready, 1)

            with_fills(T_FF2, F_XT4, x_sb, lambda n: pe.wait_ge(x_new, 12), pair(0))
            ff_tiles(T_FF2 + 8, 0, 1, 0, 4)
            pe.wait_ge(tp_free, F_XT4 + 8)
            ff2_turn(0, 0)
            ff_tiles(T_FF2 + 8, 0, 1, 4, 8)
            with pe.Fori(1, FB) as j:
                pe.wait_ge(gemm_free[0], G_FF2 + j)
                ff_tiles(T_FF2, 16 * j, 0, 0, 4)
                pe.wait_ge(ct_free, 2 * j - 1)
                ff2_turn(j - 1, 1)
                ff_tiles(T_FF2, 16 * j, 0, 4, 8)
                pe.wait_ge(gemm_free[1], G_FF2 + j)
                ff_tiles(T_FF2 + 8, 16 * j, 1, 0, 4)
                pe.wait_ge(ct_free, 2 * j)
                ff2_turn(j, 0)
                ff_tiles(T_FF2 + 8, 16 * j, 1, 4, 8)
            pe.wait_ge(gemm_free[0], G_FF2 + FB)
            rows_tiles(T_DN2, 0, A, DN_TILES, 0, 4, pair(0))
            pe.wait_ge(ct_free, 2 * FB - 1)
            ff2_turn(FB - 1, 1)
            rows_tiles(T_DN2, 0, A, DN_TILES, 4, 20, pair(0))
            pe.wait_ge(aT_ready, FB)
            rows_tiles(T_DN2, 0, A, DN_TILES, 20, 24, pair(0))
            rows_rest(T_DN2, A, DN_TILES)

        @block.scalar
        def _(act):
            done = [0]

            def split_hi(c0, step):
                kc, width = SHAPES[c0]
                s = c0 % RING
                act.wait_ge(raw_landed[s], landed(c0, step))
                if c0 >= RING:
                    act.wait_ge(tile_used, c0 - RING + 1 + step)
                act.activation(w_hi[:, s, :kc, :width], raw[:, s, :kc, :width], ACT.Copy).then_inc(hi_ready, 1)

            def hi_upto(n):
                for g in range(done[0], n):
                    split_hi(g, 0)
                done[0] = n

            def hi_tiles(c0, step, lo, hi):
                for g in range(c0 + lo, c0 + hi):
                    split_hi(g, step)

            count = [0]

            def step(ins):
                count[0] += 1
                ins.then_inc(act_step, 1)
                act.wait_ge(act_step, count[0])

            def fill_hi(F, dst, k, gain=None, bank=None):
                act.wait_ge(tp_ready, F + 1)
                b = 4 + F % 4
                for i in range(2):
                    at = G_AT[gain[0]] + gain[1] + i if gain else None
                    ins = act.activation(dst[:, k + i, :], ps[:, b, i * SEQ:(i + 1) * SEQ], ACT.Copy,
                                         **({"scale": gains[:, at:at + 1]} if gain else {}))
                ins.then_inc(tp_hi, 1)

            def squares(out, in_, name, at):
                return act.activation(out, in_, ACT.Square, accum_out=r_of(ss, name, at, 1))

            n = 0
            for name, k in GAINS:
                act.dma_start(rows[n:n + k, 0, :], a[name].rearrange("o (c p) -> (o c) p", p=P)).then_inc(rows_landed, 16)
                n += k
            taps = a["conv_w"][0].rearrange("k (c p) -> (k c) p", p=P)
            act.dma_start(rows[:, 1, :], taps[0:P, :]).then_inc(params_landed, 16)
            act.dma_start(rows[0:TAPS * CC - P, 2, :], taps[P:TAPS * CC, :]).then_inc(params_landed, 16)
            for k in range(3):
                act.dma_start(rows[0:2 * FC, 3 + k, :], a["conv_w_2"][0, k:k + 1, :].rearrange("o (c p) -> (o c) p", p=P))\
                   .then_inc(params_landed, 16)
            act.dma_start(rows[0:2 * FC, 6, :], a["conv_b_2"].rearrange("o (c p) -> (o c) p", p=P)).then_inc(params_landed, 16)
            act.dma_start(invf[:], a["inv_freq"].to_broadcast([P, 96])).then_inc(params_landed, 16)
            act.dma_start(kpe[:, 0, 0:TOK].bitcast(I32), a["positions"].rearrange("o (t p) -> p (o t)", p=P),
                          allow_slow_non_contiguous=True)\
               .then_inc(params_landed, 16)
            act.dma_start(sinkb[:], a["attn_sink_2"].to_broadcast([P, HEADS])).then_inc(params_landed, 16)

            act.wait_ge(rows_T, 1)
            act.activation(gains[:], ps[:, 0, 0:G_ROWS], ACT.Copy).then_inc(gains_ready, 1)
            act.wait_ge(gains_ready, 1)
            for n in range(8):
                fill_hi(F_XT1 + n, hT_hi, 2 * n, ("pre_mix_norm", 2 * n))
                if n == 3:
                    act.wait_ge(rows_T, 2)
                    act.activation(convw[:], ps[:, 2, 0:TAPS * CC], ACT.Copy).then_inc(gains_ready, 1)
                    act.wait_ge(rows_T, 3)
                    act.activation(conv2[:].rearrange("p k c -> p (k c)"), ps[:, 3, 0:8 * FC], ACT.Copy).then_inc(gains_ready, 1)
                hi_upto(n + 1)
            act.wait_ge(x_landed, 16 * TOK)
            for t in range(TOK):
                ins = squares(kv1[:, t, :], x_sb[:, t, :], "x0", t)
            ins.then_inc(sq_done, 1)
            hi_upto(11)

            def scaled(B, gend, dst, name, at, width, func=ACT.Copy, free=True):
                act.wait_ge(tile_used, gend)
                for t in range(TOK):
                    ins = act.activation(dst(t), ps[:, 2 * (B % 2) + t, :width], func, scale=r_of(rstd, name, at + t, 1))
                ins.then_inc(gemm_free[B % 2], 1)

            act.wait_ge(rstd_ready, r_count("x0"))
            scaled(0, T_IN1 + 8, lambda t: a_s[:, t, :], "x0", 0, NB)
            hi_upto(19)
            scaled(1, T_IN1 + 16, lambda t: sg_s[:, t, :], "x0", 0, NB, ACT.Sigmoid)

            def cu_evac(g):
                for f in range(2):
                    act.wait_ge(cu_ready, 2 * g + f + 1)
                    c = 4 * g + 2 * f
                    act.activation(uT[:, c:c + 2, TAPS - 1:], ps[:, 6 + f, :].rearrange("p (c s) -> p c s", c=2),
                                   ACT.Copy).then_inc(cu_free, 1)

            hi_upto(23)
            cu_evac(0)
            act.wait_ge(trig_arg, 1)
            tt = [trig_t[:, i, :].rearrange("p (t n) -> p t n", t=TOK) for i in range(4)]
            act.activation(tt[1], tt[0], ACT.Abs).then_inc(trig_abs, 1)
            act.wait_ge(trig_arg, 2)
            act.activation(trig[:, :, 0, :], tt[2], ACT.Sin)
            act.activation(trig[:, :, 1, :], tt[0], ACT.Sin).then_inc(trig_done, 1)
            hi_upto(27)
            scaled(2, T_IN1 + 24, lambda t: a_s[:, t, :], "x0", 0, NB)
            hi_upto(35)
            scaled(3, T_IN1 + 32, lambda t: sg_s[:, t, :], "x0", 0, NB, ACT.Sigmoid)
            hi_upto(39)
            cu_evac(1)
            hi_upto(43)

            def z1_block(b):
                act.wait_ge(tile_used, T_IN1 + 8 * (b + 5))
                for t in range(TOK):
                    ins = act.activation(z1[:, t, b * 448:(b + 1) * 448], ps[:, 2 * (b % 2) + t, :448], ACT.Copy,
                                         scale=r_of(rstd, "x0", t, 1))
                ins.then_inc(gemm_free[b % 2], 1)

            z1_block(0)
            hi_upto(51)
            z1_block(1)
            in_sbuf(act, 5)
            for t in range(TOK):
                squares(q1[:, t, 0:QL], z1[:, t, 0:QL], "lat", t)
            hi_upto(55)
            for n in range(3):
                fill_hi(F_LAT + n, latT_hi, 2 * n, ("q_norm", 2 * n))
            hi_upto(59)
            z1_block(2)
            in_sbuf(act, 6)
            for t in range(TOK):
                ins = squares(q1[:, t, QL:QL + KVL], z1[:, t, QL:QL + KVL], "lat", 2 + t)
            ins.then_inc(sq_done, 1)
            hi_upto(62)
            for n in range(2):
                fill_hi(F_LAT + 3 + n, latT_hi, QC + 2 * n, ("kv_norm", 2 * n))
            act.wait_ge(rstd_ready, r_count("lat"))
            for b in range(3):
                scaled(7 + b, T_UQ + 3 * (b + 1), lambda t: q1[:, t, b * NB:(b + 1) * NB], "lat", 0, NB)
                hi_upto([65, 67, 69][b])
            for b in range(4):
                scaled(10 + b, T_UKV + 2 * (b + 1), lambda t: kv1[:, t, b * NB:(b + 1) * NB], "lat", 2, NB)
                hi_upto([71, 73, 75, 77][b])

            act.wait_ge(kpe_ready, 2)
            act.activation(kpeT[:, :], ps[0:ROPE, 5, 0:SEQ], ACT.Copy).then_inc(kpe_ready, 1)

            def attn1_qk(h):
                b, e = 4 * (h % 2), h % 2
                act.wait_ge(at_T, h + 1)
                if h >= 2:
                    act.wait_ge(at_S, h - 1)
                act.activation(qkT[:, e].rearrange("p i s -> p (i s)"), ps[:, b, :], ACT.Copy)
                act.activation(qpeT[:, e, :], ps[0:ROPE, b + 1, 0:SEQ], ACT.Copy).then_inc(at_qk, 1)

            def attn_exp(h, h0, src, scale):
                e = h % 2
                act.wait_ge(at_max, h0 + h + 1)
                for t in range(TOK):
                    ins = act.activation(src(e, t), src(e, t), ACT.Exp, bias=amax[:, e, t, 2:3], scale=scale,
                                         accum_out=asum[:, e, 0, t:t + 1])
                ins.then_inc(at_exp, 1)

            def attn_pT(h, h0, dst, n):
                b, e = 4 * (h % 2), h % 2
                act.wait_ge(at_PT, h0 + h + 1)
                act.activation(dst(e), ps[:, b + 3, 0:n * P], ACT.Copy).then_inc(at_pT, 1)

            def s1(e, t):
                return att1_s[:, e, t * P:t * P + (t + 1) * P]

            attn1_qk(0)
            for h in range(HEADS + 1):
                if h + 1 < HEADS:
                    attn1_qk(h + 1)
                if h >= 1:
                    attn_pT(h - 1, 0, lambda e: att1_p[:, e, :], 3)
                if h < HEADS:
                    attn_exp(h, 0, s1, float(QKH) ** -0.5)
            act.wait_ge(at_out, HEADS)
            for t in range(TOK):
                ins = squares(kv1[:, t, 0:CONV], attn1[:, t, :], "attn", t)
            ins.then_inc(sq_done, 1)

            act.wait_ge(ln_dve, 1)
            act.activation(lnsq[:], cv[:], ACT.Square).then_inc(ln_act, 1)
            act.wait_ge(ln_dve, 3)
            for c in range(CC):
                g, b = G_AT["conv_ln_g"] + c, G_AT["conv_ln_b"] + c
                ins = act.activation(cv[:, c, :], cv[:, c, :], ACT.Silu, scale=gains[:, g:g + 1], bias=gains[:, b:b + 1])
            ins.then_inc(ln_act, 1)
            act.wait_ge(ln_act, 2)
            act.activation(lnsq[:], cv[:], ACT.Square).then_inc(ln_act, 1)
            for c in range(CC):
                g = G_AT["conv_out_norm"] + c
                ins = act.activation(hT_hi[:, c, :], cv[:, c, :], ACT.Copy, scale=gains[:, g:g + 1])
            ins.then_inc(ln_act, 1)
            for n in range(4):
                fill_hi(F_MIX1 + n, hT_hi, CC + 2 * n, ("attn_out_norm", 2 * n))
            act.wait_ge(mix_conv, 1)
            act.wait_ge(at_PV, HEADS)
            act.wait_ge(tp_free, F_MIX1 + 4)
            act.dma_start(grow_out[:], a["post_mix_norm"].to_broadcast([P, DM])).then_inc(grow_landed, 16)

            def row_squares(c_end, step, n, y, name, scale):
                act.wait_ge(tile_used, c_end + step)
                for t in range(TOK):
                    at = R[name][0]
                    ins = act.activation(y[:, bass.ts(2 * n + t, NB)], ps_flat[:, bass.ts(2 * n + t, NB)], ACT.Square,
                                         accum_out=ss4[:, bass.ts(4 * t + n, 1)],
                                         **({"scale": r_of(rstd, scale, t, 1)} if scale else {}))
                ins.then_inc(row_sq, 1)

            act.wait_ge(rstd_ready, r_count("conv"))
            hi_upto(T_OUT1 + 8)
            c0, T = T_OUT1, 8
            with act.Fori(1, 4) as n:
                hi_tiles(c0, n * T, 0, 3)
                row_squares(c0, n * T, n - 1, y_out, "out1", "conv")
                hi_tiles(c0, n * T, 3, T)
            done[0] = T_FF1
            hi_upto(T_FF1 + 3)
            row_squares(T_FF1, 0, 3, y_out, "out1", "conv")

            def x_squares(base, junk, name):
                act.wait_ge(x_new, base + 4)
                for t in range(TOK):
                    ins = squares(junk(t), x_sb[:, t, :], name, t)
                ins.then_inc(sq_done, 1)

            def with_fills(c0, F, gain):
                hi_upto(c0 + 4)
                for n in range(4):
                    fill_hi(F + n, hT_hi, 2 * n, (gain, 2 * n))
                for n in range(4, 8):
                    fill_hi(F + n, hT_hi, 2 * n, (gain, 2 * n))
                    hi_upto(c0 + n + 1)

            with_fills(T_FF1, F_XT2, "pre_ffn_norm")
            x_squares(0, lambda t: y_out[:, t * DM:(t + 1) * DM], "x1")
            act.wait_ge(rstd_ready, r_count("x1"))

            def silu1(j):
                act.wait_ge(tile_used, T_FF1 + 8 + 16 * j)
                for t in range(TOK):
                    ins = act.activation(gate_s[:, t, :], ps[:, t, :], ACT.Silu, scale=r_of(rstd, "x1", t, 1))
                ins.then_inc(gemm_free[0], 1)

            def turn_hi(j):
                for f in range(2):
                    act.wait_ge(tp_ready, F_FF1 + f + 1 + 2 * j)
                    act.activation(aT_hi_flat[:, bass.ts(2 * j + f, 2 * SEQ)], ps[:, 4 + f, :], ACT.Copy).then_inc(tp_hi, 1)

            aT_hi_flat = aT_hi[:].rearrange("p c s -> p (c s)")
            hi_upto(T_FF1 + 11)
            silu1(0)
            hi_upto(T_FF1 + 16)
            with act.Fori(1, FB) as j:
                hi_tiles(T_FF1, 16 * j, 0, 7)
                turn_hi(j - 1)
                hi_tiles(T_FF1, 16 * j, 7, 11)
                act.wait_ge(gemm_free[1], G_FF1 + j)
                silu1(j)
                hi_tiles(T_FF1, 16 * j, 11, 16)
            done[0] = T_DN1
            hi_upto(T_DN1 + 7)
            turn_hi(FB - 1)
            act.dma_start(grow_dn[:], a["post_ffn_norm"].to_broadcast([P, DM])).then_inc(grow_landed, 16)
            hi_upto(T_DN1 + 24)
            c0, T = T_DN1, 24
            with act.Fori(1, 4) as n:
                hi_tiles(c0, n * T, 0, 3)
                row_squares(c0, n * T, n - 1, y_dn, "dn1", None)
                hi_tiles(c0, n * T, 3, T)
            done[0] = T_IN2
            hi_upto(T_IN2 + 3)
            row_squares(T_IN2, 0, 3, y_dn, "dn1", None)

            act.wait_ge(row_y, 8)
            for i, name in enumerate(("attn_q_norm_g_2", "attn_k_norm_g_2")):
                act.dma_start(gqk[:, i, :], a[name].to_broadcast([P, HD])).then_inc(late_landed, 16)
            act.dma_start(gla_g[:], a["gla_out_norm_g_2"].to_broadcast([P, DV])).then_inc(late_landed, 16)
            for d, name in enumerate(("fwd", "bwd")):
                act.dma_start(wa2[0:RANK, d, :], a[f"gla_wa2_{name}_2"][0]).then_inc(late_landed, 16)
                act.dma_start(wa2[RANK:RANK + 1, d, :], a[f"gla_ba_{name}_2"]).then_inc(late_landed, 16)
            with_fills(T_IN2, F_XT3, "norm1_g_2")
            x_squares(4, lambda t: fac[:, t].rearrange("p a h s -> p (a h s)")[:, 0:DM], "x2")
            act.wait_ge(rstd_ready, r_count("x2"))

            def z2_block(p):
                n = B2_ORDER[p]
                act.wait_ge(tile_used, T_IN2 + 8 * (p + 1))
                for t in range(TOK):
                    ins = act.activation(z2[:, t, n * W2:(n + 1) * W2], ps[:, 2 * (p % 2) + t, :W2], ACT.Copy,
                                         scale=r_of(rstd, "x2", t, 1))
                ins.then_inc(gemm_free[p % 2], 1)

            b_sum = [gb[:, 1, d, :].rearrange("p (h s) -> p h s", h=GH) for d in range(2)]
            hi_upto(T_IN2 + 11)
            z2_block(0)
            hi_upto(T_IN2 + 15)
            act.wait_ge(gl_mm, 1)
            act.wait_ge(consts_ready, 3)
            act.activation(lrT[0:RANK].rearrange("p d s -> p (d s)"), ps[0:RANK, 4, :], ACT.Copy).then_inc(gl_act, 1)
            hi_upto(T_IN2 + 19)
            z2_block(1)
            act.wait_ge(gl_mm, 2)
            for d in range(2):
                for t in range(TOK):
                    g = gb[:, 0, d, t * NB:(t + 1) * NB]
                    step(act.activation(g, ps[:, 4 + 2 * d + t, :], ACT.Abs))
            step(act.activation(gb[:, 0], gb[:, 0], ACT.Exp, scale=-1.0))
            act.activation(gb[:, 0], gb[:, 0], ACT.Ln, bias=1.0).then_inc(gl_act, 1)
            hi_upto(T_IN2 + 27)
            z2_block(2)
            hi_upto(T_IN2 + 31)
            act.wait_ge(gl_mm, 3)
            for d in range(2):
                for i in range(2):
                    ins = act.activation(gb[:, 1, d, i * NB:(i + 1) * NB], ps[:, 4 + 2 * d + i, :], ACT.Copy)
            ins.then_inc(gl_act, 1)
            hi_upto(T_IN2 + 35)
            z2_block(3)
            hi_upto(T_IN2 + 43)
            z2_block(4)
            act.wait_ge(gl_mm, 4)
            for i in range(2):
                act.activation(qT2[:, 2 * i:2 * i + 2, :], ps[:, 4 + i, :].rearrange("p (h s) -> p h s", h=2), ACT.Copy,
                               scale=float(DK) ** -0.5)
                ins = act.activation(kT2[:, 2 * i:2 * i + 2, :], ps[:, 6 + i, :].rearrange("p (h s) -> p h s", h=2), ACT.Copy)
            ins.then_inc(gl_act, 1)
            S16 = 1.0 / 16.0
            for d in range(2):
                dd = [gb[:, 0, i, :].rearrange("p (h s) -> p h s", h=GH) for i in range(2)]
                act.wait_ge(fac_exp, 2 * d + 1)
                act.activation(fac[:, d, 0], dd[0], ACT.Exp, scale=S16)
                act.activation(fac[:, d, 1], dd[0], ACT.Exp, scale=-S16)
                hi_upto(T_IN2 + 45 + 4 * d)
                act.activation(fac[:, d, 2], b_sum[d], ACT.Exp, scale=S16)
                act.activation(decay[:, d, :], last_of(b_sum[d], d), ACT.Exp, scale=S16)
                act.activation(fac[:, d, 3], dd[1], ACT.Exp, scale=-S16).then_inc(fac_exp, 1)
                hi_upto(T_IN2 + 47 + 4 * d)
            z2_block(5)
            for p in range(6, 10):
                hi_upto(T_IN2 + 8 * p + 11)
                if p == 9:
                    act.wait_ge(fac_ready, 2)
                    in_sbuf(act, 7, G_IN2)
                    in_sbuf(act, 8, G_IN2)
                    act.activation(gb_flat[:, 0:2560].rearrange("p (t n) -> p t n", t=TOK), z2[:, :, 0:1280],
                                   ACT.Square).then_inc(sq_done, 1)
                z2_block(p)

            act.wait_ge(kpe_ready, 4)
            act.activation(kaT[:].rearrange("p g s -> p (g s)"), ps[:, 4, :], ACT.Copy).then_inc(kpe_ready, 1)

            def attn2_qk(h):
                b, e = 4 * (h % 2), h % 2
                act.wait_ge(at_T, HEADS + h + 1)
                if h >= 2:
                    act.wait_ge(at_S, HEADS + h - 1)
                act.activation(att2_q[:, e, :], ps[:, b, 0:SEQ], ACT.Copy).then_inc(at_qk, 1)

            attn2_qk(0)
            for h in range(HEADS + 1):
                if h + 1 < HEADS:
                    attn2_qk(h + 1)
                if h >= 1:
                    attn_pT(h - 1, HEADS, lambda e: att2_p[:, e].rearrange("p k s -> p (k s)"), 4)
                if h < HEADS:
                    e = h % 2
                    act.wait_ge(at_max, HEADS + h + 1)
                    for t in range(TOK):
                        act.activation(amax[:, e, t, 3:4], sinkb[:, h:h + 1], ACT.Exp, bias=amax[:, e, t, 2:3])
                    attn_exp(h, HEADS, lambda e, t: att2_s[:, e, t, :], float(HD) ** -0.5)

            for h in range(GH):
                e = h % 2
                act.wait_ge(g_KT, h + 1)
                if h >= 2:
                    act.wait_ge(g_SS, h - 1)
                act.activation(ktok[:, e].rearrange("p d t k -> p (d t k)"), ps[:, 1, :], ACT.Copy).then_inc(g_kt, 1)
            for h in range(GH):
                act.wait_ge(g_o, h + 1)
                for t in range(TOK):
                    ins = act.activation(fac[:, t, 0, 0, :], z2[:, t, QG + h * DV:QG + (h + 1) * DV], ACT.Square,
                                         accum_out=r_of(ss, "gla", t * GH + h, 1))
                    if h < GH - 1 or t < TOK - 1:
                        step(ins)
            ins.then_inc(sq_done, 1)
            in_sbuf(act, 8, G_IN2)
            in_sbuf(act, 9, G_IN2)
            act.activation(z2[:, :, GG:GG + 2 * NB], z2[:, :, GG:GG + 2 * NB], ACT.Silu).then_inc(gate2_ready, 1)
            for n in range(8):
                F = F_MIX2 + n
                act.wait_ge(tp_ready, F + 1)
                act.activation(hT_hi[:, 2 * n:2 * n + 2, :], ps[:, 4 + F % 4, :].rearrange("p (c s) -> p c s", c=2),
                               ACT.Copy).then_inc(tp_hi, 1)
            hi_upto(T_OUT2 + 8)
            with act.Fori(1, 4) as n:
                hi_tiles(T_OUT2, 8 * n, 0, 8)
            done[0] = T_FF2

            with_fills(T_FF2, F_XT4, "norm2_g_2")
            x_squares(8, lambda t: y_out[:, t * DM:(t + 1) * DM], "x3")
            act.wait_ge(rstd_ready, r_count("x3"))

            def copy2(j, half):
                act.wait_ge(tile_used, T_FF2 + 8 + 8 * half + 16 * j)
                for t in range(TOK):
                    ins = act.activation(raw_s[:, t, :], ps[:, 2 * half + t, :], ACT.Copy, scale=r_of(rstd, "x3", t, 1))
                ins.then_inc(gemm_free[half], 1)

            def center2(j, half):
                act.wait_ge(ct_ready, 2 * j + half + 1)
                dst = cg if half == 0 else cval
                for c in range(4):
                    k = 4 * j + c + FC * half
                    ins = act.activation(dst[:, c, :], ps[:, 4 + 2 * half + c // 2, (c % 2) * SEQ:(c % 2 + 1) * SEQ],
                                         ACT.Identity, scale=conv2[:, 1, bass.ts(k, 1)], bias=conv2[:, 3, bass.ts(k, 1)])
                    if c % 2:
                        ins.then_inc(ct_center, 1)

            def silu2(j):
                act.wait_ge(ct_free, 2 * j + 1)
                act.activation(cg[:], cg[:], ACT.Silu).then_inc(cg_silu, 1)

            def hidden_hi(j):
                act.wait_ge(prod_ready, j + 1)
                act.activation(aT_hi_flat[:, bass.ts(j, 4 * SEQ)], cg[:].rearrange("p c s -> p (c s)"), ACT.Copy)\
                   .then_inc(aT_hi_ready, 1)

            hi_upto(T_FF2 + 11)
            copy2(0, 0)
            hi_upto(T_FF2 + 15)
            center2(0, 0)
            hi_upto(T_FF2 + 16)
            with act.Fori(1, FB) as j:
                hi_tiles(T_FF2, 16 * j, 0, 2)
                silu2(j - 1)
                hi_tiles(T_FF2, 16 * j, 2, 3)
                act.wait_ge(ct_ready, 2 * j - 1)
                copy2(j - 1, 1)
                hi_tiles(T_FF2, 16 * j, 3, 7)
                center2(j - 1, 1)
                hi_tiles(T_FF2, 16 * j, 7, 11)
                act.wait_ge(ct_ready, 2 * j)
                copy2(j, 0)
                hidden_hi(j - 1)
                hi_tiles(T_FF2, 16 * j, 11, 15)
                act.wait_ge(aT_ready, j)
                center2(j, 0)
                hi_tiles(T_FF2, 16 * j, 15, 16)
            done[0] = T_DN2
            hi_upto(T_DN2 + 2)
            silu2(FB - 1)
            hi_upto(T_DN2 + 3)
            act.wait_ge(ct_ready, 2 * FB - 1)
            copy2(FB - 1, 1)
            hi_upto(T_DN2 + 7)
            center2(FB - 1, 1)
            hi_upto(T_DN2 + 11)
            hidden_hi(FB - 1)
            hi_upto(T_DN2 + 24)
            with act.Fori(1, 4) as n:
                hi_tiles(T_DN2, 24 * n, 0, 24)

        @block.vector
        def _(dve):
            done = [0]
            count = [0]

            def split_lo(c0, step):
                kc, width = SHAPES[c0]
                s = c0 % RING
                dve.wait_ge(hi_ready, c0 + 1 + step)
                dve.tensor_tensor(w_lo[:, s, :kc, :width], raw[:, s, :kc, :width],
                                  w_hi[:, s, :kc, :width].bitcast(F32), ALU.subtract).then_inc(lo_ready, 1)

            def lo_upto(n):
                for g in range(done[0], n):
                    split_lo(g, 0)
                done[0] = n

            def lo_tiles(c0, step, lo, hi):
                for g in range(c0 + lo, c0 + hi):
                    split_lo(g, step)

            def step(ins):
                count[0] += 1
                ins.then_inc(dve_step, 1)
                dve.wait_ge(dve_step, count[0])

            def fill_lo(F, hi, lo, k, gain=None):
                dve.wait_ge(tp_hi, F + 1)
                b = 4 + F % 4
                for i in range(2):
                    src = ps[:, b, i * SEQ:(i + 1) * SEQ]
                    h = hi[:, k + i, :].bitcast(F32)
                    if gain:
                        at = G_AT[gain[0]] + gain[1] + i
                        ins = dve.scalar_tensor_tensor(out=lo[:, k + i, :], in0=src, scalar=gains[:, at:at + 1],
                                                       in1=h, op0=ALU.mult, op1=ALU.subtract)
                    else:
                        ins = dve.tensor_tensor(lo[:, k + i, :], src, h, ALU.subtract)
                ins.then_inc(tp_free, 1)

            def mean_sq(name, width, src=None):
                dve.tensor_scalar(r_of(ms, name), r_of(ss, name) if src is None else src, 1.0 / width, EPS, ALU.mult,
                                  ALU.add).then_inc(ms_ready, 1)

            dve.memset(ones[:], 1.0).then_inc(consts_ready, 1)
            dve.memset(minus_half[:], -0.5).then_inc(consts_ready, 1)
            step(dve.memset(uT[:, :, 0:TAPS - 1], 0.0))
            for n in range(4):
                if n == 0:
                    dve.wait_ge(gains_ready, 1)
                fill_lo(F_XT1 + n, hT_hi, hT_lo, 2 * n, ("pre_mix_norm", 2 * n))
                lo_upto(n + 1)
            for n in range(4, 8):
                fill_lo(F_XT1 + n, hT_hi, hT_lo, 2 * n, ("pre_mix_norm", 2 * n))
                lo_upto(n + 1)
            dve.wait_ge(sq_done, 1)
            mean_sq("x0", DM)
            lo_upto(12)

            TWO_PI = 2.0 * np.pi
            C1 = 6.28125
            C2 = float(np.float32(np.round((TWO_PI - C1) * 2 ** 21) / 2 ** 21))
            C3 = float(np.float32(TWO_PI - C1 - C2))
            ROUND = 12582912.0
            PI_IN = 3.1415925
            dve.wait_ge(params_landed, 16 * 9)
            dve.wait_ge(masks_ready, 1)
            dve.wait_ge(gains_ready, 3)
            step(dve.tensor_copy(posf[:, 0, :], kpe[:, 0, 0:TOK].bitcast(I32)))
            tt = [trig_t[:, i, :].rearrange("p (t n) -> p t n", t=TOK) for i in range(4)]
            for t in range(TOK):
                dve.tensor_scalar(tt[0][:, t, 0:32], invf[:, 0:32], posf[:, 0, t:t + 1], None, ALU.mult)
                ins = dve.tensor_scalar(tt[0][:, t, 32:96], invf[:, 32:96], posf[:, 1, t:t + 1], None, ALU.mult)
            step(ins)
            step(dve.tensor_scalar(tt[1], tt[0], float(1.0 / TWO_PI), None, ALU.mult))
            step(dve.tensor_scalar(tt[1], tt[1], ROUND, None, ALU.add))
            step(dve.tensor_scalar(tt[1], tt[1], -ROUND, None, ALU.add))
            lo_upto(14)
            for c in (C1, C2, C3):
                step(dve.scalar_tensor_tensor(out=tt[0], in0=tt[1], scalar=-c, in1=tt[0], op0=ALU.mult, op1=ALU.add))
            dve.tensor_scalar(tt[0], tt[0], PI_IN, -PI_IN, ALU.min, ALU.max).then_inc(trig_arg, 1)
            lo_upto(16)
            lo_upto(19)

            def gate_u(g):
                dve.wait_ge(gemm_free[1], g + 1)
                dve.tensor_tensor(a_s, a_s, sg_s, ALU.mult).then_inc(u_ready, 1)

            gate_u(0)
            lo_upto(23)
            dve.wait_ge(trig_abs, 1)
            dve.tensor_scalar(tt[2], tt[1], -1.0, float(np.pi / 2), ALU.mult, ALU.add).then_inc(trig_arg, 1)

            tap = [0]

            def taps(n):
                for _ in range(n):
                    i = tap[0]
                    if i == TAPS * CC:
                        return
                    g, r = divmod(i, 4 * TAPS)
                    j, c = divmod(r, 4)
                    c += 4 * g
                    if j == 0 and c == 4 * g:
                        dve.wait_ge(cu_free, 2 * g + 2)
                    w = convw[:, j * CC + c:j * CC + c + 1]
                    u = uT[:, c, j:j + SEQ]
                    if j == 0:
                        b = G_AT["conv_b"] + c
                        ins = dve.tensor_scalar(cv[:, c, :], u, w, gains[:, b:b + 1], ALU.mult, ALU.add)
                    else:
                        dve.wait_ge(conv_tap, i - 3)
                        ins = dve.scalar_tensor_tensor(out=cv[:, c, :], in0=u, scalar=w, in1=cv[:, c, :],
                                                       op0=ALU.mult, op1=ALU.add)
                    ins.then_inc(conv_tap, 1)
                    tap[0] += 1

            for g in range(24, 36):
                lo_upto(g)
                taps(4)
            gate_u(1)
            for g in range(36, 56):
                lo_upto(g)
                taps(4)
            for n in range(3):
                fill_lo(F_LAT + n, latT_hi, latT_lo, 2 * n, ("q_norm", 2 * n))
            for g in range(56, 60):
                lo_upto(g)
                taps(4)
            lo_upto(60)
            dve.wait_ge(sq_done, 2)
            at = R["lat"][0]
            dve.tensor_scalar(ms[:, at:at + 2], ss[:, at:at + 2], 1.0 / QL, EPS, ALU.mult, ALU.add)
            dve.tensor_scalar(ms[:, at + 2:at + 4], ss[:, at + 2:at + 4], 1.0 / KVL, EPS, ALU.mult,
                              ALU.add).then_inc(ms_ready, 1)
            lo_upto(62)
            for n in range(2):
                fill_lo(F_LAT + 3 + n, latT_hi, latT_lo, QC + 2 * n, ("kv_norm", 2 * n))
            for g in range(63, 71):
                lo_upto(g)
                taps(4)

            def rope(dst, src, half, heads, at, tmp, sem_done):
                x1, x2 = src[:, :, :, 0:half], src[:, :, :, half:2 * half]
                cos, sin = (trig[:, :, i, at:at + half].unsqueeze(2).to_broadcast([P, TOK, heads, half]) for i in range(2))
                t1, t2 = tmp
                dve.tensor_tensor(t1, x1, cos, ALU.mult)
                step(dve.tensor_tensor(t2, x2, sin, ALU.mult))
                dve.tensor_tensor(dst[:, :, :, 0:half], t1, t2, ALU.subtract)
                step(dve.tensor_tensor(dst[:, :, :, half:2 * half], x2, cos, ALU.mult))
                step(dve.tensor_tensor(t1, x1, sin, ALU.mult))
                dve.tensor_tensor(dst[:, :, :, half:2 * half], dst[:, :, :, half:2 * half], t1, ALU.add).then_inc(sem_done, 1)

            dve.wait_ge(trig_done, 1)
            in_sbuf(dve, 6)
            tmp = [z1[:, :, 512 + 256 * i:768 + 256 * i].rearrange("p t (h n) -> p t h n", h=HEADS) for i in range(2)]
            rope(kpe[:].unsqueeze(2), z1[:, :, QL + KVL:Z1].unsqueeze(2), 32, 1, 0, [t[:, :, 0:1, :] for t in tmp], kpe_ready)
            lo_upto(73)
            in_sbuf(dve, 8)
            in_sbuf(dve, 9)
            dve.wait_ge(kpe_ready, 1)
            rope(z1[:, :, 0:512].rearrange("p t (h n) -> p t h n", h=HEADS),
                 q1[:].rearrange("p t (h n) -> p t h n", h=HEADS)[:, :, :, NOPE:QKH], 32, HEADS, 0, tmp, rope_ready)
            lo_upto(77)

            def attn1_max(h):
                b, e = 4 * (h % 2), h % 2
                dve.wait_ge(at_S, h + 1)
                if h >= 2:
                    dve.wait_ge(at_PT, h - 1)
                step(dve.tensor_tensor(att1_s[:, e, :], ps[:, b + 2, 0:3 * P], mask1[:], ALU.add))
                dve.tensor_reduce(amax[:, e, 0, 0:1], att1_s[:, e, 0:P], X, ALU.max)
                step(dve.tensor_reduce(amax[:, e, 1, 0:1], att1_s[:, e, P:3 * P], X, ALU.max))
                dve.tensor_scalar(amax[:, e, :, 2:3], amax[:, e, :, 0:1], -float(QKH) ** -0.5, None,
                                  ALU.mult).then_inc(at_max, 1)

            def attn_out(h, h0, dst):
                b, e = 4 * (h % 2), h % 2
                dve.wait_ge(at_PV, h0 + h + 1)
                for t in range(TOK):
                    ins = dve.tensor_scalar(dst(t), ps[:, b + 3, t * P:(t + 1) * P], asum[:, e, 1, t:t + 1], None, ALU.mult)
                ins.then_inc(at_out, 1)

            for h in range(HEADS + 1):
                if h < HEADS:
                    attn1_max(h)
                if h >= 1:
                    e = (h - 1) % 2
                    dve.wait_ge(at_exp, h)
                    step(dve.reciprocal(asum[:, e, 1, :], asum[:, e, 0, :]))
                    taps(4)
                    attn_out(h - 1, 0, lambda t: attn1[:, t, (h - 1) * VD:h * VD])
            dve.wait_ge(sq_done, 3)
            mean_sq("attn", CONV)
            taps(TAPS * CC)

            dve.wait_ge(ln_mm, 1)
            dve.wait_ge(conv_tap, TAPS * CC)
            sums = ps[:, 0, 0:SEQ].unsqueeze(1).to_broadcast([P, CC, SEQ])
            dve.scalar_tensor_tensor(out=cv[:], in0=sums, scalar=-1.0 / CONV, in1=cv[:], op0=ALU.mult,
                                     op1=ALU.add).then_inc(ln_dve, 1)
            dve.wait_ge(rstd_ready, r_count("attn"))
            for t in range(TOK):
                ins = dve.tensor_scalar(attn1[:, t, :], attn1[:, t, :], r_of(rstd, "attn", t, 1), None, ALU.mult)
            step(ins)
            dve.wait_ge(ln_mm, 2)
            mean_sq("ln", CONV, ps[:, 1, 0:TOK])
            dve.wait_ge(rstd_ready, r_count("ln"))
            for t in range(TOK):
                ins = dve.tensor_scalar(lnsq[:, 0, t * P:(t + 1) * P], ident[:], r_of(rstd, "ln", t, 1), None, ALU.mult)
            ins.then_inc(ln_dve, 1)
            dve.wait_ge(ln_mm, 3)
            spread = ps[:, 0, 0:SEQ].unsqueeze(1).to_broadcast([P, CC, SEQ])
            dve.tensor_tensor(cv[:], spread, cv[:], ALU.mult).then_inc(ln_dve, 1)
            dve.wait_ge(ln_mm, 4)
            mean_sq("conv", CONV, ps[:, 1, 0:TOK])
            dve.wait_ge(rstd_ready, r_count("conv"))
            step(dve.reciprocal(r_of(ms, "attn"), r_of(rstd, "conv")))
            for t in range(TOK):
                ins = dve.tensor_scalar(attn1[:, t, :], attn1[:, t, :], ms[:, R["attn"][0] + t:R["attn"][0] + t + 1],
                                        None, ALU.mult)
            ins.then_inc(attn_scaled, 1)
            dve.wait_ge(ln_act, 4)
            for c in range(CC):
                g = G_AT["conv_out_norm"] + c
                ins = dve.scalar_tensor_tensor(out=hT_lo[:, c, :], in0=cv[:, c, :], scalar=gains[:, g:g + 1],
                                               in1=hT_hi[:, c, :].bitcast(F32), op0=ALU.mult, op1=ALU.subtract)
            ins.then_inc(mix_conv, 1)
            for n in range(4):
                fill_lo(F_MIX1 + n, hT_hi, hT_lo, CC + 2 * n, ("attn_out_norm", 2 * n))


            def row_scale(base, n, y, grow, scale):
                dve.wait_ge(row_sq, base + 1 + n)
                for t in range(TOK):
                    ins = dve.scalar_tensor_tensor(out=y[:, bass.ts(2 * n + t, NB)], in0=ps_flat[:, bass.ts(2 * n + t, NB)],
                                                   scalar=r_of(rstd, scale, t, 1) if scale else 1.0,
                                                   in1=grow[:, cols(n)], op0=ALU.mult, op1=ALU.mult)
                ins.then_inc(row_y, 1)

            def new_x(name, y, c_next):
                step(dve.tensor_reduce(r_of(ss, name), ss4.rearrange("p (t n) -> p t n", t=TOK), X, ALU.add))
                mean_sq(name, DM)
                lo_upto(c_next + 1)
                dve.wait_ge(rstd_ready, r_count(name))
                for n in range(4):
                    for t in range(TOK):
                        ins = dve.scalar_tensor_tensor(out=x_sb[:, t, cols(n)], in0=y[:, bass.ts(2 * n + t, NB)],
                                                       scalar=r_of(rstd, name, t, 1), in1=x_sb[:, t, cols(n)],
                                                       op0=ALU.mult, op1=ALU.add)
                    ins.then_inc(x_new, 1)

            def with_fills(c0, F, gain):
                for n in range(4):
                    fill_lo(F + n, hT_hi, hT_lo, 2 * n, (gain, 2 * n))
                    lo_upto(c0 + n + 1)
                for n in range(4, 8):
                    fill_lo(F + n, hT_hi, hT_lo, 2 * n, (gain, 2 * n))
                    lo_upto(c0 + n + 1)

            lo_upto(T_OUT1 + 8)
            dve.wait_ge(grow_landed, 16)
            with dve.Fori(1, 4) as n:
                lo_tiles(T_OUT1, 8 * n, 0, 3)
                row_scale(0, n - 1, y_out, grow_out, "conv")
                lo_tiles(T_OUT1, 8 * n, 3, 8)
            done[0] = T_FF1
            row_scale(0, 3, y_out, grow_out, "conv")
            dve.wait_ge(row_y, 4)
            new_x("out1", y_out, T_FF1)

            with_fills(T_FF1, F_XT2, "pre_ffn_norm")
            dve.wait_ge(sq_done, 4)
            mean_sq("x1", DM)
            lo_upto(T_FF1 + 16)
            dve.wait_ge(rstd_ready, r_count("x1"))

            def product(j):
                dve.wait_ge(gemm_free[0], G_FF1 + 1 + j)
                dve.wait_ge(tile_used, T_FF1 + 16 + 16 * j)
                for t in range(TOK):
                    ins = dve.scalar_tensor_tensor(out=prod_s[:, t, :], in0=ps[:, 2 + t, :], scalar=r_of(rstd, "x1", t, 1),
                                                   in1=gate_s[:, t, :], op0=ALU.mult, op1=ALU.mult)
                ins.then_inc(gemm_free[1], 1)

            aT_hi_flat = aT_hi[:].rearrange("p c s -> p (c s)")
            aT_lo_flat = aT_lo[:].rearrange("p c s -> p (c s)")

            def turn_lo(j):
                for f in range(2):
                    dve.wait_ge(tp_hi, F_FF1 + f + 1 + 2 * j)
                    dve.tensor_tensor(aT_lo_flat[:, bass.ts(2 * j + f, 2 * SEQ)], ps[:, 4 + f, :],
                                      aT_hi_flat[:, bass.ts(2 * j + f, 2 * SEQ)].bitcast(F32),
                                      ALU.subtract).then_inc(tp_free, 1)

            with dve.Fori(1, FB) as j:
                lo_tiles(T_FF1, 16 * j, 0, 3)
                product(j - 1)
                lo_tiles(T_FF1, 16 * j, 3, 7)
                turn_lo(j - 1)
                lo_tiles(T_FF1, 16 * j, 7, 16)
            done[0] = T_DN1
            lo_upto(T_DN1 + 3)
            product(FB - 1)
            lo_upto(T_DN1 + 7)
            turn_lo(FB - 1)
            lo_upto(T_DN1 + 24)
            dve.wait_ge(grow_landed, 32)
            with dve.Fori(1, 4) as n:
                lo_tiles(T_DN1, 24 * n, 0, 3)
                row_scale(4, n - 1, y_dn, grow_dn, None)
                lo_tiles(T_DN1, 24 * n, 3, 24)
            done[0] = T_IN2
            row_scale(4, 3, y_dn, grow_dn, None)
            dve.wait_ge(row_y, 8)
            dve.memset(lrT[:], 1.0).then_inc(consts_ready, 1)
            new_x("dn1", y_dn, T_IN2)

            with_fills(T_IN2, F_XT3, "norm1_g_2")
            dve.wait_ge(sq_done, 5)
            mean_sq("x2", DM)
            lo_upto(T_IN2 + 20)
            dve.wait_ge(gl_act, 2)
            for d in range(2):
                for t in range(TOK):
                    g = gb[:, 0, d, t * NB:(t + 1) * NB]
                    ins = dve.scalar_tensor_tensor(out=g, in0=ps[:, 4 + 2 * d + t, :], scalar=0.0, in1=g,
                                                   op0=ALU.min, op1=ALU.subtract)
            ins.then_inc(gl_dve, 1)
            lo_upto(T_IN2 + 36)
            dd = [gb[:, 0, i, :].rearrange("p (g s) -> p g s", s=CHUNK) for i in range(2)]
            dve.wait_ge(gl_act, 3)
            for d in range(2):
                b = gb[:, 1, d, :].rearrange("p (g s) -> p g s", s=CHUNK)
                ref, last = (CHUNK // 2, CHUNK - 1) if d == 0 else (CHUNK // 2 - 1, 0)
                if d == 1:
                    dve.wait_ge(fac_exp, 2)
                for i, r in enumerate((ref, last)):
                    ins = dve.tensor_tensor(dd[i], b, b[:, :, r:r + 1].to_broadcast([P, GH * NCH, CHUNK]), ALU.subtract)
                ins.then_inc(fac_exp, 1)
                lo_upto(T_IN2 + 44 + 4 * d)
                dve.wait_ge(gl_act, 4)
                dve.wait_ge(fac_exp, 2 * d + 2)
                for i, src in enumerate((qT2, kT2, qT2, kT2)):
                    ins = dve.tensor_tensor(fac[:, d, i], fac[:, d, i], src[:], ALU.mult)
                    if i % 2 == 0:
                        lo_upto(done[0] + 1)
                ins.then_inc(fac_ready, 1)
            lo_upto(T_IN2 + 80)

            in_sbuf(dve, 7, G_IN2)
            in_sbuf(dve, 8, G_IN2)
            dve.wait_ge(late_landed, 16 * 7)
            dve.wait_ge(sq_done, 6)
            sq = gb_flat[:, 0:2560].rearrange("p (t h n) -> p (t h) n", t=TOK, n=HD)
            step(dve.tensor_reduce(r_of(ss, "qk"), sq, X, ALU.add))
            mean_sq("qk", HD)
            dve.wait_ge(rstd_ready, r_count("qk"))
            qk = z2[:, :, 0:1280].rearrange("p t (h n) -> p t h n", n=HD)
            rq = r_of(rstd, "qk").rearrange("p (t h) -> p t h", t=TOK).unsqueeze(3).to_broadcast([P, TOK, 10, HD])
            step(dve.tensor_tensor(qk, qk, rq, ALU.mult))
            for i, (lo, hi) in enumerate(((0, 8), (8, 10))):
                g = gqk[:, i, :].unsqueeze(1).unsqueeze(1).to_broadcast([P, TOK, hi - lo, HD])
                ins = dve.tensor_tensor(qk[:, :, lo:hi, :], qk[:, :, lo:hi, :], g, ALU.mult)
            step(ins)
            half = HD // 2
            x1, x2 = qk[:, :, :, 0:half], qk[:, :, :, half:HD]
            cos, sin = (trig[:, :, i, 32:96].unsqueeze(2).to_broadcast([P, TOK, 10, half]) for i in range(2))
            r1, r2, r3 = (gb_flat[:, 1280 * i:1280 * (i + 1)].rearrange("p (t h n) -> p t h n", t=TOK, n=half) for i in range(3))
            dve.tensor_tensor(r1, x1, sin, ALU.mult)
            dve.tensor_tensor(r2, x2, sin, ALU.mult)
            step(dve.tensor_tensor(r3, x1, cos, ALU.mult))
            step(dve.tensor_tensor(x1, r3, r2, ALU.subtract))
            step(dve.tensor_tensor(r3, x2, cos, ALU.mult))
            dve.tensor_tensor(x2, r3, r1, ALU.add).then_inc(rope_ready, 1)
            dve.wait_ge(tile_used, T_OUT2)
            step(dve.memset(at_sb[:], 0.0))

            for h in range(HEADS + 1):
                if h < HEADS:
                    b, e = 4 * (h % 2), h % 2
                    scale = float(HD) ** -0.5
                    dve.wait_ge(at_S, HEADS + h + 1)
                    if h >= 2:
                        dve.wait_ge(at_PT, HEADS + h - 1)
                    step(dve.tensor_tensor(att2_s[:, e].rearrange("p t s -> p (t s)"), ps[:, b + 2, :], mask2[:], ALU.add))
                    step(dve.tensor_reduce(amax[:, e, :, 0:1], att2_s[:, e], X, ALU.max))
                    step(dve.tensor_scalar(amax[:, e, :, 1:2], amax[:, e, :, 0:1], scale, sinkb[:, h:h + 1], ALU.mult, ALU.max))
                    dve.tensor_scalar(amax[:, e, :, 2:3], amax[:, e, :, 1:2], -1.0, None, ALU.mult).then_inc(at_max, 1)
                if h >= 1:
                    e = (h - 1) % 2
                    dve.wait_ge(at_exp, HEADS + h)
                    step(dve.tensor_tensor(asum[:, e, 1, :], asum[:, e, 0, :], amax[:, e, :, 3], ALU.add))
                    step(dve.reciprocal(asum[:, e, 1, :], asum[:, e, 1, :]))
                    attn_out(h - 1, HEADS, lambda t: z2[:, t, (h - 1) * HD:h * HD])

            for h in range(GH):
                e = h % 2
                dve.wait_ge(g_AT, h + 1)
                if h >= 2:
                    dve.wait_ge(g_O, h - 1)
                for d in range(2):
                    ins = dve.copy_predicated(at_sb[:, e], gmask[:, d, :].unsqueeze(1).to_broadcast([P, TOK, P]),
                                              ps[:, 0, 2 * d * P:2 * (d + 1) * P].rearrange("p (t s) -> p t s", t=TOK))
                    if d == 0:
                        step(ins)
                ins.then_inc(g_at, 1)
                dve.wait_ge(g_SS, h + 1)
                for n in range(3):
                    for d in range(2):
                        c = n if d == 0 else 3 - n
                        new = gla_sum(d, c)
                        if n == 0:
                            ins = dve.tensor_copy(state[:, e, d, 0, :], new)
                        else:
                            ins = dve.scalar_tensor_tensor(out=state[:, e, d, n, :], in0=state[:, e, d, n - 1, :],
                                                           scalar=decay[:, d, h * NCH + c:h * NCH + c + 1], in1=new,
                                                           op0=ALU.mult, op1=ALU.add)
                        if d == 1 and n < 2:
                            step(ins)
                ins.then_inc(g_st, 1)
                dve.wait_ge(g_O, h + 1)
                dve.tensor_copy(z2[:, :, QG + h * DV:QG + (h + 1) * DV], ps[:, 5, :].rearrange("p (t n) -> p t n", t=TOK))\
                   .then_inc(g_o, 1)
            dve.wait_ge(sq_done, 7)
            mean_sq("gla", DV)
            dve.wait_ge(rstd_ready, r_count("gla"))
            og = z2[:, :, QG:QG + 2 * NB].rearrange("p t (h n) -> p t h n", h=GH)
            rg = r_of(rstd, "gla").rearrange("p (t h) -> p t h", t=TOK).unsqueeze(3).to_broadcast([P, TOK, GH, DV])
            step(dve.tensor_tensor(og, og, rg, ALU.mult))
            step(dve.tensor_tensor(og, og, gla_g[:].unsqueeze(1).unsqueeze(1).to_broadcast([P, TOK, GH, DV]), ALU.mult))
            dve.wait_ge(gate2_ready, 1)
            dve.tensor_tensor(z2[:, :, QG:QG + 2 * NB], z2[:, :, QG:QG + 2 * NB], z2[:, :, GG:GG + 2 * NB],
                              ALU.mult).then_inc(mix2_ready, 1)
            for n in range(8):
                F = F_MIX2 + n
                dve.wait_ge(tp_hi, F + 1)
                dve.tensor_tensor(hT_lo[:, 2 * n:2 * n + 2, :], ps[:, 4 + F % 4, :].rearrange("p (c s) -> p c s", c=2),
                                  hT_hi[:, 2 * n:2 * n + 2, :].bitcast(F32), ALU.subtract).then_inc(tp_free, 1)

            def row_add(c_end, step_, n, sem_done):
                dve.wait_ge(tile_used, c_end + step_)
                for t in range(TOK):
                    ins = dve.tensor_tensor(x_sb[:, t, cols(n)], ps_flat[:, bass.ts(2 * n + t, NB)], x_sb[:, t, cols(n)],
                                            ALU.add)
                ins.then_inc(sem_done, 1)

            lo_upto(T_OUT2 + 8)
            with dve.Fori(1, 4) as n:
                lo_tiles(T_OUT2, 8 * n, 0, 3)
                row_add(T_OUT2, 8 * n, n - 1, x_new)
                lo_tiles(T_OUT2, 8 * n, 3, 8)
            done[0] = T_FF2
            row_add(T_FF2, 0, 3, x_new)

            with_fills(T_FF2, F_XT4, "norm2_g_2")
            dve.wait_ge(sq_done, 8)
            mean_sq("x3", DM)
            lo_upto(T_FF2 + 16)

            def taps2(j, half):
                dst = cg if half == 0 else cval
                n = 0
                for f in range(2):
                    dve.wait_ge(ct_center, 4 * j + 2 * half + f + 1)
                    for c in range(2 * f, 2 * f + 2):
                        k = 4 * j + c + FC * half
                        src = ps[:, 4 + 2 * half + f, (c % 2) * SEQ:(c % 2 + 1) * SEQ]
                        ins = dve.scalar_tensor_tensor(out=dst[:, c, 1:SEQ], in0=src[:, 0:SEQ - 1],
                                                       scalar=conv2[:, 0, bass.ts(k, 1)], in1=dst[:, c, 1:SEQ],
                                                       op0=ALU.mult, op1=ALU.add)
                        ins.then_inc(conv2_step, 1)
                    for c in range(2 * f, 2 * f + 2):
                        k = 4 * j + c + FC * half
                        src = ps[:, 4 + 2 * half + f, (c % 2) * SEQ:(c % 2 + 1) * SEQ]
                        dve.wait_ge(conv2_step, 8 * j + 4 * half + c + 1)
                        ins = dve.scalar_tensor_tensor(out=dst[:, c, 0:SEQ - 1], in0=src[:, 1:SEQ],
                                                       scalar=conv2[:, 2, bass.ts(k, 1)], in1=dst[:, c, 0:SEQ - 1],
                                                       op0=ALU.mult, op1=ALU.add)
                ins.then_inc(ct_free, 1)

            def product2(j):
                dve.wait_ge(cg_silu, j + 1)
                dve.wait_ge(ct_free, 2 * j + 2)
                dve.tensor_tensor(cg[:], cg[:], cval[:], ALU.mult).then_inc(prod_ready, 1)

            def hidden_lo(j):
                dve.wait_ge(aT_hi_ready, j + 1)
                dve.tensor_tensor(aT_lo_flat[:, bass.ts(j, 4 * SEQ)], cg[:].rearrange("p c s -> p (c s)"),
                                  aT_hi_flat[:, bass.ts(j, 4 * SEQ)].bitcast(F32), ALU.subtract).then_inc(aT_ready, 1)

            taps2(0, 0)
            with dve.Fori(1, FB) as j:
                lo_tiles(T_FF2, 16 * j, 0, 8)
                taps2(j - 1, 1)
                product2(j - 1)
                lo_tiles(T_FF2, 16 * j, 8, 12)
                hidden_lo(j - 1)
                lo_tiles(T_FF2, 16 * j, 12, 16)
                taps2(j, 0)
            done[0] = T_DN2
            lo_upto(T_DN2 + 8)
            taps2(FB - 1, 1)
            product2(FB - 1)
            lo_upto(T_DN2 + 12)
            hidden_lo(FB - 1)
            lo_upto(T_DN2 + 24)
            with dve.Fori(1, 4) as n:
                lo_tiles(T_DN2, 24 * n, 0, 3)
                row_add(T_DN2, 24 * n, n - 1, row_y)
                lo_tiles(T_DN2, 24 * n, 3, 24)
            row_add(T_END, 0, 3, row_y)


_INS = ["x", "positions", "pre_mix_norm", "w_in", "q_norm", "w_uq", "kv_norm", "w_ukv", "conv_w", "conv_b",
        "conv_ln_g", "conv_ln_b", "conv_out_norm", "attn_out_norm", "w_out", "post_mix_norm", "pre_ffn_norm",
        "w_gate", "w_up", "w_down", "post_ffn_norm", "norm1_g_2", "w_in_2", "attn_q_norm_g_2",
        "attn_k_norm_g_2", "attn_sink_2", "gla_wa2_fwd_2", "gla_ba_fwd_2", "gla_wa2_bwd_2", "gla_ba_bwd_2",
        "gla_out_norm_g_2", "w_out_2", "norm2_g_2", "w_up_2", "conv_w_2", "conv_b_2", "w_down_2"]


def inverse_frequencies():
    f = np.float32
    one = f(THETA) ** (-np.arange(0, ROPE, 2, dtype=f) / f(ROPE))
    two = f(1.0) / (f(THETA) ** (np.arange(HD // 2, dtype=f) / f(HD // 2)))
    return np.concatenate([one, two]).astype(f)[None, :]


def kernel(**inputs):
    import concourse.bacc as _bacc
    from concourse.bass_utils import run_bass_kernel_spmd as _run

    nc = _bacc.Bacc("TRN2", target_bir_lowering=False, num_devices=1)
    arrays = {f"in_{name}": np.ascontiguousarray(inputs[name]) for name in _INS}
    arrays["in_inv_freq"] = inverse_frequencies()
    aps = {name[3:]: nc.dram_tensor(name, v.shape, mybir.dt.from_np(v.dtype), kind="ExternalInput").ap()
           for name, v in arrays.items()}
    out = nc.dram_tensor("out_0", (1, SEQ, DM), F32, kind="ExternalOutput").ap()
    build(nc, aps, out)
    r = _run(nc, [arrays], core_ids=[0])
    return r.results[0]["out_0"]
```

```python
from contextlib import ExitStack

import numpy as np

import concourse.bass as bass
from concourse import mybir

F32 = mybir.dt.float32
F32R = mybir.dt.float32r
I32 = mybir.dt.int32
ALU = mybir.AluOpType
ACT = mybir.ActivationFunctionType
X = mybir.AxisListType.X

P = 128
SEQ = 256
TOK = SEQ // P
DM = 2048
KD = DM // P
NB = 512
EPS = 1e-6
RING = 4
MASKED = -3.0e38

CONV = 1024
CC = CONV // P
TAPS = 31
HEADS = 8
NOPE, ROPE, VD = 128, 64, 128
QKH = NOPE + ROPE
QL, KVL = 768, 512
QC, KVC = QL // P, KVL // P
Z1 = QL + KVL + ROPE
DFF = 5632
FC = DFF // P
FB = DFF // NB
THETA = 10000.0

HD = 128
KVH = 2
GH, DK, DV, RANK, CHUNK = 4, 128, 256, 16, 64
NCH = SEQ // CHUNK
Z2 = 4640
W2 = Z2 // 10
QA, KA, VA, QG, KG, VG, GG, LR = 0, 1024, 1280, 1536, 2048, 2560, 3584, 4608
B2_ORDER = [9, 3, 4, 5, 6, 7, 2, 1, 8, 0]
GLA0, GLA_STEP = 51, 5
MIX_FILL = 78
HEAD_ORDER = [4, 5, 6, 7, 0, 1, 2, 3]
PAIR_ORDER = [2, 3, 0, 1]
OUT2_TILES = ([(0, i) for i in range(3)] + [(1, i) for i in range(3)] + [(0, 3), (1, 3)]
              + [(2, i) for i in range(4)] + [(3, i) for i in range(4)])

SHAPES = []


def _phase(blocks, tiles, width):
    start = len(SHAPES)
    SHAPES.extend([(kc, width(b)) for b in range(blocks) for kc in tiles])
    return start


IN1_COLS = [(0, 512), (1024, 512), (512, 512), (1536, 512), (2048, 448), (2496, 448), (2944, 448)]
T_IN1 = _phase(7, [2] * 8, lambda b: IN1_COLS[b][1])
T_UQ = _phase(3, [2] * 3, lambda b: NB)
T_UKV = _phase(4, [2] * 2, lambda b: NB)
T_OUT1 = _phase(8, [2] * 4, lambda b: NB)
T_FF1 = _phase(2 * FB, [2] * 8, lambda b: NB)
DN_TILES = [2] * 20 + [1] * 4
T_DN1 = _phase(4, DN_TILES, lambda b: NB)
T_IN2 = _phase(10, [2] * 8, lambda b: W2)
T_OUT2 = _phase(8, [2] * 4, lambda b: NB)
T_FF2 = _phase(2 * FB, [2] * 8, lambda b: NB)
T_DN2 = _phase(4, DN_TILES, lambda b: NB)
T_END = len(SHAPES)

G_FF1 = 9
G_IN2 = G_FF1 + FB
G_FF2 = G_IN2 + 5

F_XT1, F_LAT, F_MIX1, F_XT2, F_FF1 = 0, 8, 13, 17, 25
F_XT3 = F_FF1 + 2 * FB
F_MIX2, F_XT4 = F_XT3 + 8, F_XT3 + 16

GAINS = [("pre_mix_norm", KD), ("q_norm", QC), ("kv_norm", KVC), ("conv_b", CC), ("conv_ln_g", CC),
         ("conv_ln_b", CC), ("conv_out_norm", CC), ("attn_out_norm", CC), ("pre_ffn_norm", KD),
         ("norm1_g_2", KD), ("norm2_g_2", KD)]
G_AT, _n = {}, 0
for _name, _k in GAINS:
    G_AT[_name] = _n
    _n += _k
G_ROWS = _n


def build(nc, a, out):
    ctx = ExitStack()
    with ctx:
        def sb(name, shape, dt=F32):
            return ctx.enter_context(nc.sbuf_tensor(name, shape, dt))

        def overlay(tensors, stay=False):
            inner = ExitStack()
            got = [inner.enter_context(nc.sbuf_tensor(n, s, d)) for n, s, d in tensors]
            if stay:
                ctx.push(inner)
            else:
                inner.close()
            return got

        def sem(name):
            return ctx.enter_context(nc.semaphore(name))

        x_sb = sb("x_sb", [P, TOK, DM])
        raw = sb("raw", [P, RING, 2, NB])
        w_hi = sb("w_hi", [P, RING, 2, NB], F32R)
        w_lo = sb("w_lo", [P, RING, 2, NB], F32R)
        ident = sb("ident", [P, P])
        ones = sb("ones", [P, P])
        gains = sb("gains", [P, G_ROWS])
        convw = sb("convw", [P, TAPS * CC])
        conv2 = sb("conv2", [P, 4, 2 * FC])
        masks = sb("masks", [P, 5 * P])
        mask1 = masks[:, 0:3 * P]
        mask2 = masks[:, P:5 * P]
        tri = sb("tri", [P, 2, P])
        gmask = sb("gmask", [P, 2, P], I32)
        posf = sb("posf", [P, 2, TOK])
        trig = sb("trig", [P, TOK, 2, 96])
        invf = sb("invf", [P, 96])
        ss = sb("ss", [P, 64])
        ms = sb("ms", [P, 64])
        rstd = sb("rstd", [P, 64])
        minus_half = sb("minus_half", [P, 20])
        amax = sb("amax", [P, 2, 2, 4])
        asum = sb("asum", [P, 2, 2, 2])
        sinkb = sb("sinkb", [P, HEADS])
        decay = sb("decay", [P, 2, GH * NCH])
        y_dn, _, grow_dn = overlay([("y_dn", [P, TOK * DM], F32), ("under_grow", [P, DM], F32), ("grow_dn", [P, DM], F32)])
        hT_hi = sb("hT_hi", [P, KD, SEQ], F32R)
        hT_lo = sb("hT_lo", [P, KD, SEQ], F32R)
        z1, uT, cv, q1, kv1, attn1, qkT, qpeT, att1_s, att1_p, kpe, kpeT = overlay([
            ("z1", [P, TOK, Z1], F32), ("uT", [P, CC, SEQ + TAPS - 1], F32), ("cv", [P, CC, SEQ], F32),
            ("q1", [P, TOK, HEADS * QKH], F32), ("kv1", [P, TOK, DM], F32), ("attn1", [P, TOK, CONV], F32),
            ("qkT", [P, 2, 2, SEQ], F32), ("qpeT", [ROPE, 2, SEQ], F32), ("att1_s", [P, 2, 3 * P], F32),
            ("att1_p", [P, 2, 3 * P], F32), ("kpe", [P, TOK, ROPE], F32), ("kpeT", [ROPE, SEQ], F32)])
        taken = sum([TOK * Z1, CC * (SEQ + TAPS - 1), CC * SEQ, TOK * HEADS * QKH, TOK * DM, TOK * CONV,
                     4 * SEQ, 2 * SEQ, 6 * P, 6 * P, TOK * ROPE, SEQ])
        _, latT_hi, latT_lo = overlay([("under_lat", [P, taken], F32),
                                       ("latT_hi", [P, QC + KVC, SEQ], F32R), ("latT_lo", [P, QC + KVC, SEQ], F32R)])
        _, lnsq = overlay([("under_ln", [P, taken], F32), ("lnsq", [P, CC, SEQ], F32)])
        taken += 2 * (QC + KVC) * SEQ
        _, tap_prod = overlay([("under_tap", [P, taken], F32), ("tap_prod", [P, 2, SEQ], F32)])
        taken = TOK * Z1 + CC * (SEQ + TAPS - 1) + CC * SEQ
        _, grow_out = overlay([("under_gout", [P, taken], F32), ("grow_out", [P, DM], F32)])
        taken += TOK * HEADS * QKH
        _, y_out = overlay([("under_y", [P, taken], F32), ("y_out", [P, TOK * DM], F32)])
        z2, gb, qT2, kT2, fac, kaT, gqk, gla_g, at_sb = overlay([
            ("z2", [P, TOK, Z2], F32), ("gb", [P, 2, 2, 2 * NB], F32), ("qT2", [P, GH, SEQ], F32),
            ("kT2", [P, GH, SEQ], F32), ("fac", [P, 2, 4, GH, SEQ], F32), ("kaT", [P, KVH, SEQ], F32),
            ("gqk", [P, 2, HD], F32), ("gla_g", [P, DV], F32), ("at_sb", [P, TOK, P], F32)])
        taken = TOK * Z2 + 8 * NB
        _, state, ktok = overlay([("under_st", [P, taken], F32), ("state", [P, 2, 3, DV], F32), ("ktok", [P, 2, TOK, P], F32)])
        taken += 2 * GH * SEQ
        _, att2_q, att2_s, att2_p = overlay([
            ("under_at", [P, taken], F32), ("att2_q", [P, 2, 2, SEQ], F32), ("att2_s", [P, 2, TOK, SEQ], F32),
            ("att2_p", [P, 2, 4, P], F32)])
        taken = TOK * Z2 + 8 * NB + 2 * GH * SEQ + 6 * GH * SEQ
        _, lrT, wa2 = overlay([("under_lr", [P, taken], F32), ("lrT", [RANK + 1, 2, SEQ], F32),
                               ("wa2", [RANK + 1, 2, NB], F32)])
        rows, = overlay([("rows", [P, 8, P], F32)])
        trig_t, = overlay([("under_trig", [P, 8 * P], F32), ("trig_t", [P, 4, TOK * 96], F32)])[1:]
        aT_hi = sb("aT_hi", [P, FC, SEQ], F32R)
        aT_lo = sb("aT_lo", [P, FC, SEQ], F32R)
        stage = sb("stage", [P, 3, 4, SEQ])
        ps = ctx.enter_context(nc.psum_tensor("ps", [P, 8, NB], F32))

        gate_s = stage[:, 0].rearrange("p c s -> p (c s)").rearrange("p (t n) -> p t n", t=TOK)
        prod_s = stage[:, 1].rearrange("p c s -> p (c s)").rearrange("p (t n) -> p t n", t=TOK)
        raw_s = gate_s
        cg, cval = stage[:, 1], stage[:, 2]
        a_s = attn1[:, :, 0:NB]
        sg_s = attn1[:, :, NB:2 * NB]

        raw_landed = [sem(f"raw_landed{s}") for s in range(RING)]
        hi_ready, lo_ready, tile_used = sem("hi_ready"), sem("lo_ready"), sem("tile_used")
        gemm_free = [sem("gemm_free0"), sem("gemm_free1")]
        tp_ready, tp_hi, tp_free = sem("tp_ready"), sem("tp_hi"), sem("tp_free")
        x_landed, params_landed, late_landed, grow_landed, out_landed = (
            sem("x_landed"), sem("params_landed"), sem("late_landed"), sem("grow_landed"), sem("out_landed"))
        rows_landed = sem("rows_landed")
        ident_ready, consts_ready, masks_ready = sem("ident_ready"), sem("consts_ready"), sem("masks_ready")
        rows_T, gains_ready = sem("rows_T"), sem("gains_ready")
        dve_step, act_step, pool_step = sem("dve_step"), sem("act_step"), sem("pool_step")
        ms_ready, rstd_ready, sq_done = sem("ms_ready"), sem("rstd_ready"), sem("sq_done")
        u_ready, cu_ready, cu_free = sem("u_ready"), sem("cu_ready"), sem("cu_free")
        conv_tap, pool_mul, pool_add = sem("conv_tap"), sem("pool_mul"), sem("pool_add")
        trig_arg, trig_abs, trig_done = sem("trig_arg"), sem("trig_abs"), sem("trig_done")
        at_T, at_qk, at_S, at_max, at_exp, at_PT, at_pT, at_PV, at_out = (
            sem("at_T"), sem("at_qk"), sem("at_S"), sem("at_max"), sem("at_exp"), sem("at_PT"), sem("at_pT"),
            sem("at_PV"), sem("at_out"))
        rope_ready, kpe_ready = sem("rope_ready"), sem("kpe_ready")
        ln_mm, ln_dve, ln_act = sem("ln_mm"), sem("ln_dve"), sem("ln_act")
        mix_conv, conv_hi, y_ready = sem("mix_conv"), sem("conv_hi"), sem("y_ready")
        row_sq, row_y, x_new = sem("row_sq"), sem("row_y"), sem("x_new")
        ct_ready, ct_center, ct_free, cg_silu, prod_ready, aT_hi_ready, aT_ready, conv2_step = (
            sem("ct_ready"), sem("ct_center"), sem("ct_free"), sem("cg_silu"), sem("prod_ready"),
            sem("aT_hi_ready"), sem("aT_ready"), sem("conv2_step"))
        gl_mm, gl_act, gl_dve = sem("gl_mm"), sem("gl_act"), sem("gl_dve")
        fac_exp, fac_ready = sem("fac_exp"), sem("fac_ready")
        g_AT, g_at, g_KT, g_kt, g_SS, g_st, g_O, g_o = (
            sem("g_AT"), sem("g_at"), sem("g_KT"), sem("g_kt"), sem("g_SS"), sem("g_st"), sem("g_O"), sem("g_o"))
        mix2_ready, gate2_ready = sem("mix2_ready"), sem("gate2_ready")
        qk_normed, at_sum, half_added = sem("qk_normed"), sem("at_sum"), sem("half_added")

        def chunks(w):
            return w[0].rearrange("(c p) n -> p c n", p=P)

        w_in, w_uq, w_ukv, w_out = chunks(a["w_in"]), chunks(a["w_uq"]), chunks(a["w_ukv"]), chunks(a["w_out"])
        w_gate, w_up, w_down = chunks(a["w_gate"]), chunks(a["w_up"]), chunks(a["w_down"])
        w_in2, w_out2, w_up2, w_down2 = (chunks(a["w_in_2"]), chunks(a["w_out_2"]), chunks(a["w_up_2"]),
                                         chunks(a["w_down_2"]))

        def landed(c0, step):
            return 16 * (c0 // RING + 1) + (16 // RING) * step

        def cols(n, w=NB):
            return bass.ts(n, w)

        def in_sbuf(eng, B, base=0):
            eng.wait_ge(gemm_free[B % 2], base + B // 2 + 1)

        def last_of(b, d):
            return b.rearrange("p h (c s) -> p (h c) s", s=CHUNK)[:, :, CHUNK - 1 if d == 0 else 0]

        def gla_sum(d, c):
            bank = 6 + c % 2
            i = {(0, 0): 0, (0, 2): 1, (0, 1): 0, (1, 3): 0, (1, 1): 1, (1, 2): 0}[d, c]
            return ps[:, bank, i * DV:(i + 1) * DV]

        def gla_slot(g):
            return divmod(g - GLA0, GLA_STEP)

        QK_PARTS = [("k", 8, 2, 6, 1), ("qa", 4, 4, 7, 0), ("qb", 0, 4, 9, 0)]

        gb_flat = gb[:].rearrange("p a d n -> p (a d n)")
        ps_flat = ps[:].rearrange("p b n -> p (b n)")
        ss4 = ss[:, 56:64]

        block = ctx.enter_context(nc.Block())

        @block.sync
        def _(sp):
            for t in range(TOK):
                sp.dma_start(x_sb[:, t, :], a["x"][0, t * P:(t + 1) * P, :]).then_inc(x_landed, 16)

            def load(c0, step, w, k0, at):
                kc, width = SHAPES[c0]
                s = c0 % RING
                if c0 >= RING:
                    sp.wait_ge(lo_ready, c0 - RING + 1 + step)
                sp.dma_start(raw[:, s, :kc, :width], w[:, k0:k0 + kc, at]).then_inc(raw_landed[s], 16)

            def load_block(c0, step, w, tiles, at):
                k0 = 0
                for n, kc in enumerate(tiles):
                    load(c0 + n, step, w, k0, at)
                    k0 += kc

            def rows_phase(c0, w, tiles):
                T = len(tiles)
                load_block(c0, 0, w, tiles, cols(0))
                with sp.Fori(1, 4) as n:
                    load_block(c0, n * T, w, tiles, cols(n))

            for b, (n0, width) in enumerate(IN1_COLS):
                load_block(T_IN1 + 8 * b, 0, w_in, [2] * 8, slice(n0, n0 + width))
            for b in range(3):
                load_block(T_UQ + 3 * b, 0, w_uq, [2] * 3, cols(b))
            for b in range(4):
                load_block(T_UKV + 2 * b, 0, w_ukv, [2] * 2, cols(b))
            for half in range(2):
                for n in range(4):
                    for i in range(4):
                        load(T_OUT1 + 16 * half + 4 * n + i, 0, w_out, CC * (1 - half) + 2 * i, cols(n))

            def ff1(j):
                load_block(T_FF1, 16 * j, w_gate, [2] * 8, cols(j))
                load_block(T_FF1 + 8, 16 * j, w_up, [2] * 8, cols(j))
            with sp.Fori(0, FB) as j:
                ff1(j)
            rows_phase(T_DN1, w_down, DN_TILES)
            for b, n in enumerate(B2_ORDER):
                load_block(T_IN2 + 8 * b, 0, w_in2, [2] * 8, slice(n * W2, (n + 1) * W2))
            for g in range(16):
                load(T_OUT2 + g, 0, w_out2, CC + 2 * (g % 4), cols(g // 4))
            for g, (b, i) in enumerate(OUT2_TILES):
                load(T_OUT2 + 16 + g, 0, w_out2, 2 * PAIR_ORDER[i], cols(b))
            with sp.Fori(0, FB) as j:
                load_block(T_FF2, 16 * j, w_up2, [2] * 8, cols(j))
                load_block(T_FF2 + 8, 16 * j, w_up2, [2] * 8, cols(j + FB))
            rows_phase(T_DN2, w_down2, DN_TILES)
            for n in range(4):
                sp.wait_ge(row_y, 9 + n)
                sp.dma_start(out[0, :, cols(n)].rearrange("(t p) n -> p t n", p=P), x_sb[:, :, cols(n)])\
                  .then_inc(out_landed, 16)
            sp.wait_ge(out_landed, 16 * 4)

        R = {}
        at = 0
        for name, n in [("x0", 2), ("lat", 4), ("ln", 2), ("conv", 2), ("attn", 2), ("out1", 2), ("x1", 2),
                        ("dn1", 2), ("x2", 2), ("k", 4), ("qa", 8), ("gla", 8), ("qb", 8), ("x3", 2)]:
            R[name] = (at, n)
            at += n
        R_ORDER = ["x0", "lat", "attn", "ln", "conv", "out1", "x1", "dn1", "x2", "k", "qa", "gla", "qb", "x3"]

        def r_count(name):
            return R_ORDER.index(name) + 1

        def r_of(tensor, name, lo=0, n=None):
            at, k = R[name]
            return tensor[:, at + lo:at + lo + (k - lo if n is None else n)]

        @block.gpsimd
        def _(pool):
            count = [0]

            def step(ins):
                count[0] += 1
                ins.then_inc(pool_step, 1)
                pool.wait_ge(pool_step, count[0])

            step(pool.memset(ident[:], 0.0))
            pool.affine_select(out=ident[:], in_=ident[:], compare_op=ALU.not_equal, fill=1.0, base=0,
                               pattern=[[-1, P]], channel_multiplier=1).then_inc(ident_ready, 1)
            step(pool.memset(masks[:], 0.0))
            step(pool.memset(tri[:], 1.0))
            for at, sign in ((0, 1), (2 * P, 1), (3 * P, -1)):
                step(pool.affine_select(out=masks[:, at:at + P], in_=masks[:, at:at + P], compare_op=ALU.is_ge,
                                        fill=MASKED, base=0, pattern=[[-sign, P]], channel_multiplier=sign))
            for d, (m, c) in enumerate([(-1, 1), (1, -1)]):
                step(pool.affine_select(out=tri[:, d, :], in_=tri[:, d, :], compare_op=ALU.is_ge, fill=0.0,
                                        base=0, pattern=[[c, P]], channel_multiplier=m))
                step(pool.affine_select(out=tri[:, d, 0:CHUNK], in_=tri[:, d, 0:CHUNK], compare_op=ALU.is_ge,
                                        fill=0.0, base=CHUNK - 1, pattern=[[0, CHUNK]], channel_multiplier=-1))
                step(pool.affine_select(out=tri[:, d, CHUNK:P], in_=tri[:, d, CHUNK:P], compare_op=ALU.is_ge,
                                        fill=0.0, base=-CHUNK, pattern=[[0, CHUNK]], channel_multiplier=1))
            step(pool.tensor_copy(gmask[:], tri[:]))
            step(pool.affine_select(out=gmask[:, 1, :], in_=gmask[:, 1, :], compare_op=ALU.is_gt, fill=0.0,
                                    base=0, pattern=[[-1, P]], channel_multiplier=1))
            pool.iota(posf[:, 1, :], pattern=[[P, TOK]], base=0, channel_multiplier=1,
                      allow_small_or_imprecise_dtypes=True).then_inc(masks_ready, 1)

            def conv_pair(g):
                c, base = 4 * g + 2, (TAPS - 1) * g
                acc = cv[:, c:c + 2, :]

                def tap(out, j):
                    w = convw[:, bass.ds(j * CC + c, 2)].unsqueeze(2).to_broadcast([P, 2, SEQ])
                    return pool.tensor_tensor(out, uT[:, c:c + 2, bass.ds(j, SEQ)], w, ALU.mult)

                pool.wait_ge(gains_ready, 3)
                pool.wait_ge(cu_free, 2 * g + 2)
                step(tap(acc, 0))
                at = G_AT["conv_b"] + c
                bias = gains[:, at:at + 2].unsqueeze(2).to_broadcast([P, 2, SEQ])
                step(pool.tensor_tensor(acc, acc, bias, ALU.add))
                with pool.Fori(1, TAPS) as j:
                    tap(tap_prod[:], j).then_inc(pool_mul, 1)
                    pool.wait_ge(pool_mul, base + j)
                    pool.tensor_tensor(acc, acc, tap_prod[:], ALU.add).then_inc(pool_add, 1)
                    pool.wait_ge(pool_add, base + j)


            def rotate(part):
                _, h0, n, _, _ = QK_PARTS[part]
                half = HD // 2
                qk = z2[:, :, h0 * HD:(h0 + n) * HD].rearrange("p t (h n) -> p t h n", n=HD)
                x1, x2 = qk[:, :, :, 0:half], qk[:, :, :, half:HD]
                cos, sin = (trig[:, :, i, 32:96].unsqueeze(2).to_broadcast([P, TOK, n, half]) for i in range(2))
                r1, r2, r3, r4 = (gb_flat[:, 1536 + 512 * i:1536 + 512 * i + TOK * n * half]
                                  .rearrange("p (t h n) -> p t h n", t=TOK, n=half) for i in range(4))
                pool.wait_ge(trig_done, 1)
                pool.wait_ge(qk_normed, part + 1)
                pool.tensor_tensor(r1, x1, sin, ALU.mult)
                pool.tensor_tensor(r2, x2, sin, ALU.mult)
                pool.tensor_tensor(r3, x1, cos, ALU.mult)
                step(pool.tensor_tensor(r4, x2, cos, ALU.mult))
                pool.tensor_tensor(x1, r3, r2, ALU.subtract)
                pool.tensor_tensor(x2, r4, r1, ALU.add).then_inc(rope_ready, 1)
                pool.wait_ge(rope_ready, part + 2)

            pool.wait_ge(consts_ready, 2)
            for n, name in enumerate(R_ORDER):
                pool.wait_ge(ms_ready, n + 1)
                k = R[name][1]
                pool.tensor_tensor(r_of(rstd, name), r_of(ms, name), minus_half[:, 0:k],
                                   ALU.pow).then_inc(rstd_ready, 1)
                if name in ("x0", "lat"):
                    conv_pair(0 if name == "x0" else 1)
                if name in ("k", "qa", "qb"):
                    rotate([q[0] for q in QK_PARTS].index(name))

        @block.tensor
        def _(pe):
            def gemm_tile(c0, step, A, k0, banks, start, stop):
                kc, width = SHAPES[c0]
                s = c0 % RING
                pe.wait_ge(lo_ready, c0 + 1 + step)
                for k in range(kc):
                    for t in range(TOK):
                        o = banks(t, width)
                        first, last = start and k == 0, stop and k == kc - 1
                        xh, xl = A[0][:, k0 + k, t * P:(t + 1) * P], A[1][:, k0 + k, t * P:(t + 1) * P]
                        wh, wl = w_hi[:, s, k, :width], w_lo[:, s, k, :width]
                        pe.matmul(o, xh, wh, start=first, stop=False)
                        pe.matmul(o, xh, wl, start=False, stop=False)
                        mm = pe.matmul(o, xl, wh, start=False, stop=last)
                mm.then_inc(tile_used, 1)

            def pair(p):
                return lambda t, width: ps[:, 2 * p + t, :width]

            H = (hT_hi, hT_lo)

            def fill(F, src, n, wait=None):
                if F >= 4:
                    pe.wait_ge(tp_free, F - 3)
                for k in range(2):
                    for t in range(TOK):
                        mm = pe.transpose(ps[:, 4 + F % 4, k * SEQ + t * P:k * SEQ + (t + 1) * P],
                                          src[:, t, (2 * n + k) * P:(2 * n + k + 1) * P], ident[:])
                mm.then_inc(tp_ready, 1)

            def with_fills(c0, F, src, ready, banks):
                for n in range(4):
                    ready(n)
                    fill(F + n, src, n)
                for n in range(8):
                    pe.wait_ge(tp_free, F + n + 1)
                    gemm_tile(c0 + n, 0, H, 2 * n, banks, n == 0, n == 7)
                    if n < 4:
                        ready(n + 4)
                        fill(F + n + 4, src, n + 4)

            pe.wait_ge(ident_ready, 1)
            pe.wait_ge(consts_ready, 1)
            pe.wait_ge(rows_landed, 16 * len(GAINS))
            mm = pe.transpose(ps[:, 0, 0:G_ROWS], rows[0:G_ROWS, 0, :], ident[0:G_ROWS, 0:G_ROWS])
            mm.then_inc(rows_T, 1)
            pe.wait_ge(x_landed, 16 * TOK)

            def x0_ready(n):
                pass

            for n in range(4):
                fill(F_XT1 + n, x_sb, n)
            pe.wait_ge(params_landed, 16 * 9)
            pe.transpose(ps[:, 2, 0:P], rows[:, 1, :], ident[:])
            pe.transpose(ps[:, 2, P:TAPS * CC], rows[0:TAPS * CC - P, 2, :],
                         ident[0:TAPS * CC - P, 0:TAPS * CC - P]).then_inc(rows_T, 1)
            for n in range(4):
                mm = pe.transpose(ps[:, 3, n * 2 * FC:(n + 1) * 2 * FC], rows[0:2 * FC, 3 + n, :],
                                  ident[0:2 * FC, 0:2 * FC])
            mm.then_inc(rows_T, 1)
            pe.wait_ge(gains_ready, 3)
            for n in range(8):
                pe.wait_ge(tp_free, F_XT1 + n + 1)
                gemm_tile(T_IN1 + n, 0, H, 2 * n, pair(0), n == 0, n == 7)
                if n < 4:
                    fill(F_XT1 + n + 4, x_sb, n + 4)

            def cu_fills(g):
                pe.wait_ge(u_ready, g + 1)
                if g == 0:
                    pe.wait_ge(tp_free, 8)
                for f in range(2):
                    if g > 0:
                        pe.wait_ge(cu_free, 2 * (g - 1) + f + 1)
                    for k in range(2):
                        for t in range(TOK):
                            c = 2 * f + k
                            mm = pe.transpose(ps[:, 6 + f, k * SEQ + t * P:k * SEQ + (t + 1) * P],
                                              a_s[:, t, c * P:(c + 1) * P], ident[:])
                    mm.then_inc(cu_ready, 1)

            def in1_tiles(lo, hi):
                for g in range(lo, hi):
                    b, n = divmod(g, 8)
                    if n == 0 and b >= 2:
                        pe.wait_ge(gemm_free[b % 2], b // 2)
                    gemm_tile(T_IN1 + g, 0, H, 2 * n, pair(b % 2), n == 0, n == 7)

            in1_tiles(8, 20)
            cu_fills(0)
            in1_tiles(20, 36)
            cu_fills(1)
            in1_tiles(36, 52)
            pe.wait_ge(cu_free, 4)
            in_sbuf(pe, 4)
            in_sbuf(pe, 5)
            for n in range(3):
                fill(F_LAT + n, z1, n)
            in1_tiles(52, 56)
            L = (latT_hi, latT_lo)

            def up_tiles(first, lo, hi):
                for g in range(lo, hi):
                    b, n = divmod(g, 3)
                    B = 7 + b
                    if n == 0:
                        pe.wait_ge(gemm_free[B % 2], B // 2)
                    pe.wait_ge(tp_free, F_LAT + n + 1)
                    gemm_tile(T_UQ + g, 0, L, 2 * n, pair(B % 2), n == 0, n == 2)

            up_tiles(0, 0, 3)
            in_sbuf(pe, 6)
            for n in range(2):
                fill(F_LAT + 3 + n, z1, QC // 2 + n)
            up_tiles(0, 3, 9)
            for b in range(4):
                B = 10 + b
                pe.wait_ge(gemm_free[B % 2], B // 2)
                for n in range(2):
                    pe.wait_ge(tp_free, F_LAT + 4 + n)
                    gemm_tile(T_UKV + 2 * b + n, 0, L, QC + 2 * n, pair(B % 2), n == 0, n == 1)

            pe.wait_ge(tp_free, F_LAT + 5)
            pe.wait_ge(gemm_free[0], 7)
            pe.wait_ge(gemm_free[1], 7)
            pe.wait_ge(kpe_ready, 1)
            for t in range(TOK):
                mm = pe.transpose(ps[0:ROPE, 5, t * P:(t + 1) * P], kpe[:, t, :], ident[:])
            mm.then_inc(kpe_ready, 1)
            pe.wait_ge(rope_ready, 1)
            pe.wait_ge(kpe_ready, 3)

            def attn1_T(h):
                b = 4 * (h % 2)
                if h >= 2:
                    pe.wait_ge(at_qk, h - 1)
                for t in range(TOK):
                    pe.transpose(ps[:, b, t * P:(t + 1) * P], q1[:, t, h * QKH:h * QKH + NOPE], ident[:])
                    pe.transpose(ps[:, b, SEQ + t * P:SEQ + (t + 1) * P], kv1[:, t, h * 2 * VD:h * 2 * VD + NOPE],
                                 ident[:])
                    mm = pe.transpose(ps[0:ROPE, b + 1, t * P:(t + 1) * P],
                                      z1[:, t, h * ROPE:(h + 1) * ROPE], ident[:])
                mm.then_inc(at_T, 1)

            def attn1_S(h):
                b, e = 4 * (h % 2), h % 2
                pe.wait_ge(at_qk, h + 1)
                if h >= 2:
                    pe.wait_ge(at_max, h - 1)
                for t in range(TOK):
                    n = (t + 1) * P
                    o = ps[:, b + 2, t * P:t * P + n]
                    pe.matmul(o, qkT[:, e, 0, t * P:(t + 1) * P], qkT[:, e, 1, 0:n], start=True, stop=False)
                    mm = pe.matmul(o, qpeT[:, e, t * P:(t + 1) * P], kpeT[:, 0:n], start=False, stop=True)
                mm.then_inc(at_S, 1)

            def attn_PT(h, h0, n, src):
                b, e = 4 * (h % 2), h % 2
                pe.wait_ge(at_exp, h0 + h + 1)
                if h >= 2:
                    pe.wait_ge(at_out, h0 + h - 1)
                for k in range(n):
                    mm = pe.transpose(ps[:, b + 3, k * P:(k + 1) * P], src(e, k), ident[:])
                mm.then_inc(at_PT, 1)

            def attn1_PV(h):
                b, e = 4 * (h % 2), h % 2
                pe.wait_ge(at_pT, h + 1)
                v = [kv1[:, t, h * 2 * VD + NOPE:(h + 1) * 2 * VD] for t in range(TOK)]
                pT = [att1_p[:, e, k * P:(k + 1) * P] for k in range(3)]
                pe.matmul(ps[:, b + 3, 0:VD], pT[0], v[0], start=True, stop=True)
                pe.matmul(ps[:, b + 3, VD:2 * VD], pT[1], v[0], start=True, stop=False)
                pe.matmul(ps[:, b + 3, VD:2 * VD], pT[2], v[1], start=False, stop=True).then_inc(at_PV, 1)

            def src1(e, k):
                return att1_s[:, e, k * P:(k + 1) * P]

            attn1_T(0)
            for h in range(HEADS + 1):
                if h + 1 < HEADS:
                    attn1_T(h + 1)
                if h < HEADS:
                    attn1_S(h)
                if h >= 1:
                    attn_PT(h - 1, 0, 3, src1)
                    attn1_PV(h - 1)

            pe.wait_ge(at_out, HEADS)
            for n in range(4):
                fill(F_MIX1 + n, attn1, n)

            def column_sums(bank):
                for t in range(TOK):
                    for c in range(CC):
                        mm = pe.matmul(ps[:, bank, t:t + 1], lnsq[:, c, t * P:(t + 1) * P], ones[:, 0:1],
                                       start=(c == 0), stop=(c == CC - 1))
                mm.then_inc(ln_mm, 1)

            for g in range(32):
                half, b, i = g // 16, g // 4, g % 4
                if g == 2:
                    pe.wait_ge(conv_tap, TAPS * CC // 2)
                    pe.wait_ge(pool_add, 2 * (TAPS - 1))
                    pe.wait_ge(tp_free, F_MIX1 + 4)
                    for c in range(CC):
                        mm = pe.matmul(ps[:, 4, 0:SEQ], ones[:], cv[:, c, :], start=(c == 0), stop=(c == CC - 1))
                    mm.then_inc(ln_mm, 1)
                if g == 6:
                    pe.wait_ge(ln_act, 1)
                    column_sums(5)
                if g == 8:
                    pe.wait_ge(ln_dve, 2)
                    for t in range(TOK):
                        mm = pe.matmul(ps[:, 4, t * P:(t + 1) * P], ones[:], lnsq[:, 0, t * P:(t + 1) * P],
                                       start=True, stop=True)
                    mm.then_inc(ln_mm, 1)
                if g == 14:
                    pe.wait_ge(ln_act, 3)
                    column_sums(5)
                if i == 0 and b < 6:
                    pe.wait_ge(gemm_free[b % 2], 7 + b // 2)
                if i == 0 and b >= 6:
                    pe.wait_ge(y_ready, b - 5)
                if g < 4:
                    pe.wait_ge(tp_free, F_MIX1 + i + 1)
                if 16 <= g < 20:
                    pe.wait_ge(mix_conv, i + 1)
                gemm_tile(T_OUT1 + g, 0, H, CC * (1 - half) + 2 * i, pair(b % 2), i == 0, i == 3)

            def rows_tiles(c0, step, A, tiles, lo, hi, banks):
                k0 = sum(tiles[:lo])
                for n in range(lo, hi):
                    gemm_tile(c0 + n, step, A, k0, banks, n == 0, n == len(tiles) - 1)
                    k0 += tiles[n]

            def rows_rest(c0, A, tiles):
                T = len(tiles)
                with pe.Fori(1, 4) as n:
                    rows_tiles(c0, n * T, A, tiles, 0, T, lambda t, width: ps_flat[:, bass.ts(2 * n + t, NB)])

            def x_ready(base):
                return lambda n: pe.wait_ge(x_new, base + n // 2 + 1)

            def ff_tiles(c0, step, p, lo, hi):
                for n in range(lo, hi):
                    gemm_tile(c0 + n, step, H, 2 * n, pair(p), n == 0, n == 7)

            def ff1_turn(j):
                pe.wait_ge(gemm_free[1], G_FF1 + 1 + j)
                for f in range(2):
                    pe.wait_ge(tp_free, F_FF1 + f - 1 + 2 * j)
                    for k in range(2):
                        for t in range(TOK):
                            c = 2 * f + k
                            mm = pe.transpose(ps[:, 4 + f, k * SEQ + t * P:k * SEQ + (t + 1) * P],
                                              prod_s[:, t, c * P:(c + 1) * P], ident[:])
                    mm.then_inc(tp_ready, 1)

            with_fills(T_FF1, F_XT2, x_sb, x_ready(0), pair(0))
            ff_tiles(T_FF1 + 8, 0, 1, 0, 8)
            with pe.Fori(1, FB) as j:
                pe.wait_ge(gemm_free[0], G_FF1 + j)
                ff_tiles(T_FF1, 16 * j, 0, 0, 4)
                ff1_turn(j - 1)
                ff_tiles(T_FF1, 16 * j, 0, 4, 8)
                pe.wait_ge(gemm_free[1], G_FF1 + j)
                ff_tiles(T_FF1 + 8, 16 * j, 1, 0, 8)
            A = (aT_hi, aT_lo)
            pe.wait_ge(gemm_free[0], G_FF1 + FB)
            rows_tiles(T_DN1, 0, A, DN_TILES, 0, 4, pair(0))
            ff1_turn(FB - 1)
            rows_tiles(T_DN1, 0, A, DN_TILES, 4, 20, pair(0))
            pe.wait_ge(tp_free, F_XT3)
            rows_tiles(T_DN1, 0, A, DN_TILES, 20, 24, pair(0))
            rows_rest(T_DN1, A, DN_TILES)

            with_fills(T_IN2, F_XT3, x_sb, x_ready(4), pair(0))

            def in2_tiles(lo, hi):
                for g in range(lo, hi):
                    b, n = divmod(g, 8)
                    if n == 0:
                        pe.wait_ge(gemm_free[b % 2], G_IN2 + b // 2)
                    gemm_tile(T_IN2 + g, 0, H, 2 * n, pair(b % 2), n == 0, n == 7)

            in2_tiles(8, 12)
            in_sbuf(pe, 0, G_IN2)
            pe.wait_ge(tp_free, F_XT3 + 8)
            for d in range(2):
                for t in range(TOK):
                    mm = pe.transpose(ps[0:RANK, 4, d * SEQ + t * P:d * SEQ + (t + 1) * P],
                                      z2[:, t, LR + d * RANK:LR + (d + 1) * RANK], ident[:])
            mm.then_inc(gl_mm, 1)
            in2_tiles(12, 16)
            pe.wait_ge(gl_act, 1)
            pe.wait_ge(late_landed, 16 * 7)
            for d in range(2):
                for t in range(TOK):
                    mm = pe.matmul(ps[:, 4 + 2 * d + t, :], lrT[:, d, t * P:(t + 1) * P], wa2[:, d, :],
                                   start=True, stop=True)
            mm.then_inc(gl_mm, 1)
            in2_tiles(16, 28)
            pe.wait_ge(gl_dve, 1)
            for d in range(2):
                for h in range(GH):
                    for t in range(TOK):
                        at = h * SEQ + t * P
                        mm = pe.matmul(ps[:, 4 + 2 * d + at // NB, at % NB:at % NB + P],
                                       gb[:, 0, d, t * NB + h * DK:t * NB + (h + 1) * DK], tri[:, d, :],
                                       start=True, stop=True)
            mm.then_inc(gl_mm, 1)
            in2_tiles(28, 36)
            in_sbuf(pe, 2, G_IN2)
            in_sbuf(pe, 3, G_IN2)
            pe.wait_ge(gl_act, 3)
            for i, c0 in enumerate((QG, KG)):
                for h in range(GH):
                    for t in range(TOK):
                        at = h * SEQ + t * P
                        mm = pe.transpose(ps[:, 4 + 2 * i + at // NB, at % NB:at % NB + P],
                                          z2[:, t, c0 + h * DK:c0 + (h + 1) * DK], ident[:])
            mm.then_inc(gl_mm, 1)
            in2_tiles(36, 50)

            pe.wait_ge(fac_ready, 2)
            QE, KE, QI, KO = range(4)

            def gla_A(h):
                if h == 0:
                    pe.wait_ge(gl_act, 4)
                else:
                    pe.wait_ge(g_at, h)
                for d in range(2):
                    for t in range(TOK):
                        mm = pe.matmul(ps[:, 4, (2 * d + t) * P:(2 * d + t + 1) * P],
                                       fac[:, d, KE, h, t * P:(t + 1) * P], fac[:, d, QE, h, t * P:(t + 1) * P],
                                       start=True, stop=True)
                mm.then_inc(g_AT, 1)

            def gla_KT(h):
                if h >= 1:
                    pe.wait_ge(g_o, h)
                for d in range(2):
                    for t in range(TOK):
                        mm = pe.transpose(ps[:, 5, (2 * d + t) * P:(2 * d + t + 1) * P],
                                          fac[:, d, KO, h, t * P:(t + 1) * P], ident[:])
                mm.then_inc(g_KT, 1)

            def gla_S(h, d):
                pe.wait_ge(g_kt, h + 1)
                if h + d >= 1:
                    pe.wait_ge(g_st, 2 * h + d)
                for n in range(3):
                    c = n if d == 0 else 3 - n
                    r = slice(CHUNK * (c % 2), CHUNK * (c % 2) + CHUNK)
                    mm = pe.matmul(gla_sum(d, c), ktok[r, d, c // 2, :],
                                   z2[r, c // 2, VG + h * DV:VG + (h + 1) * DV], start=True, stop=True)
                mm.then_inc(g_SS, 1)

            def gla_O(h):
                pe.wait_ge(g_at, h + 1)
                pe.wait_ge(g_st, 2 * h + 2)
                for t in range(TOK):
                    o = ps[:, 5, t * DV:(t + 1) * DV]
                    pe.matmul(o, at_sb[:, t, :], z2[:, t, VG + h * DV:VG + (h + 1) * DV],
                              start=True, stop=False, skip_group_check=True)
                    parts = []
                    for half in range(2):
                        c = 2 * t + half
                        if c >= 1:
                            parts.append((half, 0, c, c - 1))
                        if c <= 2:
                            parts.append((half, 1, c, 2 - c))
                    for n, (half, d, c, i) in enumerate(parts):
                        mm = pe.matmul(ps[half * CHUNK:(half + 1) * CHUNK, 5, t * DV:(t + 1) * DV],
                                       fac[:, d, QI, h, c * CHUNK:(c + 1) * CHUNK], state[:, d, i, :],
                                       start=False, stop=(n == len(parts) - 1), skip_group_check=True)
                mm.then_inc(g_O, 1)

            def gated_fill(n):
                pe.wait_ge(mix2_ready, n + 1)
                if n == 3:
                    pe.wait_ge(kpe_ready, 5)
                fill(F_MIX2 + n, z2[:, :, QG:QG + 2 * NB], n)

            for g in range(50, 80):
                h, k = gla_slot(g)
                if k == 0 and 1 <= h <= GH:
                    gla_O(h - 1)
                if k == 0 and 0 <= h < GH:
                    gla_A(h)
                if k == 1 and 0 <= h < GH:
                    gla_KT(h)
                if k in (2, 4) and 0 <= h < GH:
                    gla_S(h, k // 2 - 1)
                if g == 74:
                    pe.wait_ge(rope_ready, 2)
                    pe.wait_ge(g_st, 2 * GH)
                    for q in range(KVH):
                        for t in range(TOK):
                            mm = pe.transpose(ps[:, 6, q * SEQ + t * P:q * SEQ + (t + 1) * P],
                                              z2[:, t, KA + q * HD:KA + (q + 1) * HD], ident[:])
                    mm.then_inc(kpe_ready, 1)
                if g >= MIX_FILL:
                    gated_fill(g - MIX_FILL)
                in2_tiles(g, g + 1)

            def attn2_T(p):
                if p < 2:
                    pe.wait_ge(rope_ready, 3)
                    pe.wait_ge(tp_free, F_MIX2 + 2)
                else:
                    pe.wait_ge(rope_ready, 4)
                    pe.wait_ge(tp_free, F_MIX2 + 3 + p)
                if p == 1:
                    pe.wait_ge(at_qk, HEADS + 1)
                for k in range(2):
                    h = HEAD_ORDER[2 * p + k]
                    for t in range(TOK):
                        mm = pe.transpose(ps[:, 4, k * SEQ + t * P:k * SEQ + (t + 1) * P],
                                          z2[:, t, h * HD:(h + 1) * HD], ident[:])
                mm.then_inc(at_T, 1)

            def attn2_S(i):
                g = HEAD_ORDER[i] * KVH // HEADS
                pe.wait_ge(at_qk, HEADS + i // 2 + 1)
                if i == 0:
                    pe.wait_ge(kpe_ready, 5)
                    pe.wait_ge(tp_free, F_MIX2 + 3)
                else:
                    pe.wait_ge(at_exp, HEADS + i)
                for t in range(TOK):
                    mm = pe.matmul(ps[:, 5, t * SEQ:(t + 1) * SEQ], att2_q[:, i // 2 % 2, i % 2, t * P:(t + 1) * P],
                                   kaT[:, g, :], start=True, stop=True)
                mm.then_inc(at_S, 1)

            def attn2_PT(i):
                pe.wait_ge(at_exp, HEADS + i + 1)
                if i == 0:
                    pe.wait_ge(tp_free, F_MIX2 + 4)
                else:
                    pe.wait_ge(at_pT, HEADS + i)
                for k in range(4):
                    mm = pe.transpose(ps[:, 6, k * P:(k + 1) * P],
                                      att2_s[:, i % 2, k // 2, (k % 2) * P:(k % 2 + 1) * P], ident[:])
                mm.then_inc(at_PT, 1)

            def attn2_PV(i):
                g = HEAD_ORDER[i] * KVH // HEADS
                pe.wait_ge(at_pT, HEADS + i + 1)
                if i >= 1:
                    pe.wait_ge(at_out, HEADS + i)
                for t in range(TOK):
                    for k in range(TOK):
                        at = (i % 2) * SEQ + t * HD
                        mm = pe.matmul(ps[:, 7, at:at + HD], att2_p[:, i % 2, 2 * t + k, :],
                                       z2[:, k, VA + g * HD:VA + (g + 1) * HD], start=(k == 0), stop=(k == 1))
                mm.then_inc(at_PV, 1)

            def attn2_fill(p):
                pe.wait_ge(at_out, HEADS + 2 * p + 2)
                pe.wait_ge(at_qk, HEADS + min(p + 2, 4))
                pe.wait_ge(tp_free, F_MIX2 + 4 + p)
                for k in range(2):
                    h = HEAD_ORDER[2 * p + k]
                    for t in range(TOK):
                        mm = pe.transpose(ps[:, 4, k * SEQ + t * P:k * SEQ + (t + 1) * P],
                                          z2[:, t, h * HD:(h + 1) * HD], ident[:])
                mm.then_inc(tp_ready, 1)

            pe.wait_ge(gemm_free[0], G_FF2)
            for g in range(32):
                if g < MIX_FILL + 4 - 80:
                    gated_fill(80 - MIX_FILL + g)
                if g % 4 == 0 and g // 4 < 4:
                    attn2_T(g // 4)
                if g % 2 == 1:
                    if 0 <= (g - 3) // 2 < HEADS:
                        attn2_PT((g - 3) // 2)
                    if 0 <= (g - 1) // 2 < HEADS:
                        attn2_S((g - 1) // 2)
                elif 0 <= (g - 4) // 2 < HEADS:
                    attn2_PV((g - 4) // 2)
                if g % 4 == 3 and 0 <= (g - 7) // 4 < 4:
                    attn2_fill((g - 7) // 4)
                if g < 16:
                    b, i = g // 4, g % 4
                    k0 = CC + 2 * i
                    if g < 4:
                        pe.wait_ge(tp_free, F_MIX2 + i + 1)
                    if i == 0 and b == 1:
                        pe.wait_ge(gemm_free[1], G_FF2)
                    if i == 0 and b >= 2:
                        pe.wait_ge(half_added, b - 1)
                else:
                    b, i = OUT2_TILES[g - 16]
                    k0 = 2 * PAIR_ORDER[i]
                    if b == 0:
                        pe.wait_ge(tp_free, F_MIX2 + 4 + i + 1)
                    if i == 0:
                        if b < 2:
                            pe.wait_ge(half_added, b + 3)
                        else:
                            pe.wait_ge(x_new, 8 + b - 1)
                gemm_tile(T_OUT2 + g, 0, H, k0, pair(b % 2), i == 0, i == 3)

            def ff2_turn(j, half):
                pe.wait_ge(gemm_free[half], G_FF2 + 1 + j)
                for c in range(4):
                    for t in range(TOK):
                        mm = pe.transpose(ps[:, 4 + 2 * half + c // 2, (c % 2) * SEQ + t * P:(c % 2) * SEQ + (t + 1) * P],
                                          raw_s[:, t, c * P:(c + 1) * P], ident[:])
                mm.then_inc(ct_ready, 1)

            with_fills(T_FF2, F_XT4, x_sb, lambda n: pe.wait_ge(x_new, 12), pair(0))
            ff_tiles(T_FF2 + 8, 0, 1, 0, 4)
            pe.wait_ge(tp_free, F_XT4 + 8)
            ff2_turn(0, 0)
            ff_tiles(T_FF2 + 8, 0, 1, 4, 8)
            with pe.Fori(1, FB) as j:
                pe.wait_ge(gemm_free[0], G_FF2 + j)
                ff_tiles(T_FF2, 16 * j, 0, 0, 4)
                pe.wait_ge(ct_free, 2 * j - 1)
                ff2_turn(j - 1, 1)
                ff_tiles(T_FF2, 16 * j, 0, 4, 8)
                pe.wait_ge(gemm_free[1], G_FF2 + j)
                ff_tiles(T_FF2 + 8, 16 * j, 1, 0, 4)
                pe.wait_ge(ct_free, 2 * j)
                ff2_turn(j, 0)
                ff_tiles(T_FF2 + 8, 16 * j, 1, 4, 8)
            pe.wait_ge(gemm_free[0], G_FF2 + FB)
            rows_tiles(T_DN2, 0, A, DN_TILES, 0, 4, pair(0))
            pe.wait_ge(ct_free, 2 * FB - 1)
            ff2_turn(FB - 1, 1)
            rows_tiles(T_DN2, 0, A, DN_TILES, 4, 20, pair(0))
            pe.wait_ge(aT_ready, FB)
            rows_tiles(T_DN2, 0, A, DN_TILES, 20, 24, pair(0))
            rows_rest(T_DN2, A, DN_TILES)

        @block.scalar
        def _(act):
            done = [0]

            def split_hi(c0, step):
                kc, width = SHAPES[c0]
                s = c0 % RING
                act.wait_ge(raw_landed[s], landed(c0, step))
                if c0 >= RING:
                    act.wait_ge(tile_used, c0 - RING + 1 + step)
                act.activation(w_hi[:, s, :kc, :width], raw[:, s, :kc, :width], ACT.Copy).then_inc(hi_ready, 1)

            def hi_upto(n):
                for g in range(done[0], n):
                    split_hi(g, 0)
                done[0] = max(done[0], n)

            def hi_tiles(c0, step, lo, hi):
                for g in range(c0 + lo, c0 + hi):
                    split_hi(g, step)

            count = [0]

            def step(ins):
                count[0] += 1
                ins.then_inc(act_step, 1)
                act.wait_ge(act_step, count[0])

            def fill_hi(F, dst, k, gain=None, bank=None):
                act.wait_ge(tp_ready, F + 1)
                b = 4 + F % 4
                for i in range(2):
                    at = G_AT[gain[0]] + gain[1] + i if gain else None
                    ins = act.activation(dst[:, k + i, :], ps[:, b, i * SEQ:(i + 1) * SEQ], ACT.Copy,
                                         **({"scale": gains[:, at:at + 1]} if gain else {}))
                ins.then_inc(tp_hi, 1)

            def squares(out, in_, name, at):
                return act.activation(out, in_, ACT.Square, accum_out=r_of(ss, name, at, 1))

            n = 0
            for name, k in GAINS:
                act.dma_start(rows[n:n + k, 0, :], a[name].rearrange("o (c p) -> (o c) p", p=P)).then_inc(rows_landed, 16)
                n += k
            taps = a["conv_w"][0].rearrange("k (c p) -> (k c) p", p=P)
            act.dma_start(rows[:, 1, :], taps[0:P, :]).then_inc(params_landed, 16)
            act.dma_start(rows[0:TAPS * CC - P, 2, :], taps[P:TAPS * CC, :]).then_inc(params_landed, 16)
            for k in range(3):
                act.dma_start(rows[0:2 * FC, 3 + k, :], a["conv_w_2"][0, k:k + 1, :].rearrange("o (c p) -> (o c) p", p=P))\
                   .then_inc(params_landed, 16)
            act.dma_start(rows[0:2 * FC, 6, :], a["conv_b_2"].rearrange("o (c p) -> (o c) p", p=P)).then_inc(params_landed, 16)
            act.dma_start(invf[:], a["inv_freq"].to_broadcast([P, 96])).then_inc(params_landed, 16)
            act.dma_start(kpe[:, 0, 0:TOK].bitcast(I32), a["positions"].rearrange("o (t p) -> p (o t)", p=P),
                          allow_slow_non_contiguous=True)\
               .then_inc(params_landed, 16)
            act.dma_start(sinkb[:], a["attn_sink_2"].to_broadcast([P, HEADS])).then_inc(params_landed, 16)

            act.wait_ge(rows_T, 1)
            act.activation(gains[:], ps[:, 0, 0:G_ROWS], ACT.Copy).then_inc(gains_ready, 1)
            act.wait_ge(gains_ready, 1)
            for n in range(8):
                fill_hi(F_XT1 + n, hT_hi, 2 * n, ("pre_mix_norm", 2 * n))
                if n == 3:
                    act.wait_ge(rows_T, 2)
                    act.activation(convw[:], ps[:, 2, 0:TAPS * CC], ACT.Copy).then_inc(gains_ready, 1)
                    act.wait_ge(rows_T, 3)
                    act.activation(conv2[:].rearrange("p k c -> p (k c)"), ps[:, 3, 0:8 * FC], ACT.Copy).then_inc(gains_ready, 1)
                hi_upto(n + 1)
            act.wait_ge(x_landed, 16 * TOK)
            for t in range(TOK):
                ins = squares(kv1[:, t, :], x_sb[:, t, :], "x0", t)
            ins.then_inc(sq_done, 1)
            hi_upto(11)

            def scaled(B, gend, dst, name, at, width, func=ACT.Copy, free=True):
                act.wait_ge(tile_used, gend)
                for t in range(TOK):
                    ins = act.activation(dst(t), ps[:, 2 * (B % 2) + t, :width], func, scale=r_of(rstd, name, at + t, 1))
                ins.then_inc(gemm_free[B % 2], 1)

            act.wait_ge(rstd_ready, r_count("x0"))
            scaled(0, T_IN1 + 8, lambda t: a_s[:, t, :], "x0", 0, NB)
            hi_upto(19)
            scaled(1, T_IN1 + 16, lambda t: sg_s[:, t, :], "x0", 0, NB, ACT.Sigmoid)

            def cu_evac(g):
                for f in range(2):
                    act.wait_ge(cu_ready, 2 * g + f + 1)
                    c = 4 * g + 2 * f
                    act.activation(uT[:, c:c + 2, TAPS - 1:], ps[:, 6 + f, :].rearrange("p (c s) -> p c s", c=2),
                                   ACT.Copy).then_inc(cu_free, 1)

            hi_upto(23)
            cu_evac(0)
            act.wait_ge(trig_arg, 1)
            tt = [trig_t[:, i, :].rearrange("p (t n) -> p t n", t=TOK) for i in range(4)]
            act.activation(tt[1], tt[0], ACT.Abs).then_inc(trig_abs, 1)
            act.wait_ge(trig_arg, 2)
            act.activation(trig[:, :, 0, :], tt[2], ACT.Sin)
            act.activation(trig[:, :, 1, :], tt[0], ACT.Sin).then_inc(trig_done, 1)
            hi_upto(27)
            scaled(2, T_IN1 + 24, lambda t: a_s[:, t, :], "x0", 0, NB)
            hi_upto(35)
            scaled(3, T_IN1 + 32, lambda t: sg_s[:, t, :], "x0", 0, NB, ACT.Sigmoid)
            hi_upto(39)
            cu_evac(1)
            hi_upto(43)

            def z1_block(b):
                act.wait_ge(tile_used, T_IN1 + 8 * (b + 5))
                for t in range(TOK):
                    ins = act.activation(z1[:, t, b * 448:(b + 1) * 448], ps[:, 2 * (b % 2) + t, :448], ACT.Copy,
                                         scale=r_of(rstd, "x0", t, 1))
                ins.then_inc(gemm_free[b % 2], 1)

            z1_block(0)
            hi_upto(51)
            z1_block(1)
            in_sbuf(act, 5)
            for t in range(TOK):
                squares(q1[:, t, 0:QL], z1[:, t, 0:QL], "lat", t)
            hi_upto(55)
            for n in range(3):
                fill_hi(F_LAT + n, latT_hi, 2 * n, ("q_norm", 2 * n))
            hi_upto(59)
            z1_block(2)
            in_sbuf(act, 6)
            for t in range(TOK):
                ins = squares(q1[:, t, QL:QL + KVL], z1[:, t, QL:QL + KVL], "lat", 2 + t)
            ins.then_inc(sq_done, 1)
            hi_upto(62)
            for n in range(2):
                fill_hi(F_LAT + 3 + n, latT_hi, QC + 2 * n, ("kv_norm", 2 * n))
            act.wait_ge(rstd_ready, r_count("lat"))
            for b in range(3):
                scaled(7 + b, T_UQ + 3 * (b + 1), lambda t: q1[:, t, b * NB:(b + 1) * NB], "lat", 0, NB)
                hi_upto([65, 67, 69][b])
            for b in range(4):
                scaled(10 + b, T_UKV + 2 * (b + 1), lambda t: kv1[:, t, b * NB:(b + 1) * NB], "lat", 2, NB)
                hi_upto([71, 73, 75, 77][b])

            act.wait_ge(kpe_ready, 2)
            act.activation(kpeT[:, :], ps[0:ROPE, 5, 0:SEQ], ACT.Copy).then_inc(kpe_ready, 1)

            def attn1_qk(h):
                b, e = 4 * (h % 2), h % 2
                act.wait_ge(at_T, h + 1)
                if h >= 2:
                    act.wait_ge(at_S, h - 1)
                act.activation(qkT[:, e].rearrange("p i s -> p (i s)"), ps[:, b, :], ACT.Copy)
                act.activation(qpeT[:, e, :], ps[0:ROPE, b + 1, 0:SEQ], ACT.Copy).then_inc(at_qk, 1)

            def attn_exp(h, h0, src, scale):
                e = h % 2
                act.wait_ge(at_max, h0 + h + 1)
                for t in range(TOK):
                    ins = act.activation(src(e, t), src(e, t), ACT.Exp, bias=amax[:, e, t, 2:3], scale=scale,
                                         accum_out=asum[:, e, 0, t:t + 1])
                ins.then_inc(at_exp, 1)

            def attn_pT(h, h0, dst, n):
                b, e = 4 * (h % 2), h % 2
                act.wait_ge(at_PT, h0 + h + 1)
                act.activation(dst(e), ps[:, b + 3, 0:n * P], ACT.Copy).then_inc(at_pT, 1)

            def s1(e, t):
                return att1_s[:, e, t * P:t * P + (t + 1) * P]

            attn1_qk(0)
            for h in range(HEADS + 1):
                if h + 1 < HEADS:
                    attn1_qk(h + 1)
                if h >= 1:
                    attn_pT(h - 1, 0, lambda e: att1_p[:, e, :], 3)
                if h < HEADS:
                    attn_exp(h, 0, s1, float(QKH) ** -0.5)
            act.wait_ge(at_out, HEADS)
            act.dma_start(grow_out[:], a["post_mix_norm"].to_broadcast([P, DM])).then_inc(grow_landed, 16)
            for t in range(TOK):
                ins = squares(kv1[:, t, 0:CONV], attn1[:, t, :], "attn", t)
            ins.then_inc(sq_done, 1)
            for n in range(4):
                fill_hi(F_MIX1 + n, hT_hi, CC + 2 * n, ("attn_out_norm", 2 * n))
            hi_upto(T_OUT1 + 5)

            def attn_half(n):
                scaled(14 + n, T_OUT1 + 4 * (n + 1), lambda t: y_out[:, (2 * n + t) * NB:(2 * n + t + 1) * NB], "attn",
                       0, NB)

            act.wait_ge(ln_dve, 1)
            act.activation(lnsq[:], cv[:], ACT.Square).then_inc(ln_act, 1)
            act.wait_ge(rstd_ready, r_count("attn"))
            hi_upto(T_OUT1 + 8)
            attn_half(0)
            hi_upto(T_OUT1 + 11)
            act.wait_ge(ln_dve, 3)
            for c in range(CC):
                g, b = G_AT["conv_ln_g"] + c, G_AT["conv_ln_b"] + c
                ins = act.activation(cv[:, c, :], cv[:, c, :], ACT.Silu, scale=gains[:, g:g + 1], bias=gains[:, b:b + 1])
            ins.then_inc(ln_act, 1)
            attn_half(1)
            hi_upto(T_OUT1 + 13)
            act.wait_ge(ln_act, 2)
            act.activation(lnsq[:], cv[:], ACT.Square).then_inc(ln_act, 1)
            for c in range(CC):
                g = G_AT["conv_out_norm"] + c
                ins = act.activation(hT_hi[:, c, :], cv[:, c, :], ACT.Copy, scale=gains[:, g:g + 1])
                if c % 2 == 1:
                    ins.then_inc(conv_hi, 1)
            hi_upto(T_OUT1 + 16)
            attn_half(2)
            hi_upto(T_OUT1 + 19)
            attn_half(3)

            def y_squares(n):
                act.wait_ge(y_ready, n + 1)
                for t in range(TOK):
                    ins = act.activation(lnsq[:].rearrange("p c s -> p (c s)")[:, bass.ts(2 * (n % 2) + t, NB)],
                                         y_out[:, (2 * n + t) * NB:(2 * n + t + 1) * NB], ACT.Square,
                                         accum_out=ss4[:, 4 * t + n:4 * t + n + 1])
                ins.then_inc(row_sq, 1)

            for n in range(4):
                hi_upto(T_OUT1 + 16 + 4 * n + 7)
                y_squares(n)

            def row_squares(c_end, step, n, y):
                act.wait_ge(tile_used, c_end + step)
                for t in range(TOK):
                    ins = act.activation(y[:, bass.ts(2 * n + t, NB)], ps_flat[:, bass.ts(2 * n + t, NB)], ACT.Square,
                                         accum_out=ss4[:, bass.ts(4 * t + n, 1)])
                ins.then_inc(row_sq, 1)

            def x_squares(base, junk, name):
                act.wait_ge(x_new, base + 4)
                for t in range(TOK):
                    ins = squares(junk(t), x_sb[:, t, :], name, t)
                ins.then_inc(sq_done, 1)

            def with_fills(c0, F, gain):
                hi_upto(c0 + 4)
                for n in range(4):
                    fill_hi(F + n, hT_hi, 2 * n, (gain, 2 * n))
                for n in range(4, 8):
                    fill_hi(F + n, hT_hi, 2 * n, (gain, 2 * n))
                    hi_upto(c0 + n + 1)

            with_fills(T_FF1, F_XT2, "pre_ffn_norm")
            x_squares(0, lambda t: y_out[:, t * DM:(t + 1) * DM], "x1")
            act.wait_ge(rstd_ready, r_count("x1"))

            def silu1(j):
                act.wait_ge(tile_used, T_FF1 + 8 + 16 * j)
                for t in range(TOK):
                    ins = act.activation(gate_s[:, t, :], ps[:, t, :], ACT.Silu, scale=r_of(rstd, "x1", t, 1))
                ins.then_inc(gemm_free[0], 1)

            def turn_hi(j):
                for f in range(2):
                    act.wait_ge(tp_ready, F_FF1 + f + 1 + 2 * j)
                    act.activation(aT_hi_flat[:, bass.ts(2 * j + f, 2 * SEQ)], ps[:, 4 + f, :], ACT.Copy).then_inc(tp_hi, 1)

            aT_hi_flat = aT_hi[:].rearrange("p c s -> p (c s)")
            hi_upto(T_FF1 + 11)
            silu1(0)
            hi_upto(T_FF1 + 16)
            with act.Fori(1, FB) as j:
                hi_tiles(T_FF1, 16 * j, 0, 7)
                turn_hi(j - 1)
                hi_tiles(T_FF1, 16 * j, 7, 11)
                act.wait_ge(gemm_free[1], G_FF1 + j)
                silu1(j)
                hi_tiles(T_FF1, 16 * j, 11, 16)
            done[0] = T_DN1
            hi_upto(T_DN1 + 7)
            turn_hi(FB - 1)
            act.dma_start(grow_dn[:], a["post_ffn_norm"].to_broadcast([P, DM])).then_inc(grow_landed, 16)
            hi_upto(T_DN1 + 24)
            c0, T = T_DN1, 24
            with act.Fori(1, 4) as n:
                hi_tiles(c0, n * T, 0, 3)
                row_squares(c0, n * T, n - 1, y_dn)
                hi_tiles(c0, n * T, 3, T)
            done[0] = T_IN2
            hi_upto(T_IN2 + 3)
            row_squares(T_IN2, 0, 3, y_dn)

            act.wait_ge(row_y, 8)
            for i, name in enumerate(("attn_q_norm_g_2", "attn_k_norm_g_2")):
                act.dma_start(gqk[:, i, :], a[name].to_broadcast([P, HD])).then_inc(late_landed, 16)
            act.dma_start(gla_g[:], a["gla_out_norm_g_2"].to_broadcast([P, DV])).then_inc(late_landed, 16)
            for d, name in enumerate(("fwd", "bwd")):
                act.dma_start(wa2[0:RANK, d, :], a[f"gla_wa2_{name}_2"][0]).then_inc(late_landed, 16)
                act.dma_start(wa2[RANK:RANK + 1, d, :], a[f"gla_ba_{name}_2"]).then_inc(late_landed, 16)
            with_fills(T_IN2, F_XT3, "norm1_g_2")
            x_squares(4, lambda t: fac[:, t].rearrange("p a h s -> p (a h s)")[:, 0:DM], "x2")
            act.wait_ge(rstd_ready, r_count("x2"))

            def z2_block(p):
                n = B2_ORDER[p]
                act.wait_ge(tile_used, T_IN2 + 8 * (p + 1))
                for t in range(TOK):
                    ins = act.activation(z2[:, t, n * W2:(n + 1) * W2], ps[:, 2 * (p % 2) + t, :W2], ACT.Copy,
                                         scale=r_of(rstd, "x2", t, 1))
                ins.then_inc(gemm_free[p % 2], 1)

            b_sum = [gb[:, 1, d, :].rearrange("p (h s) -> p h s", h=GH) for d in range(2)]
            hi_upto(T_IN2 + 11)
            z2_block(0)
            hi_upto(T_IN2 + 15)
            act.wait_ge(gl_mm, 1)
            act.wait_ge(consts_ready, 3)
            act.activation(lrT[0:RANK].rearrange("p d s -> p (d s)"), ps[0:RANK, 4, :], ACT.Copy).then_inc(gl_act, 1)
            hi_upto(T_IN2 + 19)
            z2_block(1)
            act.wait_ge(gl_mm, 2)
            for d in range(2):
                for t in range(TOK):
                    g = gb[:, 0, d, t * NB:(t + 1) * NB]
                    step(act.activation(g, ps[:, 4 + 2 * d + t, :], ACT.Abs))
            step(act.activation(gb[:, 0], gb[:, 0], ACT.Exp, scale=-1.0))
            act.activation(gb[:, 0], gb[:, 0], ACT.Ln, bias=1.0).then_inc(gl_act, 1)
            hi_upto(T_IN2 + 27)
            z2_block(2)
            hi_upto(T_IN2 + 31)
            act.wait_ge(gl_mm, 3)
            for d in range(2):
                for i in range(2):
                    ins = act.activation(gb[:, 1, d, i * NB:(i + 1) * NB], ps[:, 4 + 2 * d + i, :], ACT.Copy)
            ins.then_inc(gl_act, 1)
            hi_upto(T_IN2 + 35)
            z2_block(3)
            hi_upto(T_IN2 + 39)
            act.wait_ge(gl_mm, 4)
            for i in range(2):
                act.activation(qT2[:, 2 * i:2 * i + 2, :], ps[:, 4 + i, :].rearrange("p (h s) -> p h s", h=2), ACT.Copy,
                               scale=float(DK) ** -0.5)
                ins = act.activation(kT2[:, 2 * i:2 * i + 2, :], ps[:, 6 + i, :].rearrange("p (h s) -> p h s", h=2), ACT.Copy)
            ins.then_inc(gl_act, 1)
            S16 = 1.0 / 16.0
            for d in range(2):
                dd = [gb[:, 0, i, :].rearrange("p (h s) -> p h s", h=GH) for i in range(2)]
                act.wait_ge(fac_exp, 2 * d + 1)
                act.activation(fac[:, d, 0], dd[0], ACT.Exp, scale=S16)
                act.activation(fac[:, d, 1], dd[0], ACT.Exp, scale=-S16)
                hi_upto(T_IN2 + 41 + 4 * d)
                act.activation(fac[:, d, 2], b_sum[d], ACT.Exp, scale=S16)
                act.activation(decay[:, d, :], last_of(b_sum[d], d), ACT.Exp, scale=S16)
                act.activation(fac[:, d, 3], dd[1], ACT.Exp, scale=-S16).then_inc(fac_exp, 1)
                hi_upto(T_IN2 + 43 + 4 * d)
                if d == 0:
                    z2_block(4)

            def part_squares(part):
                name, h0, n, p, _ = QK_PARTS[part]
                in_sbuf(act, p, G_IN2)
                in_sbuf(act, p - 1, G_IN2)
                if part == 2:
                    act.wait_ge(sq_done, 7)
                base = (0, 4, 0)[part]
                for t in range(TOK):
                    for h in range(n):
                        i = t * n + h
                        ins = squares(gb_flat[:, (base + i) * HD:(base + i + 1) * HD],
                                      z2[:, t, (h0 + h) * HD:(h0 + h + 1) * HD], name, i)
                ins.then_inc(sq_done, 1)

            def k_copy(h):
                act.wait_ge(g_KT, h + 1)
                if h >= 1:
                    act.wait_ge(g_SS, 2 * h)
                act.activation(ktok[:].rearrange("p d t k -> p (d t k)"), ps[:, 5, :], ACT.Copy).then_inc(g_kt, 1)

            def gla_squares(h):
                act.wait_ge(g_o, h + 1)
                for t in range(TOK):
                    ins = act.activation(gb_flat[:, 3584 + t * DV:3584 + (t + 1) * DV],
                                         z2[:, t, QG + h * DV:QG + (h + 1) * DV], ACT.Square,
                                         accum_out=r_of(ss, "gla", t * GH + h, 1))
                    if h < GH - 1:
                        step(ins)
                if h == GH - 1:
                    ins.then_inc(sq_done, 1)

            def split_copy(F, pair_at, bank, after=None):
                act.wait_ge(tp_ready, F + 1)
                if after is not None:
                    act.wait_ge(tile_used, after)
                act.activation(hT_hi[:, 2 * pair_at:2 * pair_at + 2, :], ps[:, bank, :].rearrange("p (c s) -> p c s", c=2),
                               ACT.Copy).then_inc(tp_hi, 1)

            for g in range(47, 80):
                h, k = gla_slot(g - 2)
                if g % 8 == 3:
                    z2_block(g // 8 - 1)
                if k == 0 and 1 <= h <= GH:
                    gla_squares(h - 1)
                if k == 1 and 0 <= h < GH:
                    k_copy(h)
                if g == 60:
                    part_squares(0)
                if g == 68:
                    part_squares(1)
                if g == 76:
                    act.wait_ge(kpe_ready, 4)
                    act.activation(kaT[:].rearrange("p g s -> p (g s)"), ps[:, 6, :], ACT.Copy).then_inc(kpe_ready, 1)
                    for p in (0, 5, 8):
                        in_sbuf(act, p, G_IN2)
                    act.activation(z2[:, :, GG:GG + 2 * NB], z2[:, :, GG:GG + 2 * NB], ACT.Silu).then_inc(gate2_ready, 1)
                hi_upto(T_IN2 + g + 1)

            for g in range(32):
                if 0 <= g - 2 - (MIX_FILL - 80) < 4:
                    n = g - 2 - (MIX_FILL - 80)
                    split_copy(F_MIX2 + n, 4 + n, 4 + (F_MIX2 + n) % 4, T_IN2 + 77 + n)
                if g == 3:
                    z2_block(9)
                if g % 4 == 2 and g // 4 < 4:
                    p = g // 4
                    act.wait_ge(at_T, HEADS + p + 1)
                    if p >= 2:
                        act.wait_ge(at_S, HEADS + 2 * p - 2)
                    act.activation(att2_q[:, p % 2].rearrange("p k s -> p (k s)"), ps[:, 4, :], ACT.Copy).then_inc(at_qk, 1)
                if g == 4:
                    part_squares(2)
                if g % 2 == 1:
                    i = (g - 5) // 2
                    if 0 <= i < HEADS:
                        act.wait_ge(at_PT, HEADS + i + 1)
                        if i >= 2:
                            act.wait_ge(at_PV, HEADS + i - 1)
                        act.activation(att2_p[:, i % 2].rearrange("p k s -> p (k s)"), ps[:, 6, :], ACT.Copy).then_inc(at_pT, 1)
                    i = (g - 3) // 2
                    if 0 <= i < HEADS:
                        e, h = i % 2, HEAD_ORDER[i]
                        act.wait_ge(at_max, HEADS + i + 1)
                        if i >= 2:
                            act.wait_ge(at_PT, HEADS + i - 1)
                        for t in range(TOK):
                            act.activation(amax[:, e, t, 3:4], sinkb[:, h:h + 1], ACT.Exp, bias=amax[:, e, t, 2:3])
                        for t in range(TOK):
                            ins = act.activation(att2_s[:, e, t, :], ps[:, 5, t * SEQ:(t + 1) * SEQ], ACT.Exp,
                                                 bias=amax[:, e, t, 2:3], scale=float(HD) ** -0.5,
                                                 accum_out=asum[:, e, 0, t:t + 1])
                        ins.then_inc(at_exp, 1)
                i = (g - 6) // 2
                if g % 2 == 0 and 0 <= i < HEADS:
                    e, h = i % 2, HEAD_ORDER[i]
                    act.wait_ge(at_PV, HEADS + i + 1)
                    act.wait_ge(at_sum, i + 1)
                    for t in range(TOK):
                        ins = act.activation(z2[:, t, h * HD:(h + 1) * HD],
                                             ps[:, 7, e * SEQ + t * HD:e * SEQ + (t + 1) * HD], ACT.Copy,
                                             scale=asum[:, e, 1, t:t + 1])
                    ins.then_inc(at_out, 1)
                if g % 4 == 1 and 0 <= (g - 9) // 4 < 4:
                    p = (g - 9) // 4
                    split_copy(F_MIX2 + 4 + p, PAIR_ORDER[p], 4)
                hi_upto(T_OUT2 + g + 1)

            with_fills(T_FF2, F_XT4, "norm2_g_2")
            x_squares(8, lambda t: y_out[:, t * DM:(t + 1) * DM], "x3")
            act.wait_ge(rstd_ready, r_count("x3"))

            def copy2(j, half):
                act.wait_ge(tile_used, T_FF2 + 8 + 8 * half + 16 * j)
                for t in range(TOK):
                    ins = act.activation(raw_s[:, t, :], ps[:, 2 * half + t, :], ACT.Copy, scale=r_of(rstd, "x3", t, 1))
                ins.then_inc(gemm_free[half], 1)

            def center2(j, half):
                act.wait_ge(ct_ready, 2 * j + half + 1)
                dst = cg if half == 0 else cval
                for c in range(4):
                    k = 4 * j + c + FC * half
                    ins = act.activation(dst[:, c, :], ps[:, 4 + 2 * half + c // 2, (c % 2) * SEQ:(c % 2 + 1) * SEQ],
                                         ACT.Identity, scale=conv2[:, 1, bass.ts(k, 1)], bias=conv2[:, 3, bass.ts(k, 1)])
                    if c % 2:
                        ins.then_inc(ct_center, 1)

            def silu2(j):
                act.wait_ge(ct_free, 2 * j + 1)
                act.activation(cg[:], cg[:], ACT.Silu).then_inc(cg_silu, 1)

            def hidden_hi(j):
                act.wait_ge(prod_ready, j + 1)
                act.activation(aT_hi_flat[:, bass.ts(j, 4 * SEQ)], cg[:].rearrange("p c s -> p (c s)"), ACT.Copy)\
                   .then_inc(aT_hi_ready, 1)

            hi_upto(T_FF2 + 11)
            copy2(0, 0)
            hi_upto(T_FF2 + 15)
            center2(0, 0)
            hi_upto(T_FF2 + 16)
            with act.Fori(1, FB) as j:
                hi_tiles(T_FF2, 16 * j, 0, 2)
                silu2(j - 1)
                hi_tiles(T_FF2, 16 * j, 2, 3)
                act.wait_ge(ct_ready, 2 * j - 1)
                copy2(j - 1, 1)
                hi_tiles(T_FF2, 16 * j, 3, 7)
                center2(j - 1, 1)
                hi_tiles(T_FF2, 16 * j, 7, 11)
                act.wait_ge(ct_ready, 2 * j)
                copy2(j, 0)
                hidden_hi(j - 1)
                hi_tiles(T_FF2, 16 * j, 11, 15)
                act.wait_ge(aT_ready, j)
                center2(j, 0)
                hi_tiles(T_FF2, 16 * j, 15, 16)
            done[0] = T_DN2
            hi_upto(T_DN2 + 2)
            silu2(FB - 1)
            hi_upto(T_DN2 + 3)
            act.wait_ge(ct_ready, 2 * FB - 1)
            copy2(FB - 1, 1)
            hi_upto(T_DN2 + 7)
            center2(FB - 1, 1)
            hi_upto(T_DN2 + 11)
            hidden_hi(FB - 1)
            hi_upto(T_DN2 + 24)
            with act.Fori(1, 4) as n:
                hi_tiles(T_DN2, 24 * n, 0, 24)

        @block.vector
        def _(dve):
            done = [0]
            count = [0]

            def split_lo(c0, step):
                kc, width = SHAPES[c0]
                s = c0 % RING
                dve.wait_ge(hi_ready, c0 + 1 + step)
                dve.tensor_tensor(w_lo[:, s, :kc, :width], raw[:, s, :kc, :width],
                                  w_hi[:, s, :kc, :width].bitcast(F32), ALU.subtract).then_inc(lo_ready, 1)

            def lo_upto(n):
                for g in range(done[0], n):
                    split_lo(g, 0)
                done[0] = max(done[0], n)

            def lo_tiles(c0, step, lo, hi):
                for g in range(c0 + lo, c0 + hi):
                    split_lo(g, step)

            def step(ins):
                count[0] += 1
                ins.then_inc(dve_step, 1)
                dve.wait_ge(dve_step, count[0])

            def fill_lo(F, hi, lo, k, gain=None):
                dve.wait_ge(tp_hi, F + 1)
                b = 4 + F % 4
                for i in range(2):
                    src = ps[:, b, i * SEQ:(i + 1) * SEQ]
                    h = hi[:, k + i, :].bitcast(F32)
                    if gain:
                        at = G_AT[gain[0]] + gain[1] + i
                        ins = dve.scalar_tensor_tensor(out=lo[:, k + i, :], in0=src, scalar=gains[:, at:at + 1],
                                                       in1=h, op0=ALU.mult, op1=ALU.subtract)
                    else:
                        ins = dve.tensor_tensor(lo[:, k + i, :], src, h, ALU.subtract)
                ins.then_inc(tp_free, 1)

            def mean_sq(name, width, src=None):
                dve.tensor_scalar(r_of(ms, name), r_of(ss, name) if src is None else src, 1.0 / width, EPS, ALU.mult,
                                  ALU.add).then_inc(ms_ready, 1)

            dve.memset(ones[:], 1.0).then_inc(consts_ready, 1)
            dve.memset(minus_half[:], -0.5).then_inc(consts_ready, 1)
            step(dve.memset(uT[:, :, 0:TAPS - 1], 0.0))
            for n in range(4):
                if n == 0:
                    dve.wait_ge(gains_ready, 1)
                fill_lo(F_XT1 + n, hT_hi, hT_lo, 2 * n, ("pre_mix_norm", 2 * n))
                lo_upto(n + 1)
            for n in range(4, 8):
                fill_lo(F_XT1 + n, hT_hi, hT_lo, 2 * n, ("pre_mix_norm", 2 * n))
                lo_upto(n + 1)
            dve.wait_ge(sq_done, 1)
            mean_sq("x0", DM)
            lo_upto(12)

            TWO_PI = 2.0 * np.pi
            C1 = 6.28125
            C2 = float(np.float32(np.round((TWO_PI - C1) * 2 ** 21) / 2 ** 21))
            C3 = float(np.float32(TWO_PI - C1 - C2))
            ROUND = 12582912.0
            PI_IN = 3.1415925
            dve.wait_ge(params_landed, 16 * 9)
            dve.wait_ge(masks_ready, 1)
            dve.wait_ge(gains_ready, 3)
            step(dve.tensor_copy(posf[:, 0, :], kpe[:, 0, 0:TOK].bitcast(I32)))
            tt = [trig_t[:, i, :].rearrange("p (t n) -> p t n", t=TOK) for i in range(4)]
            for t in range(TOK):
                dve.tensor_scalar(tt[0][:, t, 0:32], invf[:, 0:32], posf[:, 0, t:t + 1], None, ALU.mult)
                ins = dve.tensor_scalar(tt[0][:, t, 32:96], invf[:, 32:96], posf[:, 1, t:t + 1], None, ALU.mult)
            step(ins)
            step(dve.tensor_scalar(tt[1], tt[0], float(1.0 / TWO_PI), None, ALU.mult))
            step(dve.tensor_scalar(tt[1], tt[1], ROUND, None, ALU.add))
            step(dve.tensor_scalar(tt[1], tt[1], -ROUND, None, ALU.add))
            lo_upto(14)
            for c in (C1, C2, C3):
                step(dve.scalar_tensor_tensor(out=tt[0], in0=tt[1], scalar=-c, in1=tt[0], op0=ALU.mult, op1=ALU.add))
            dve.tensor_scalar(tt[0], tt[0], PI_IN, -PI_IN, ALU.min, ALU.max).then_inc(trig_arg, 1)
            lo_upto(16)
            lo_upto(19)

            def gate_u(g):
                dve.wait_ge(gemm_free[1], g + 1)
                dve.tensor_tensor(a_s, a_s, sg_s, ALU.mult).then_inc(u_ready, 1)

            gate_u(0)
            lo_upto(23)
            dve.wait_ge(trig_abs, 1)
            dve.tensor_scalar(tt[2], tt[1], -1.0, float(np.pi / 2), ALU.mult, ALU.add).then_inc(trig_arg, 1)

            tap = [0]

            def taps(n):
                for _ in range(n):
                    i = tap[0]
                    if i == TAPS * CC // 2:
                        return
                    g, r = divmod(i, 2 * TAPS)
                    j, c = divmod(r, 2)
                    c += 4 * g
                    if r == 0:
                        dve.wait_ge(cu_free, 2 * g + 2)
                    w = convw[:, j * CC + c:j * CC + c + 1]
                    u = uT[:, c, j:j + SEQ]
                    if j == 0:
                        b = G_AT["conv_b"] + c
                        ins = dve.tensor_scalar(cv[:, c, :], u, w, gains[:, b:b + 1], ALU.mult, ALU.add)
                    else:
                        dve.wait_ge(conv_tap, i - 1)
                        ins = dve.scalar_tensor_tensor(out=cv[:, c, :], in0=u, scalar=w, in1=cv[:, c, :],
                                                       op0=ALU.mult, op1=ALU.add)
                    ins.then_inc(conv_tap, 1)
                    tap[0] += 1

            for g in range(24, 36):
                lo_upto(g)
                taps(3)
            gate_u(1)
            for g in range(36, 56):
                lo_upto(g)
                taps(3)
            for n in range(3):
                fill_lo(F_LAT + n, latT_hi, latT_lo, 2 * n, ("q_norm", 2 * n))
            for g in range(56, 60):
                lo_upto(g)
                taps(3)
            lo_upto(60)
            dve.wait_ge(sq_done, 2)
            at = R["lat"][0]
            dve.tensor_scalar(ms[:, at:at + 2], ss[:, at:at + 2], 1.0 / QL, EPS, ALU.mult, ALU.add)
            dve.tensor_scalar(ms[:, at + 2:at + 4], ss[:, at + 2:at + 4], 1.0 / KVL, EPS, ALU.mult,
                              ALU.add).then_inc(ms_ready, 1)
            lo_upto(62)
            for n in range(2):
                fill_lo(F_LAT + 3 + n, latT_hi, latT_lo, QC + 2 * n, ("kv_norm", 2 * n))
            for g in range(63, 71):
                lo_upto(g)
                taps(3)

            def rope(dst, src, half, heads, at, tmp, sem_done):
                x1, x2 = src[:, :, :, 0:half], src[:, :, :, half:2 * half]
                cos, sin = (trig[:, :, i, at:at + half].unsqueeze(2).to_broadcast([P, TOK, heads, half]) for i in range(2))
                t1, t2 = tmp
                dve.tensor_tensor(t1, x1, cos, ALU.mult)
                step(dve.tensor_tensor(t2, x2, sin, ALU.mult))
                dve.tensor_tensor(dst[:, :, :, 0:half], t1, t2, ALU.subtract)
                step(dve.tensor_tensor(dst[:, :, :, half:2 * half], x2, cos, ALU.mult))
                step(dve.tensor_tensor(t1, x1, sin, ALU.mult))
                dve.tensor_tensor(dst[:, :, :, half:2 * half], dst[:, :, :, half:2 * half], t1, ALU.add).then_inc(sem_done, 1)

            dve.wait_ge(trig_done, 1)
            in_sbuf(dve, 6)
            tmp = [z1[:, :, 512 + 256 * i:768 + 256 * i].rearrange("p t (h n) -> p t h n", h=HEADS) for i in range(2)]
            rope(kpe[:].unsqueeze(2), z1[:, :, QL + KVL:Z1].unsqueeze(2), 32, 1, 0, [t[:, :, 0:1, :] for t in tmp], kpe_ready)
            lo_upto(73)
            in_sbuf(dve, 8)
            in_sbuf(dve, 9)
            dve.wait_ge(kpe_ready, 1)
            rope(z1[:, :, 0:512].rearrange("p t (h n) -> p t h n", h=HEADS),
                 q1[:].rearrange("p t (h n) -> p t h n", h=HEADS)[:, :, :, NOPE:QKH], 32, HEADS, 0, tmp, rope_ready)
            lo_upto(77)

            def attn1_max(h):
                b, e = 4 * (h % 2), h % 2
                dve.wait_ge(at_S, h + 1)
                if h >= 2:
                    dve.wait_ge(at_PT, h - 1)
                step(dve.tensor_tensor(att1_s[:, e, :], ps[:, b + 2, 0:3 * P], mask1[:], ALU.add))
                dve.tensor_reduce(amax[:, e, 0, 0:1], att1_s[:, e, 0:P], X, ALU.max)
                step(dve.tensor_reduce(amax[:, e, 1, 0:1], att1_s[:, e, P:3 * P], X, ALU.max))
                dve.tensor_scalar(amax[:, e, :, 2:3], amax[:, e, :, 0:1], -float(QKH) ** -0.5, None,
                                  ALU.mult).then_inc(at_max, 1)

            def attn_out(h, h0, dst):
                b, e = 4 * (h % 2), h % 2
                dve.wait_ge(at_PV, h0 + h + 1)
                for t in range(TOK):
                    ins = dve.tensor_scalar(dst(t), ps[:, b + 3, t * P:(t + 1) * P], asum[:, e, 1, t:t + 1], None, ALU.mult)
                ins.then_inc(at_out, 1)

            for h in range(HEADS + 1):
                if h < HEADS:
                    attn1_max(h)
                if h >= 1:
                    e = (h - 1) % 2
                    dve.wait_ge(at_exp, h)
                    step(dve.reciprocal(asum[:, e, 1, :], asum[:, e, 0, :]))
                    taps(4)
                    attn_out(h - 1, 0, lambda t: attn1[:, t, (h - 1) * VD:h * VD])
            dve.wait_ge(sq_done, 3)
            mean_sq("attn", CONV)
            taps(TAPS * CC)
            for n in range(4):
                fill_lo(F_MIX1 + n, hT_hi, hT_lo, CC + 2 * n, ("attn_out_norm", 2 * n))
            lo_upto(T_OUT1 + 5)

            dve.wait_ge(ln_mm, 1)
            dve.wait_ge(conv_tap, TAPS * CC // 2)
            sums = ps[:, 4, 0:SEQ].unsqueeze(1).to_broadcast([P, CC, SEQ])
            dve.scalar_tensor_tensor(out=cv[:], in0=sums, scalar=-1.0 / CONV, in1=cv[:], op0=ALU.mult,
                                     op1=ALU.add).then_inc(ln_dve, 1)
            lo_upto(T_OUT1 + 8)
            dve.wait_ge(ln_mm, 2)
            mean_sq("ln", CONV, ps[:, 5, 0:TOK])
            dve.wait_ge(rstd_ready, r_count("ln"))
            for t in range(TOK):
                ins = dve.tensor_scalar(lnsq[:, 0, t * P:(t + 1) * P], ident[:], r_of(rstd, "ln", t, 1), None, ALU.mult)
            ins.then_inc(ln_dve, 1)
            lo_upto(T_OUT1 + 9)
            dve.wait_ge(ln_mm, 3)
            spread = ps[:, 4, 0:SEQ].unsqueeze(1).to_broadcast([P, CC, SEQ])
            dve.tensor_tensor(cv[:], spread, cv[:], ALU.mult).then_inc(ln_dve, 1)
            lo_upto(T_OUT1 + 13)
            for c in range(CC):
                g = G_AT["conv_out_norm"] + c
                if c % 2 == 0:
                    dve.wait_ge(conv_hi, c // 2 + 1)
                ins = dve.scalar_tensor_tensor(out=hT_lo[:, c, :], in0=cv[:, c, :], scalar=gains[:, g:g + 1],
                                               in1=hT_hi[:, c, :].bitcast(F32), op0=ALU.mult, op1=ALU.subtract)
                if c % 2 == 1:
                    ins.then_inc(mix_conv, 1)
            lo_upto(T_OUT1 + 15)
            dve.wait_ge(ln_mm, 4)
            mean_sq("conv", CONV, ps[:, 5, 0:TOK])
            lo_upto(T_OUT1 + 19)
            dve.wait_ge(rstd_ready, r_count("conv"))

            def conv_half(n):
                dve.wait_ge(tile_used, T_OUT1 + 16 + 4 * (n + 1))
                in_sbuf(dve, 14 + n)
                for t in range(TOK):
                    y = y_out[:, (2 * n + t) * NB:(2 * n + t + 1) * NB]
                    ins = dve.scalar_tensor_tensor(out=y, in0=ps[:, 2 * (n % 2) + t, :], scalar=r_of(rstd, "conv", t, 1),
                                                   in1=y, op0=ALU.mult, op1=ALU.add)
                ins.then_inc(y_ready, 1)

            def times_gain(n):
                dve.wait_ge(row_sq, n + 1)
                y = y_out[:, 2 * n * NB:(2 * n + 2) * NB].rearrange("p (t n) -> p t n", t=TOK)
                dve.tensor_tensor(y, y, grow_out[:, cols(n)].unsqueeze(1).to_broadcast([P, TOK, NB]),
                                  ALU.mult).then_inc(row_y, 1)

            dve.wait_ge(grow_landed, 16)
            for n in range(4):
                lo_upto(T_OUT1 + 16 + 4 * n + 6)
                conv_half(n)
                if n > 0:
                    times_gain(n - 1)


            def row_scale(base, n, y, grow, scale):
                dve.wait_ge(row_sq, base + 1 + n)
                for t in range(TOK):
                    ins = dve.scalar_tensor_tensor(out=y[:, bass.ts(2 * n + t, NB)], in0=ps_flat[:, bass.ts(2 * n + t, NB)],
                                                   scalar=r_of(rstd, scale, t, 1) if scale else 1.0,
                                                   in1=grow[:, cols(n)], op0=ALU.mult, op1=ALU.mult)
                ins.then_inc(row_y, 1)

            def new_x(name, y, c_next, between=None):
                if between:
                    dve.wait_ge(row_sq, 4)
                step(dve.tensor_reduce(r_of(ss, name), ss4.rearrange("p (t n) -> p t n", t=TOK), X, ALU.add))
                mean_sq(name, DM)
                if between:
                    between()
                    dve.wait_ge(row_y, 4)
                lo_upto(c_next + 1)
                dve.wait_ge(rstd_ready, r_count(name))
                for n in range(4):
                    for t in range(TOK):
                        ins = dve.scalar_tensor_tensor(out=x_sb[:, t, cols(n)], in0=y[:, bass.ts(2 * n + t, NB)],
                                                       scalar=r_of(rstd, name, t, 1), in1=x_sb[:, t, cols(n)],
                                                       op0=ALU.mult, op1=ALU.add)
                    ins.then_inc(x_new, 1)

            def with_fills(c0, F, gain):
                for n in range(4):
                    fill_lo(F + n, hT_hi, hT_lo, 2 * n, (gain, 2 * n))
                    lo_upto(c0 + n + 1)
                for n in range(4, 8):
                    fill_lo(F + n, hT_hi, hT_lo, 2 * n, (gain, 2 * n))
                    lo_upto(c0 + n + 1)

            new_x("out1", y_out, T_FF1, lambda: times_gain(3))

            with_fills(T_FF1, F_XT2, "pre_ffn_norm")
            dve.wait_ge(sq_done, 4)
            mean_sq("x1", DM)
            lo_upto(T_FF1 + 16)
            dve.wait_ge(rstd_ready, r_count("x1"))

            def product(j):
                dve.wait_ge(gemm_free[0], G_FF1 + 1 + j)
                dve.wait_ge(tile_used, T_FF1 + 16 + 16 * j)
                for t in range(TOK):
                    ins = dve.scalar_tensor_tensor(out=prod_s[:, t, :], in0=ps[:, 2 + t, :], scalar=r_of(rstd, "x1", t, 1),
                                                   in1=gate_s[:, t, :], op0=ALU.mult, op1=ALU.mult)
                ins.then_inc(gemm_free[1], 1)

            aT_hi_flat = aT_hi[:].rearrange("p c s -> p (c s)")
            aT_lo_flat = aT_lo[:].rearrange("p c s -> p (c s)")

            def turn_lo(j):
                for f in range(2):
                    dve.wait_ge(tp_hi, F_FF1 + f + 1 + 2 * j)
                    dve.tensor_tensor(aT_lo_flat[:, bass.ts(2 * j + f, 2 * SEQ)], ps[:, 4 + f, :],
                                      aT_hi_flat[:, bass.ts(2 * j + f, 2 * SEQ)].bitcast(F32),
                                      ALU.subtract).then_inc(tp_free, 1)

            with dve.Fori(1, FB) as j:
                lo_tiles(T_FF1, 16 * j, 0, 3)
                product(j - 1)
                lo_tiles(T_FF1, 16 * j, 3, 7)
                turn_lo(j - 1)
                lo_tiles(T_FF1, 16 * j, 7, 16)
            done[0] = T_DN1
            lo_upto(T_DN1 + 3)
            product(FB - 1)
            lo_upto(T_DN1 + 7)
            turn_lo(FB - 1)
            lo_upto(T_DN1 + 24)
            dve.wait_ge(grow_landed, 32)
            with dve.Fori(1, 4) as n:
                lo_tiles(T_DN1, 24 * n, 0, 3)
                row_scale(4, n - 1, y_dn, grow_dn, None)
                lo_tiles(T_DN1, 24 * n, 3, 24)
            done[0] = T_IN2
            row_scale(4, 3, y_dn, grow_dn, None)
            dve.wait_ge(row_y, 8)
            dve.memset(lrT[:], 1.0).then_inc(consts_ready, 1)
            new_x("dn1", y_dn, T_IN2)

            with_fills(T_IN2, F_XT3, "norm1_g_2")
            dve.wait_ge(sq_done, 5)
            mean_sq("x2", DM)
            lo_upto(T_IN2 + 20)
            dve.wait_ge(gl_act, 2)
            for d in range(2):
                for t in range(TOK):
                    g = gb[:, 0, d, t * NB:(t + 1) * NB]
                    ins = dve.scalar_tensor_tensor(out=g, in0=ps[:, 4 + 2 * d + t, :], scalar=0.0, in1=g,
                                                   op0=ALU.min, op1=ALU.subtract)
            ins.then_inc(gl_dve, 1)
            lo_upto(T_IN2 + 36)
            dd = [gb[:, 0, i, :].rearrange("p (g s) -> p g s", s=CHUNK) for i in range(2)]
            dve.wait_ge(gl_act, 3)
            for d in range(2):
                b = gb[:, 1, d, :].rearrange("p (g s) -> p g s", s=CHUNK)
                ref, last = (CHUNK // 2, CHUNK - 1) if d == 0 else (CHUNK // 2 - 1, 0)
                if d == 1:
                    dve.wait_ge(fac_exp, 2)
                for i, r in enumerate((ref, last)):
                    ins = dve.tensor_tensor(dd[i], b, b[:, :, r:r + 1].to_broadcast([P, GH * NCH, CHUNK]), ALU.subtract)
                ins.then_inc(fac_exp, 1)
                lo_upto(T_IN2 + 39 + 4 * d)
                dve.wait_ge(gl_act, 4)
                dve.wait_ge(fac_exp, 2 * d + 2)
                for i, src in enumerate((qT2, kT2, qT2, kT2)):
                    ins = dve.tensor_tensor(fac[:, d, i], fac[:, d, i], src[:], ALU.mult)
                    if i % 2 == 0:
                        lo_upto(done[0] + 1)
                ins.then_inc(fac_ready, 1)

            def gla_mask(h):
                dve.wait_ge(g_AT, h + 1)
                if h >= 1:
                    dve.wait_ge(g_O, h)
                for d in range(2):
                    ins = dve.copy_predicated(at_sb[:], gmask[:, d, :].unsqueeze(1).to_broadcast([P, TOK, P]),
                                              ps[:, 4, 2 * d * P:2 * (d + 1) * P].rearrange("p (t s) -> p t s", t=TOK))
                    if d == 0:
                        step(ins)
                ins.then_inc(g_at, 1)

            def gla_states(h, d):
                dve.wait_ge(g_SS, 2 * h + d + 1)
                if h >= 1:
                    dve.wait_ge(g_O, h)
                for n in range(3):
                    c = n if d == 0 else 3 - n
                    new = gla_sum(d, c)
                    if n == 0:
                        ins = dve.tensor_copy(state[:, d, 0, :], new)
                    else:
                        ins = dve.scalar_tensor_tensor(out=state[:, d, n, :], in0=state[:, d, n - 1, :],
                                                       scalar=decay[:, d, h * NCH + c:h * NCH + c + 1], in1=new,
                                                       op0=ALU.mult, op1=ALU.add)
                    if n < 2:
                        step(ins)
                ins.then_inc(g_st, 1)

            def gla_out(h):
                dve.wait_ge(g_O, h + 1)
                dve.tensor_copy(z2[:, :, QG + h * DV:QG + (h + 1) * DV], ps[:, 5, :].rearrange("p (t n) -> p t n", t=TOK))\
                   .then_inc(g_o, 1)

            def part_norm(part):
                name, h0, n, _, gain = QK_PARTS[part]
                dve.wait_ge(late_landed, 16 * 7)
                dve.wait_ge(rstd_ready, r_count(name))
                for t in range(TOK):
                    for h in range(n):
                        q = z2[:, t, (h0 + h) * HD:(h0 + h + 1) * HD]
                        ins = dve.scalar_tensor_tensor(out=q, in0=q, scalar=r_of(rstd, name, t * n + h, 1),
                                                       in1=gqk[:, gain, :], op0=ALU.mult, op1=ALU.mult)
                ins.then_inc(qk_normed, 1)

            step(dve.memset(at_sb[:], 0.0))
            for g in range(45, 80):
                h, k = gla_slot(g - 2)
                if k == 0 and 1 <= h <= GH:
                    gla_out(h - 1)
                if k == 0 and 0 <= h < GH:
                    gla_mask(h)
                if k in (2, 4) and 0 <= h < GH:
                    gla_states(h, k // 2 - 1)
                if g == 62:
                    dve.wait_ge(sq_done, 6)
                    mean_sq("k", HD)
                if g == 63:
                    part_norm(0)
                if g == 70:
                    dve.wait_ge(sq_done, 7)
                    mean_sq("qa", HD)
                if g == 71:
                    part_norm(1)
                if g == 74:
                    dve.wait_ge(sq_done, 8)
                    mean_sq("gla", DV)
                if g == 75:
                    dve.wait_ge(rstd_ready, r_count("gla"))
                if g in (75, 76):
                    for h in range(2 * (g - 75), 2 * (g - 75) + 2):
                        for t in range(TOK):
                            o = z2[:, t, QG + h * DV:QG + (h + 1) * DV]
                            ins = dve.scalar_tensor_tensor(out=o, in0=o, scalar=r_of(rstd, "gla", t * GH + h, 1),
                                                           in1=gla_g[:], op0=ALU.mult, op1=ALU.mult)
                    step(ins)
                if g in (77, 78):
                    dve.wait_ge(gate2_ready, 1)
                    for h in range(2 * (g - 77), 2 * (g - 77) + 2):
                        o = z2[:, :, QG + h * DV:QG + (h + 1) * DV]
                        dve.tensor_tensor(o, o, z2[:, :, GG + h * DV:GG + (h + 1) * DV], ALU.mult).then_inc(mix2_ready, 1)
                lo_upto(T_IN2 + g + 1)

            def split_rest(F, pair_at, bank):
                dve.wait_ge(tp_hi, F + 1)
                dve.tensor_tensor(hT_lo[:, 2 * pair_at:2 * pair_at + 2, :], ps[:, bank, :].rearrange("p (c s) -> p c s", c=2),
                                  hT_hi[:, 2 * pair_at:2 * pair_at + 2, :].bitcast(F32), ALU.subtract).then_inc(tp_free, 1)

            def half_add(end, b, sem_done):
                dve.wait_ge(tile_used, end)
                x = x_sb[:, :, cols(b)]
                p = 2 * (b % 2)
                dve.tensor_tensor(x, ps[:, p:p + 2, :], x, ALU.add).then_inc(sem_done, 1)

            for g in range(32):
                if 0 <= g - 2 - (MIX_FILL - 80) < 4:
                    n = g - 2 - (MIX_FILL - 80)
                    split_rest(F_MIX2 + n, 4 + n, 4 + (F_MIX2 + n) % 4)
                i = (g - 3) // 2
                if g % 2 == 1 and 0 <= i < HEADS:
                    e, h = i % 2, HEAD_ORDER[i]
                    dve.wait_ge(at_S, HEADS + i + 1)
                    if i >= 2:
                        dve.wait_ge(at_out, HEADS + i - 1)
                    step(dve.tensor_tensor(ps[:, 5, P:3 * P], ps[:, 5, P:3 * P], mask2[:, P:3 * P], ALU.add))
                    step(dve.tensor_reduce(amax[:, e, :, 0:1], ps[:, 5, :].rearrange("p (t s) -> p t s", t=TOK), X, ALU.max))
                    step(dve.tensor_scalar(amax[:, e, :, 1:2], amax[:, e, :, 0:1], float(HD) ** -0.5, sinkb[:, h:h + 1],
                                           ALU.mult, ALU.max))
                    dve.tensor_scalar(amax[:, e, :, 2:3], amax[:, e, :, 1:2], -1.0, None, ALU.mult).then_inc(at_max, 1)
                i = (g - 4) // 2
                if g % 2 == 0 and 0 <= i < HEADS:
                    e = i % 2
                    dve.wait_ge(at_exp, HEADS + i + 1)
                    step(dve.tensor_tensor(asum[:, e, 1, :], asum[:, e, 0, :], amax[:, e, :, 3], ALU.add))
                    dve.reciprocal(asum[:, e, 1, :], asum[:, e, 1, :]).then_inc(at_sum, 1)
                if g == 6:
                    dve.wait_ge(sq_done, 9)
                    mean_sq("qb", HD)
                if g == 7:
                    part_norm(2)
                if g % 4 == 1 and 0 <= (g - 9) // 4 < 4:
                    p = (g - 9) // 4
                    split_rest(F_MIX2 + 4 + p, PAIR_ORDER[p], 4)
                if g % 4 == 2 and 1 <= g // 4 <= 4:
                    half_add(T_OUT2 + 4 * (g // 4), g // 4 - 1, half_added)
                if g == 24:
                    half_add(T_OUT2 + 23, 0, x_new)
                if g == 26:
                    half_add(T_OUT2 + 24, 1, x_new)
                if g == 30:
                    half_add(T_OUT2 + 28, 2, x_new)
                lo_upto(T_OUT2 + g + 1)
            half_add(T_OUT2 + 32, 3, x_new)

            def row_add(c_end, step_, n, sem_done):
                dve.wait_ge(tile_used, c_end + step_)
                for t in range(TOK):
                    ins = dve.tensor_tensor(x_sb[:, t, cols(n)], ps_flat[:, bass.ts(2 * n + t, NB)], x_sb[:, t, cols(n)],
                                            ALU.add)
                ins.then_inc(sem_done, 1)

            with_fills(T_FF2, F_XT4, "norm2_g_2")
            dve.wait_ge(sq_done, 10)
            mean_sq("x3", DM)
            lo_upto(T_FF2 + 16)

            def taps2(j, half):
                dst = cg if half == 0 else cval
                n = 0
                for f in range(2):
                    dve.wait_ge(ct_center, 4 * j + 2 * half + f + 1)
                    for c in range(2 * f, 2 * f + 2):
                        k = 4 * j + c + FC * half
                        src = ps[:, 4 + 2 * half + f, (c % 2) * SEQ:(c % 2 + 1) * SEQ]
                        ins = dve.scalar_tensor_tensor(out=dst[:, c, 1:SEQ], in0=src[:, 0:SEQ - 1],
                                                       scalar=conv2[:, 0, bass.ts(k, 1)], in1=dst[:, c, 1:SEQ],
                                                       op0=ALU.mult, op1=ALU.add)
                        ins.then_inc(conv2_step, 1)
                    for c in range(2 * f, 2 * f + 2):
                        k = 4 * j + c + FC * half
                        src = ps[:, 4 + 2 * half + f, (c % 2) * SEQ:(c % 2 + 1) * SEQ]
                        dve.wait_ge(conv2_step, 8 * j + 4 * half + c + 1)
                        ins = dve.scalar_tensor_tensor(out=dst[:, c, 0:SEQ - 1], in0=src[:, 1:SEQ],
                                                       scalar=conv2[:, 2, bass.ts(k, 1)], in1=dst[:, c, 0:SEQ - 1],
                                                       op0=ALU.mult, op1=ALU.add)
                ins.then_inc(ct_free, 1)

            def product2(j):
                dve.wait_ge(cg_silu, j + 1)
                dve.wait_ge(ct_free, 2 * j + 2)
                dve.tensor_tensor(cg[:], cg[:], cval[:], ALU.mult).then_inc(prod_ready, 1)

            def hidden_lo(j):
                dve.wait_ge(aT_hi_ready, j + 1)
                dve.tensor_tensor(aT_lo_flat[:, bass.ts(j, 4 * SEQ)], cg[:].rearrange("p c s -> p (c s)"),
                                  aT_hi_flat[:, bass.ts(j, 4 * SEQ)].bitcast(F32), ALU.subtract).then_inc(aT_ready, 1)

            taps2(0, 0)
            with dve.Fori(1, FB) as j:
                lo_tiles(T_FF2, 16 * j, 0, 8)
                taps2(j - 1, 1)
                product2(j - 1)
                lo_tiles(T_FF2, 16 * j, 8, 12)
                hidden_lo(j - 1)
                lo_tiles(T_FF2, 16 * j, 12, 16)
                taps2(j, 0)
            done[0] = T_DN2
            lo_upto(T_DN2 + 8)
            taps2(FB - 1, 1)
            product2(FB - 1)
            lo_upto(T_DN2 + 12)
            hidden_lo(FB - 1)
            lo_upto(T_DN2 + 24)
            with dve.Fori(1, 4) as n:
                lo_tiles(T_DN2, 24 * n, 0, 3)
                row_add(T_DN2, 24 * n, n - 1, row_y)
                lo_tiles(T_DN2, 24 * n, 3, 24)
            row_add(T_END, 0, 3, row_y)


_INS = ["x", "positions", "pre_mix_norm", "w_in", "q_norm", "w_uq", "kv_norm", "w_ukv", "conv_w", "conv_b",
        "conv_ln_g", "conv_ln_b", "conv_out_norm", "attn_out_norm", "w_out", "post_mix_norm", "pre_ffn_norm",
        "w_gate", "w_up", "w_down", "post_ffn_norm", "norm1_g_2", "w_in_2", "attn_q_norm_g_2",
        "attn_k_norm_g_2", "attn_sink_2", "gla_wa2_fwd_2", "gla_ba_fwd_2", "gla_wa2_bwd_2", "gla_ba_bwd_2",
        "gla_out_norm_g_2", "w_out_2", "norm2_g_2", "w_up_2", "conv_w_2", "conv_b_2", "w_down_2"]


def inverse_frequencies():
    f = np.float32
    one = f(THETA) ** (-np.arange(0, ROPE, 2, dtype=f) / f(ROPE))
    two = f(1.0) / (f(THETA) ** (np.arange(HD // 2, dtype=f) / f(HD // 2)))
    return np.concatenate([one, two]).astype(f)[None, :]


def kernel(**inputs):
    import concourse.bacc as _bacc
    from concourse.bass_utils import run_bass_kernel_spmd as _run

    nc = _bacc.Bacc("TRN2", target_bir_lowering=False, num_devices=1)
    arrays = {f"in_{name}": np.ascontiguousarray(inputs[name]) for name in _INS}
    arrays["in_inv_freq"] = inverse_frequencies()
    aps = {name[3:]: nc.dram_tensor(name, v.shape, mybir.dt.from_np(v.dtype), kind="ExternalInput").ap()
           for name, v in arrays.items()}
    out = nc.dram_tensor("out_0", (1, SEQ, DM), F32, kind="ExternalOutput").ap()
    build(nc, aps, out)
    r = _run(nc, [arrays], core_ids=[0])
    return r.results[0]["out_0"]
```

```python
from contextlib import ExitStack

import numpy as np

import concourse.bass as bass
from concourse import mybir

F32 = mybir.dt.float32
F32R = mybir.dt.float32r
I32 = mybir.dt.int32
ALU = mybir.AluOpType
ACT = mybir.ActivationFunctionType
X = mybir.AxisListType.X

P = 128
SEQ = 256
TOK = SEQ // P
DM = 2048
KD = DM // P
NB = 512
EPS = 1e-6
RING = 4
MASKED = -3.0e38

CONV = 1024
CC = CONV // P
TAPS = 31
CONV_DVE = ([0, 1], [4, 5, 6])
CONV_POOL = ([2, 3], [7])
TILE_TAPS, ATTN_TAPS = 3, 4
DVE_TAPS = TAPS * sum(len(c) for c in CONV_DVE)
HEADS = 8
NOPE, ROPE, VD = 128, 64, 128
QKH = NOPE + ROPE
QL, KVL = 768, 512
QC, KVC = QL // P, KVL // P
Z1 = QL + KVL + ROPE
DFF = 5632
FC = DFF // P
FB = DFF // NB
THETA = 10000.0

HD = 128
KVH = 2
GH, DK, DV, RANK, CHUNK = 4, 128, 256, 16, 64
NCH = SEQ // CHUNK
Z2 = 4640
W2 = Z2 // 10
QA, KA, VA, QG, KG, VG, GG, LR = 0, 1024, 1280, 1536, 2048, 2560, 3584, 4608
B2_ORDER = [9, 3, 4, 5, 6, 7, 2, 1, 8, 0]
NORM_WARM = 20
GLA0, GLA_STEP = 51, 5
MIX_FILL = 78
HEAD_ORDER = [4, 5, 6, 7, 0, 1, 2, 3]
PAIR_ORDER = [2, 3, 0, 1]
OUT2_TILES = ([(2, i) for i in range(3)] + [(3, i) for i in range(3)] + [(2, 3), (3, 3)]
              + [(0, i) for i in range(4)] + [(1, i) for i in range(4)])
XT4_ORDER = [4, 5, 6, 7, 0, 1, 2, 3]

SHAPES = []


def _phase(blocks, tiles, width):
    start = len(SHAPES)
    SHAPES.extend([(kc, width(b)) for b in range(blocks) for kc in tiles])
    return start


IN1_COLS = [(0, 512), (1024, 512), (512, 512), (1536, 512), (2048, 448), (2496, 448), (2944, 448)]
T_IN1 = _phase(7, [2] * 8, lambda b: IN1_COLS[b][1])
T_UQ = _phase(3, [2] * 3, lambda b: NB)
T_UKV = _phase(4, [2] * 2, lambda b: NB)
T_OUT1 = _phase(8, [2] * 4, lambda b: NB)
T_FF1 = _phase(2 * FB, [2] * 8, lambda b: NB)
DN_TILES = [2] * 20 + [1] * 4
T_DN1 = _phase(4, DN_TILES, lambda b: NB)
T_IN2 = _phase(10, [2] * 8, lambda b: W2)
T_OUT2 = _phase(8, [2] * 4, lambda b: NB)
T_FF2 = _phase(2 * FB, [2] * 8, lambda b: NB)
T_DN2 = _phase(4, DN_TILES, lambda b: NB)
T_END = len(SHAPES)

G_FF1 = 9
G_IN2 = G_FF1 + FB
G_FF2 = G_IN2 + 5

F_XT1, F_LAT, F_MIX1, F_XT2, F_FF1 = 0, 8, 13, 17, 25
F_XT3 = F_FF1 + 2 * FB
F_MIX2, F_XT4 = F_XT3 + 8, F_XT3 + 16

GAINS = [("pre_mix_norm", KD), ("q_norm", QC), ("kv_norm", KVC), ("conv_b", CC), ("conv_ln_g", CC),
         ("conv_ln_b", CC), ("conv_out_norm", CC), ("attn_out_norm", CC), ("pre_ffn_norm", KD),
         ("norm1_g_2", KD), ("norm2_g_2", KD)]
G_AT, _n = {}, 0
for _name, _k in GAINS:
    G_AT[_name] = _n
    _n += _k
G_ROWS = _n
SMALL = len(GAINS) - 1 + 9


def build(nc, a, out):
    ctx = ExitStack()
    with ctx:
        def sb(name, shape, dt=F32):
            return ctx.enter_context(nc.sbuf_tensor(name, shape, dt))

        def overlay(tensors):
            inner = ExitStack()
            got = [inner.enter_context(nc.sbuf_tensor(n, s, d)) for n, s, d in tensors]
            inner.close()
            return got

        def sem(name):
            return ctx.enter_context(nc.semaphore(name))

        x_sb = sb("x_sb", [P, TOK, DM])
        raw = sb("raw", [P, RING, 2, NB])
        w_hi = sb("w_hi", [P, RING, 2, NB], F32R)
        w_lo = sb("w_lo", [P, RING, 2, NB], F32R)
        ident = sb("ident", [P, P])
        ones = sb("ones", [P, P])
        gains = sb("gains", [P, G_ROWS])
        convw = sb("convw", [P, TAPS * CC])
        conv2 = sb("conv2", [P, 4, 2 * FC])
        masks = sb("masks", [P, 5 * P])
        mask1 = masks[:, 0:3 * P]
        mask2 = masks[:, P:5 * P]
        tri = sb("tri", [P, 2, P])
        gmask = sb("gmask", [P, 2, P], I32)
        posf = sb("posf", [P, 2, TOK])
        trig = sb("trig", [P, TOK, 2, 96])
        invf = sb("invf", [P, 96])
        ss = sb("ss", [P, 64])
        ms = sb("ms", [P, 64])
        rstd = sb("rstd", [P, 64])
        minus_half = sb("minus_half", [P, 20])
        amax = sb("amax", [P, 2, 2, 4])
        asum = sb("asum", [P, 2, 2, 2])
        sinkb = sb("sinkb", [P, HEADS])
        decay = sb("decay", [P, 2, GH * NCH])
        y_dn, _, grow_dn = overlay([("y_dn", [P, TOK * DM], F32), ("under_grow", [P, DM], F32), ("grow_dn", [P, DM], F32)])
        hT_hi = sb("hT_hi", [P, KD, SEQ], F32R)
        hT_lo = sb("hT_lo", [P, KD, SEQ], F32R)
        z1, uT, cv, q1, kv1, attn1, qkT, qpeT, att1_s, att1_p, kpe, kpeT = overlay([
            ("z1", [P, TOK, Z1], F32), ("uT", [P, CC, SEQ + TAPS - 1], F32), ("cv", [P, CC, SEQ], F32),
            ("q1", [P, TOK, HEADS * QKH], F32), ("kv1", [P, TOK, DM], F32), ("attn1", [P, TOK, CONV], F32),
            ("qkT", [P, 2, 2, SEQ], F32), ("qpeT", [ROPE, 2, SEQ], F32), ("att1_s", [P, 2, 3 * P], F32),
            ("att1_p", [P, 2, 3 * P], F32), ("kpe", [P, TOK, ROPE], F32), ("kpeT", [ROPE, SEQ], F32)])
        taken = sum([TOK * Z1, CC * (SEQ + TAPS - 1), CC * SEQ, TOK * HEADS * QKH, TOK * DM, TOK * CONV,
                     4 * SEQ, 2 * SEQ, 6 * P, 6 * P, TOK * ROPE, SEQ])
        _, latT_hi, latT_lo = overlay([("under_lat", [P, taken], F32),
                                       ("latT_hi", [P, QC + KVC, SEQ], F32R), ("latT_lo", [P, QC + KVC, SEQ], F32R)])
        _, lnsq = overlay([("under_ln", [P, taken], F32), ("lnsq", [P, CC, SEQ], F32)])
        taken += 2 * (QC + KVC) * SEQ
        _, tap_prod = overlay([("under_tap", [P, taken], F32), ("tap_prod", [P, 2, SEQ], F32)])
        taken = TOK * Z1 + CC * (SEQ + TAPS - 1) + CC * SEQ
        _, grow_out = overlay([("under_gout", [P, taken], F32), ("grow_out", [P, DM], F32)])
        taken += TOK * HEADS * QKH
        _, y_out = overlay([("under_y", [P, taken], F32), ("y_out", [P, TOK * DM], F32)])
        z2, gb, qT2, kT2, fac, kaT, gqk, gla_g, at_sb = overlay([
            ("z2", [P, TOK, Z2], F32), ("gb", [P, 2, 2, 2 * NB], F32), ("qT2", [P, GH, SEQ], F32),
            ("kT2", [P, GH, SEQ], F32), ("fac", [P, 2, 4, GH, SEQ], F32), ("kaT", [P, KVH, SEQ], F32),
            ("gqk", [P, 2, HD], F32), ("gla_g", [P, DV], F32), ("at_sb", [P, TOK, P], F32)])
        taken = TOK * Z2 + 8 * NB
        _, state, ktok = overlay([("under_st", [P, taken], F32), ("state", [P, 2, 3, DV], F32), ("ktok", [P, 2, TOK, P], F32)])
        taken += 2 * GH * SEQ
        _, att2_q, att2_s, att2_p = overlay([
            ("under_at", [P, taken], F32), ("att2_q", [P, 2, 2, SEQ], F32), ("att2_s", [P, 2, TOK, SEQ], F32),
            ("att2_p", [P, 2, 4, P], F32)])
        taken = TOK * Z2 + 8 * NB + 2 * GH * SEQ + 6 * GH * SEQ
        _, lrT, wa2 = overlay([("under_lr", [P, taken], F32), ("lrT", [RANK + 1, 2, SEQ], F32),
                               ("wa2", [RANK + 1, 2, NB], F32)])
        rows, = overlay([("rows", [P, 8, P], F32)])
        trig_t, = overlay([("under_trig", [P, 8 * P], F32), ("trig_t", [P, 4, TOK * 96], F32)])[1:]
        aT_hi = sb("aT_hi", [P, FC, SEQ], F32R)
        aT_lo = sb("aT_lo", [P, FC, SEQ], F32R)
        stage = sb("stage", [P, 3, 4, SEQ])
        ps = ctx.enter_context(nc.psum_tensor("ps", [P, 8, NB], F32))

        gate_s = stage[:, 0].rearrange("p c s -> p (c s)").rearrange("p (t n) -> p t n", t=TOK)
        prod_s = stage[:, 1].rearrange("p c s -> p (c s)").rearrange("p (t n) -> p t n", t=TOK)
        raw_s = gate_s
        cg, cval = stage[:, 1], stage[:, 2]
        a_s = attn1[:, :, 0:NB]
        sg_s = attn1[:, :, NB:2 * NB]

        raw_landed = [sem(f"raw_landed{s}") for s in range(RING)]
        hi_ready, lo_ready, tile_used = sem("hi_ready"), sem("lo_ready"), sem("tile_used")
        gemm_free = [sem("gemm_free0"), sem("gemm_free1")]
        tp_ready, tp_hi, tp_free = sem("tp_ready"), sem("tp_hi"), sem("tp_free")
        x_landed = [sem(f"x_landed{n}") for n in range(4)]
        params_landed, late_landed, grow_landed, out_landed = (
            sem("params_landed"), sem("late_landed"), sem("grow_landed"), sem("out_landed"))
        rows_landed = sem("rows_landed")
        ident_ready, consts_ready, masks_ready = sem("ident_ready"), sem("consts_ready"), sem("masks_ready")
        rows_T, gains_ready = sem("rows_T"), sem("gains_ready")
        dve_step, act_step, pool_step = sem("dve_step"), sem("act_step"), sem("pool_step")
        ms_ready, rstd_ready, sq_done = sem("ms_ready"), sem("rstd_ready"), sem("sq_done")
        u_ready, cu_ready, cu_free = sem("u_ready"), sem("cu_ready"), sem("cu_free")
        conv_tap, pool_mul, pool_add = sem("conv_tap"), sem("pool_mul"), sem("pool_add")
        trig_arg, trig_abs, trig_done = sem("trig_arg"), sem("trig_abs"), sem("trig_done")
        at_T, at_qk, at_S, at_max, at_exp, at_PT, at_pT, at_PV, at_out = (
            sem("at_T"), sem("at_qk"), sem("at_S"), sem("at_max"), sem("at_exp"), sem("at_PT"), sem("at_pT"),
            sem("at_PV"), sem("at_out"))
        rope_ready, kpe_ready = sem("rope_ready"), sem("kpe_ready")
        ln_mm, ln_dve, ln_act = sem("ln_mm"), sem("ln_dve"), sem("ln_act")
        mix_conv, conv_hi, y_ready = sem("mix_conv"), sem("conv_hi"), sem("y_ready")
        row_sq, row_y, x_new = sem("row_sq"), sem("row_y"), sem("x_new")
        ct_ready, ct_center, ct_free, cg_silu, prod_ready, aT_hi_ready, aT_ready, conv2_step = (
            sem("ct_ready"), sem("ct_center"), sem("ct_free"), sem("cg_silu"), sem("prod_ready"),
            sem("aT_hi_ready"), sem("aT_ready"), sem("conv2_step"))
        gl_mm, gl_act, gl_dve = sem("gl_mm"), sem("gl_act"), sem("gl_dve")
        fac_diff, fac_exp, fac_ready = sem("fac_diff"), sem("fac_exp"), sem("fac_ready")
        g_AT, g_at, g_KT, g_kt, g_SS, g_st, g_O, g_o = (
            sem("g_AT"), sem("g_at"), sem("g_KT"), sem("g_kt"), sem("g_SS"), sem("g_st"), sem("g_O"), sem("g_o"))
        mix2_ready, gate2_ready = sem("mix2_ready"), sem("gate2_ready")
        qk_normed, at_sum, half_added = sem("qk_normed"), sem("at_sum"), sem("half_added")

        def chunks(w):
            return w[0].rearrange("(c p) n -> p c n", p=P)

        w_in, w_uq, w_ukv, w_out = chunks(a["w_in"]), chunks(a["w_uq"]), chunks(a["w_ukv"]), chunks(a["w_out"])
        w_gate, w_up, w_down = chunks(a["w_gate"]), chunks(a["w_up"]), chunks(a["w_down"])
        w_in2, w_out2, w_up2, w_down2 = (chunks(a["w_in_2"]), chunks(a["w_out_2"]), chunks(a["w_up_2"]),
                                         chunks(a["w_down_2"]))

        def landed(c0, step):
            return 16 * (c0 // RING + 1) + (16 // RING) * step

        def cols(n, w=NB):
            return bass.ts(n, w)

        def in_sbuf(eng, B, base=0):
            eng.wait_ge(gemm_free[B % 2], base + B // 2 + 1)

        def last_of(b, d):
            return b.rearrange("p h (c s) -> p (h c) s", s=CHUNK)[:, :, CHUNK - 1 if d == 0 else 0]

        def gla_sum(d, c):
            bank = 6 + c % 2
            i = {(0, 0): 0, (0, 2): 1, (0, 1): 0, (1, 3): 0, (1, 1): 1, (1, 2): 0}[d, c]
            return ps[:, bank, i * DV:(i + 1) * DV]

        def gla_slot(g):
            return divmod(g - GLA0, GLA_STEP)

        QK_PARTS = [("k", 8, 2, 6, 1), ("qa", 4, 4, 7, 0), ("qb", 0, 2, 9, 0), ("qc", 2, 2, 9, 0)]

        gb_flat = gb[:].rearrange("p a d n -> p (a d n)")
        ps_flat = ps[:].rearrange("p b n -> p (b n)")
        ss4 = ss[:, 56:64]

        block = ctx.enter_context(nc.Block())

        @block.sync
        def _(sp):
            x_in = a["x"][0].rearrange("(t p) n -> p t n", p=P)

            def small_loads():
                n = 0
                for name, k in GAINS[1:]:
                    sp.dma_start(rows[n:n + k, 0, :], a[name].rearrange("o (c p) -> (o c) p", p=P)).then_inc(params_landed, 16)
                    n += k
                taps = a["conv_w"][0].rearrange("k (c p) -> (k c) p", p=P)
                sp.dma_start(rows[:, 1, :], taps[0:P, :]).then_inc(params_landed, 16)
                sp.dma_start(rows[0:TAPS * CC - P, 2, :], taps[P:TAPS * CC, :]).then_inc(params_landed, 16)
                for k in range(3):
                    sp.dma_start(rows[0:2 * FC, 3 + k, :], a["conv_w_2"][0, k:k + 1, :].rearrange("o (c p) -> (o c) p", p=P))\
                      .then_inc(params_landed, 16)
                sp.dma_start(rows[0:2 * FC, 6, :], a["conv_b_2"].rearrange("o (c p) -> (o c) p", p=P)).then_inc(params_landed, 16)
                sp.dma_start(invf[:], a["inv_freq"].to_broadcast([P, 96])).then_inc(params_landed, 16)
                sp.dma_start(kpe[:, 0, 0:TOK].bitcast(I32), a["positions"].rearrange("o (t p) -> p (o t)", p=P),
                             allow_slow_non_contiguous=True).then_inc(params_landed, 16)
                sp.dma_start(sinkb[:], a["attn_sink_2"].to_broadcast([P, HEADS])).then_inc(params_landed, 16)

            def load(c0, step, w, k0, at):
                kc, width = SHAPES[c0]
                s = c0 % RING
                if c0 >= RING:
                    sp.wait_ge(lo_ready, c0 - RING + 1 + step)
                sp.dma_start(raw[:, s, :kc, :width], w[:, k0:k0 + kc, at]).then_inc(raw_landed[s], 16)

            def load_block(c0, step, w, tiles, at):
                k0 = 0
                for n, kc in enumerate(tiles):
                    load(c0 + n, step, w, k0, at)
                    k0 += kc

            def rows_phase(c0, w, tiles):
                T = len(tiles)
                load_block(c0, 0, w, tiles, cols(0))
                with sp.Fori(1, 4) as n:
                    load_block(c0, n * T, w, tiles, cols(n))

            for n in range(4):
                sp.dma_start(x_sb[:, :, cols(n)], x_in[:, :, cols(n)]).then_inc(x_landed[n], 16)
                load(T_IN1 + n, 0, w_in, 2 * n, slice(0, NB))
            small_loads()
            for n in range(RING, 8):
                load(T_IN1 + n, 0, w_in, 2 * n, slice(0, NB))
            for b, (n0, width) in enumerate(IN1_COLS):
                if b > 0:
                    load_block(T_IN1 + 8 * b, 0, w_in, [2] * 8, slice(n0, n0 + width))
            for b in range(3):
                load_block(T_UQ + 3 * b, 0, w_uq, [2] * 3, cols(b))
            for b in range(4):
                load_block(T_UKV + 2 * b, 0, w_ukv, [2] * 2, cols(b))
            for half in range(2):
                for n in range(4):
                    for i in range(4):
                        load(T_OUT1 + 16 * half + 4 * n + i, 0, w_out, CC * (1 - half) + 2 * i, cols(n))
                    if half == 0 and n == 1:
                        sp.wait_ge(at_T, HEADS)
                        sp.dma_start(grow_out[:], a["post_mix_norm"].to_broadcast([P, DM])).then_inc(grow_landed, 16)

            def ff1(j):
                load_block(T_FF1, 16 * j, w_gate, [2] * 8, cols(j))
                load_block(T_FF1 + 8, 16 * j, w_up, [2] * 8, cols(j))
            with sp.Fori(0, FB) as j:
                ff1(j)
            rows_phase(T_DN1, w_down, DN_TILES)
            for b, n in enumerate(B2_ORDER):
                load_block(T_IN2 + 8 * b, 0, w_in2, [2] * 8, slice(n * W2, (n + 1) * W2))
                if b == 0:
                    sp.wait_ge(row_y, 8)
                    for i, name in enumerate(("attn_q_norm_g_2", "attn_k_norm_g_2")):
                        sp.dma_start(gqk[:, i, :], a[name].to_broadcast([P, HD])).then_inc(late_landed, 16)
                    sp.dma_start(gla_g[:], a["gla_out_norm_g_2"].to_broadcast([P, DV])).then_inc(late_landed, 16)
                    for d, name in enumerate(("fwd", "bwd")):
                        sp.dma_start(wa2[0:RANK, d, :], a[f"gla_wa2_{name}_2"][0]).then_inc(late_landed, 16)
                        sp.dma_start(wa2[RANK:RANK + 1, d, :], a[f"gla_ba_{name}_2"]).then_inc(late_landed, 16)
            for g in range(16):
                load(T_OUT2 + g, 0, w_out2, CC + 2 * (g % 4), cols(g // 4))
            for g, (b, i) in enumerate(OUT2_TILES):
                load(T_OUT2 + 16 + g, 0, w_out2, 2 * PAIR_ORDER[i], cols(b))
            for n in range(8):
                load(T_FF2 + n, 0, w_up2, 2 * XT4_ORDER[n], cols(0))
            load_block(T_FF2 + 8, 0, w_up2, [2] * 8, cols(FB))
            with sp.Fori(1, FB) as j:
                load_block(T_FF2, 16 * j, w_up2, [2] * 8, cols(j))
                load_block(T_FF2 + 8, 16 * j, w_up2, [2] * 8, cols(j + FB))
            rows_phase(T_DN2, w_down2, DN_TILES)
            for n in range(4):
                sp.wait_ge(row_y, 9 + n)
                sp.dma_start(out[0, :, cols(n)].rearrange("(t p) n -> p t n", p=P), x_sb[:, :, cols(n)])\
                  .then_inc(out_landed, 16)
            sp.wait_ge(out_landed, 16 * 4)

        R = {}
        at = 0
        for name, n in [("x0", 2), ("lat", 4), ("ln", 2), ("conv", 2), ("attn", 2), ("out1", 2), ("x1", 2),
                        ("dn1", 2), ("x2", 2), ("k", 4), ("qa", 8), ("gla", 8), ("qb", 4), ("qc", 4), ("x3", 2)]:
            R[name] = (at, n)
            at += n
        R_ORDER = ["x0", "lat", "attn", "ln", "conv", "out1", "x1", "dn1", "x2", "k", "qa", "gla", "qb", "qc", "x3"]

        def r_count(name):
            return R_ORDER.index(name) + 1

        def r_of(tensor, name, lo=0, n=None):
            at, k = R[name]
            return tensor[:, at + lo:at + lo + (k - lo if n is None else n)]

        @block.gpsimd
        def _(pool):
            count = [0]

            def step(ins):
                count[0] += 1
                ins.then_inc(pool_step, 1)
                pool.wait_ge(pool_step, count[0])

            step(pool.memset(ident[:], 0.0))
            pool.affine_select(out=ident[:], in_=ident[:], compare_op=ALU.not_equal, fill=1.0, base=0,
                               pattern=[[-1, P]], channel_multiplier=1).then_inc(ident_ready, 1)
            step(pool.memset(masks[:], 0.0))
            step(pool.memset(tri[:], 1.0))
            for at, sign in ((0, 1), (2 * P, 1), (3 * P, -1)):
                step(pool.affine_select(out=masks[:, at:at + P], in_=masks[:, at:at + P], compare_op=ALU.is_ge,
                                        fill=MASKED, base=0, pattern=[[-sign, P]], channel_multiplier=sign))
            for d, (m, c) in enumerate([(-1, 1), (1, -1)]):
                step(pool.affine_select(out=tri[:, d, :], in_=tri[:, d, :], compare_op=ALU.is_ge, fill=0.0,
                                        base=0, pattern=[[c, P]], channel_multiplier=m))
                step(pool.affine_select(out=tri[:, d, 0:CHUNK], in_=tri[:, d, 0:CHUNK], compare_op=ALU.is_ge,
                                        fill=0.0, base=CHUNK - 1, pattern=[[0, CHUNK]], channel_multiplier=-1))
                step(pool.affine_select(out=tri[:, d, CHUNK:P], in_=tri[:, d, CHUNK:P], compare_op=ALU.is_ge,
                                        fill=0.0, base=-CHUNK, pattern=[[0, CHUNK]], channel_multiplier=1))
            step(pool.tensor_copy(gmask[:], tri[:]))
            step(pool.affine_select(out=gmask[:, 1, :], in_=gmask[:, 1, :], compare_op=ALU.is_gt, fill=0.0,
                                    base=0, pattern=[[-1, P]], channel_multiplier=1))
            pool.iota(posf[:, 1, :], pattern=[[P, TOK]], base=0, channel_multiplier=1,
                      allow_small_or_imprecise_dtypes=True).then_inc(masks_ready, 1)

            def pool_conv(g):
                c, k, base = CONV_POOL[g][0], len(CONV_POOL[g]), (TAPS - 1) * g
                acc, prod = cv[:, c:c + k, :], tap_prod[:, 0:k, :]

                def tap(out, j):
                    w = convw[:, bass.ds(j * CC + c, k)].unsqueeze(2).to_broadcast([P, k, SEQ])
                    return pool.tensor_tensor(out, uT[:, c:c + k, bass.ds(j, SEQ)], w, ALU.mult)

                pool.wait_ge(gains_ready, 3)
                pool.wait_ge(cu_free, 2 * g + 2)
                step(tap(acc, 0))
                at = G_AT["conv_b"] + c
                bias = gains[:, at:at + k].unsqueeze(2).to_broadcast([P, k, SEQ])
                step(pool.tensor_tensor(acc, acc, bias, ALU.add))
                with pool.Fori(0, (TAPS - 1) // 6) as r:
                    for i in range(1, 7):
                        tap(prod, 6 * r + i).then_inc(pool_mul, 1)
                        pool.wait_ge(pool_mul, base + 6 * r + i)
                        pool.tensor_tensor(acc, acc, prod, ALU.add).then_inc(pool_add, 1)
                        pool.wait_ge(pool_add, base + 6 * r + i)


            def rotate(part):
                _, h0, n, _, _ = QK_PARTS[part]
                half = HD // 2
                qk = z2[:, :, h0 * HD:(h0 + n) * HD].rearrange("p t (h n) -> p t h n", n=HD)
                x1, x2 = qk[:, :, :, 0:half], qk[:, :, :, half:HD]
                cos, sin = (trig[:, :, i, 32:96].unsqueeze(2).to_broadcast([P, TOK, n, half]) for i in range(2))
                r1, r2, r3, r4 = (gb_flat[:, 1536 + 512 * i:1536 + 512 * i + TOK * n * half]
                                  .rearrange("p (t h n) -> p t h n", t=TOK, n=half) for i in range(4))
                pool.wait_ge(trig_done, 1)
                pool.wait_ge(qk_normed, part + 1)
                pool.tensor_tensor(r1, x1, sin, ALU.mult)
                pool.tensor_tensor(r2, x2, sin, ALU.mult)
                pool.tensor_tensor(r3, x1, cos, ALU.mult)
                step(pool.tensor_tensor(r4, x2, cos, ALU.mult))
                pool.tensor_tensor(x1, r3, r2, ALU.subtract)
                pool.tensor_tensor(x2, r4, r1, ALU.add).then_inc(rope_ready, 1)
                pool.wait_ge(rope_ready, part + 2)

            pool.wait_ge(consts_ready, 2)
            for n, name in enumerate(R_ORDER):
                pool.wait_ge(ms_ready, n + 1)
                k = R[name][1]
                pool.tensor_tensor(r_of(rstd, name), r_of(ms, name), minus_half[:, 0:k],
                                   ALU.pow).then_inc(rstd_ready, 1)
                if name in ("x0", "lat"):
                    pool_conv(0 if name == "x0" else 1)
                if name in ("k", "qa", "qb", "qc"):
                    rotate([q[0] for q in QK_PARTS].index(name))

        @block.tensor
        def _(pe):
            def gemm_tile(c0, step, A, k0, banks, start, stop):
                kc, width = SHAPES[c0]
                s = c0 % RING
                pe.wait_ge(lo_ready, c0 + 1 + step)
                for k in range(kc):
                    for t in range(TOK):
                        o = banks(t, width)
                        first, last = start and k == 0, stop and k == kc - 1
                        xh, xl = A[0][:, k0 + k, t * P:(t + 1) * P], A[1][:, k0 + k, t * P:(t + 1) * P]
                        wh, wl = w_hi[:, s, k, :width], w_lo[:, s, k, :width]
                        pe.matmul(o, xh, wh, start=first, stop=False)
                        pe.matmul(o, xh, wl, start=False, stop=False)
                        mm = pe.matmul(o, xl, wh, start=False, stop=last)
                mm.then_inc(tile_used, 1)

            def pair(p):
                return lambda t, width: ps[:, 2 * p + t, :width]

            H = (hT_hi, hT_lo)

            def fill(F, src, n, wait=None):
                if F >= 4:
                    pe.wait_ge(tp_free, F - 3)
                for k in range(2):
                    for t in range(TOK):
                        mm = pe.transpose(ps[:, 4 + F % 4, k * SEQ + t * P:k * SEQ + (t + 1) * P],
                                          src[:, t, (2 * n + k) * P:(2 * n + k + 1) * P], ident[:])
                mm.then_inc(tp_ready, 1)

            def with_fills(c0, F, src, ready, banks):
                for n in range(2):
                    ready(n)
                    fill(F + n, src, n)
                for n in range(8):
                    pe.wait_ge(tp_free, F + n + 1)
                    gemm_tile(c0 + n, 0, H, 2 * n, banks, n == 0, n == 7)
                    if n < 6:
                        ready(n + 2)
                        fill(F + n + 2, src, n + 2)

            def keep_warm(n, bank):
                for _ in range(n):
                    pe.matmul(ps[:, bank, 0:P], ones[:], ones[:], start=True, stop=True)

            pe.wait_ge(consts_ready, 1)
            pe.wait_ge(ident_ready, 1)
            pe.wait_ge(rows_landed, 16)
            pe.transpose(ps[:, 0, 0:KD], rows[0:KD, 7, :], ident[0:KD, 0:KD]).then_inc(rows_T, 1)
            for n in range(2):
                pe.wait_ge(x_landed[0], 16)
                fill(F_XT1 + n, x_sb, n)
            pe.wait_ge(gains_ready, 1)
            for n in range(8):
                pe.wait_ge(tp_free, F_XT1 + n + 1)
                gemm_tile(T_IN1 + n, 0, H, 2 * n, pair(0), n == 0, n == 7)
                if n < 6:
                    pe.wait_ge(x_landed[n // 2 + 1], 16)
                    fill(F_XT1 + n + 2, x_sb, n + 2)
                if n == 4:
                    pe.wait_ge(params_landed, 16 * SMALL)
                    k = G_ROWS - KD
                    pe.transpose(ps[:, 2, NB - k:NB], rows[0:k, 0, :], ident[0:k, 0:k])
                    pe.transpose(ps[:, 2, 0:P], rows[:, 1, :], ident[:])
                    pe.transpose(ps[:, 2, P:TAPS * CC], rows[0:TAPS * CC - P, 2, :],
                                 ident[0:TAPS * CC - P, 0:TAPS * CC - P]).then_inc(rows_T, 1)
                    for i in range(4):
                        mm = pe.transpose(ps[:, 3, i * 2 * FC:(i + 1) * 2 * FC], rows[0:2 * FC, 3 + i, :],
                                          ident[0:2 * FC, 0:2 * FC])
                    mm.then_inc(rows_T, 1)
            pe.wait_ge(gains_ready, 3)

            def cu_fills(g):
                pe.wait_ge(u_ready, g + 1)
                if g == 0:
                    pe.wait_ge(tp_free, 8)
                for f in range(2):
                    if g > 0:
                        pe.wait_ge(cu_free, 2 * (g - 1) + f + 1)
                    for k in range(2):
                        for t in range(TOK):
                            c = 2 * f + k
                            mm = pe.transpose(ps[:, 6 + f, k * SEQ + t * P:k * SEQ + (t + 1) * P],
                                              a_s[:, t, c * P:(c + 1) * P], ident[:])
                    mm.then_inc(cu_ready, 1)

            def in1_tiles(lo, hi):
                for g in range(lo, hi):
                    b, n = divmod(g, 8)
                    if n == 0 and b >= 2:
                        pe.wait_ge(gemm_free[b % 2], b // 2)
                    gemm_tile(T_IN1 + g, 0, H, 2 * n, pair(b % 2), n == 0, n == 7)

            in1_tiles(8, 20)
            cu_fills(0)
            in1_tiles(20, 36)
            cu_fills(1)
            in1_tiles(36, 52)
            pe.wait_ge(cu_free, 4)
            in_sbuf(pe, 4)
            in_sbuf(pe, 5)
            for n in range(3):
                fill(F_LAT + n, z1, n)
            in1_tiles(52, 56)
            L = (latT_hi, latT_lo)

            def up_tiles(lo, hi):
                for g in range(lo, hi):
                    b, n = divmod(g, 3)
                    B = 7 + b
                    if n == 0:
                        pe.wait_ge(gemm_free[B % 2], B // 2)
                    pe.wait_ge(tp_free, F_LAT + n + 1)
                    gemm_tile(T_UQ + g, 0, L, 2 * n, pair(B % 2), n == 0, n == 2)

            up_tiles(0, 3)
            in_sbuf(pe, 6)
            for n in range(2):
                fill(F_LAT + 3 + n, z1, QC // 2 + n)
            up_tiles(3, 9)
            def attn1_T(h):
                b = 4 * ((h + 1) % 2)
                if h >= 2:
                    pe.wait_ge(at_qk, h - 1)
                for t in range(TOK):
                    pe.transpose(ps[:, b, t * P:(t + 1) * P], q1[:, t, h * QKH:h * QKH + NOPE], ident[:])
                    pe.transpose(ps[:, b, SEQ + t * P:SEQ + (t + 1) * P], kv1[:, t, h * 2 * VD:h * 2 * VD + NOPE],
                                 ident[:])
                    mm = pe.transpose(ps[0:ROPE, b + 1, t * P:(t + 1) * P],
                                      z1[:, t, h * ROPE:(h + 1) * ROPE], ident[:])
                mm.then_inc(at_T, 1)

            def attn1_S(h):
                b, e = 4 * ((h + 1) % 2), h % 2
                pe.wait_ge(at_qk, h + 1)
                if h >= 2:
                    pe.wait_ge(at_max, h - 1)
                for t in range(TOK):
                    n = (t + 1) * P
                    o = ps[:, b + 2, t * P:t * P + n]
                    pe.matmul(o, qkT[:, e, 0, t * P:(t + 1) * P], qkT[:, e, 1, 0:n], start=True, stop=False)
                    mm = pe.matmul(o, qpeT[:, e, t * P:(t + 1) * P], kpeT[:, 0:n], start=False, stop=True)
                mm.then_inc(at_S, 1)

            def attn_PT(h, h0, n, src):
                b, e = 4 * ((h + 1) % 2), h % 2
                pe.wait_ge(at_exp, h0 + h + 1)
                if h >= 2:
                    pe.wait_ge(at_out, h0 + h - 1)
                for k in range(n):
                    mm = pe.transpose(ps[:, b + 3, k * P:(k + 1) * P], src(e, k), ident[:])
                mm.then_inc(at_PT, 1)

            def attn1_PV(h):
                b, e = 4 * ((h + 1) % 2), h % 2
                pe.wait_ge(at_pT, h + 1)
                v = [kv1[:, t, h * 2 * VD + NOPE:(h + 1) * 2 * VD] for t in range(TOK)]
                pT = [att1_p[:, e, k * P:(k + 1) * P] for k in range(3)]
                pe.matmul(ps[:, b + 3, 0:VD], pT[0], v[0], start=True, stop=True)
                pe.matmul(ps[:, b + 3, VD:2 * VD], pT[1], v[0], start=True, stop=False)
                pe.matmul(ps[:, b + 3, VD:2 * VD], pT[2], v[1], start=False, stop=True).then_inc(at_PV, 1)

            def src1(e, k):
                return att1_s[:, e, k * P:(k + 1) * P]

            for g in range(8):
                b, n = divmod(g, 2)
                B = 10 + b
                if g == 4:
                    pe.wait_ge(tp_free, F_LAT + 5)
                    pe.wait_ge(kpe_ready, 1)
                    for t in range(TOK):
                        mm = pe.transpose(ps[0:ROPE, 5, t * P:(t + 1) * P], kpe[:, t, :], ident[:])
                    mm.then_inc(kpe_ready, 1)
                if n == 0:
                    pe.wait_ge(gemm_free[B % 2], B // 2)
                pe.wait_ge(tp_free, F_LAT + 4 + n)
                gemm_tile(T_UKV + g, 0, L, QC + 2 * n, pair(B % 2), n == 0, n == 1)
            pe.wait_ge(gemm_free[0], 7)
            pe.wait_ge(gemm_free[1], 7)
            pe.wait_ge(rope_ready, 1)
            pe.wait_ge(kpe_ready, 3)
            attn1_T(0)
            for h in range(HEADS + 2):
                if h + 1 < HEADS:
                    attn1_T(h + 1)
                if h < HEADS:
                    attn1_S(h)
                if 1 <= h <= HEADS:
                    attn_PT(h - 1, 0, 3, src1)
                if h >= 2:
                    attn1_PV(h - 2)

            pe.wait_ge(at_out, HEADS)
            for n in range(4):
                fill(F_MIX1 + n, attn1, n)

            def column_sums(bank):
                for t in range(TOK):
                    for c in range(CC):
                        mm = pe.matmul(ps[:, bank, t:t + 1], lnsq[:, c, t * P:(t + 1) * P], ones[:, 0:1],
                                       start=(c == 0), stop=(c == CC - 1))
                mm.then_inc(ln_mm, 1)

            for g in range(32):
                half, b, i = g // 16, g // 4, g % 4
                if g == 2:
                    pe.wait_ge(conv_tap, DVE_TAPS)
                    pe.wait_ge(pool_add, 2 * (TAPS - 1))
                    pe.wait_ge(tp_free, F_MIX1 + 4)
                    for c in range(CC):
                        mm = pe.matmul(ps[:, 4, 0:SEQ], ones[:], cv[:, c, :], start=(c == 0), stop=(c == CC - 1))
                    mm.then_inc(ln_mm, 1)
                if g == 6:
                    pe.wait_ge(ln_act, 1)
                    column_sums(5)
                if g == 8:
                    pe.wait_ge(ln_dve, 2)
                    for t in range(TOK):
                        mm = pe.matmul(ps[:, 4, t * P:(t + 1) * P], ones[:], lnsq[:, 0, t * P:(t + 1) * P],
                                       start=True, stop=True)
                    mm.then_inc(ln_mm, 1)
                if g == 14:
                    pe.wait_ge(ln_act, 3)
                    column_sums(5)
                if i == 0 and b < 6:
                    pe.wait_ge(gemm_free[b % 2], 7 + b // 2)
                if i == 0 and b >= 6:
                    pe.wait_ge(y_ready, 2 * (b - 5))
                if g < 4:
                    pe.wait_ge(tp_free, F_MIX1 + i + 1)
                if 16 <= g < 20:
                    pe.wait_ge(mix_conv, i + 1)
                gemm_tile(T_OUT1 + g, 0, H, CC * (1 - half) + 2 * i, pair(b % 2), i == 0, i == 3)

            def rows_tiles(c0, step, A, tiles, lo, hi, banks):
                k0 = sum(tiles[:lo])
                for n in range(lo, hi):
                    gemm_tile(c0 + n, step, A, k0, banks, n == 0, n == len(tiles) - 1)
                    k0 += tiles[n]

            def rows_rest(c0, A, tiles):
                T = len(tiles)
                with pe.Fori(1, 4) as n:
                    rows_tiles(c0, n * T, A, tiles, 0, T, lambda t, width: ps_flat[:, bass.ts(2 * n + t, NB)])

            def x_ready(base):
                return lambda n: pe.wait_ge(x_new, base + n + 1)

            def ff_tiles(c0, step, p, lo, hi):
                for n in range(lo, hi):
                    gemm_tile(c0 + n, step, H, 2 * n, pair(p), n == 0, n == 7)

            def ff1_turn(j):
                pe.wait_ge(gemm_free[1], G_FF1 + 1 + j)
                for f in range(2):
                    pe.wait_ge(tp_free, F_FF1 + f - 1 + 2 * j)
                    for k in range(2):
                        for t in range(TOK):
                            c = 2 * f + k
                            mm = pe.transpose(ps[:, 4 + f, k * SEQ + t * P:k * SEQ + (t + 1) * P],
                                              prod_s[:, t, c * P:(c + 1) * P], ident[:])
                    mm.then_inc(tp_ready, 1)

            keep_warm(NORM_WARM, 6)
            with_fills(T_FF1, F_XT2, x_sb, x_ready(0), pair(0))
            ff_tiles(T_FF1 + 8, 0, 1, 0, 8)
            with pe.Fori(1, FB) as j:
                pe.wait_ge(gemm_free[0], G_FF1 + j)
                ff_tiles(T_FF1, 16 * j, 0, 0, 4)
                ff1_turn(j - 1)
                ff_tiles(T_FF1, 16 * j, 0, 4, 8)
                pe.wait_ge(gemm_free[1], G_FF1 + j)
                ff_tiles(T_FF1 + 8, 16 * j, 1, 0, 8)
            A = (aT_hi, aT_lo)
            pe.wait_ge(gemm_free[0], G_FF1 + FB)
            rows_tiles(T_DN1, 0, A, DN_TILES, 0, 4, pair(0))
            ff1_turn(FB - 1)
            rows_tiles(T_DN1, 0, A, DN_TILES, 4, 20, pair(0))
            pe.wait_ge(tp_free, F_XT3)
            rows_tiles(T_DN1, 0, A, DN_TILES, 20, 24, pair(0))
            rows_rest(T_DN1, A, DN_TILES)

            pe.wait_ge(row_sq, 7)
            pe.wait_ge(row_y, 7)
            keep_warm(NORM_WARM, 4)
            with_fills(T_IN2, F_XT3, x_sb, x_ready(8), pair(0))

            def in2_tiles(lo, hi):
                for g in range(lo, hi):
                    b, n = divmod(g, 8)
                    if n == 0:
                        pe.wait_ge(gemm_free[b % 2], G_IN2 + b // 2)
                    gemm_tile(T_IN2 + g, 0, H, 2 * n, pair(b % 2), n == 0, n == 7)

            in2_tiles(8, 12)
            in_sbuf(pe, 0, G_IN2)
            pe.wait_ge(tp_free, F_XT3 + 8)
            for d in range(2):
                for t in range(TOK):
                    mm = pe.transpose(ps[0:RANK, 4, d * SEQ + t * P:d * SEQ + (t + 1) * P],
                                      z2[:, t, LR + d * RANK:LR + (d + 1) * RANK], ident[:])
            mm.then_inc(gl_mm, 1)
            in2_tiles(12, 16)
            pe.wait_ge(gl_act, 1)
            pe.wait_ge(late_landed, 16 * 7)
            for d in range(2):
                for t in range(TOK):
                    mm = pe.matmul(ps[:, 4 + 2 * d + t, :], lrT[:, d, t * P:(t + 1) * P], wa2[:, d, :],
                                   start=True, stop=True)
            mm.then_inc(gl_mm, 1)
            in2_tiles(16, 28)
            pe.wait_ge(gl_dve, 2)
            for d in range(2):
                for h in range(GH):
                    for t in range(TOK):
                        at = h * SEQ + t * P
                        mm = pe.matmul(ps[:, 4 + 2 * d + at // NB, at % NB:at % NB + P],
                                       gb[:, 0, d, t * NB + h * DK:t * NB + (h + 1) * DK], tri[:, d, :],
                                       start=True, stop=True)
            mm.then_inc(gl_mm, 1)
            in2_tiles(28, 36)
            in_sbuf(pe, 2, G_IN2)
            in_sbuf(pe, 3, G_IN2)
            pe.wait_ge(gl_act, 4)
            for i, c0 in enumerate((QG, KG)):
                for h in range(GH):
                    for t in range(TOK):
                        at = h * SEQ + t * P
                        mm = pe.transpose(ps[:, 4 + 2 * i + at // NB, at % NB:at % NB + P],
                                          z2[:, t, c0 + h * DK:c0 + (h + 1) * DK], ident[:])
            mm.then_inc(gl_mm, 1)
            in2_tiles(36, 50)

            pe.wait_ge(fac_ready, 2)
            QE, KE, QI, KO = range(4)

            def gla_A(h):
                if h == 0:
                    pe.wait_ge(gl_act, 5)
                else:
                    pe.wait_ge(g_at, h)
                for d in range(2):
                    for t in range(TOK):
                        mm = pe.matmul(ps[:, 4, (2 * d + t) * P:(2 * d + t + 1) * P],
                                       fac[:, d, KE, h, t * P:(t + 1) * P], fac[:, d, QE, h, t * P:(t + 1) * P],
                                       start=True, stop=True)
                mm.then_inc(g_AT, 1)

            def gla_KT(h):
                if h >= 1:
                    pe.wait_ge(g_o, h)
                for d in range(2):
                    for t in range(TOK):
                        mm = pe.transpose(ps[:, 5, (2 * d + t) * P:(2 * d + t + 1) * P],
                                          fac[:, d, KO, h, t * P:(t + 1) * P], ident[:])
                mm.then_inc(g_KT, 1)

            def gla_S(h, d):
                pe.wait_ge(g_kt, h + 1)
                if h + d >= 1:
                    pe.wait_ge(g_st, 2 * h + d)
                for n in range(3):
                    c = n if d == 0 else 3 - n
                    r = slice(CHUNK * (c % 2), CHUNK * (c % 2) + CHUNK)
                    mm = pe.matmul(gla_sum(d, c), ktok[r, d, c // 2, :],
                                   z2[r, c // 2, VG + h * DV:VG + (h + 1) * DV], start=True, stop=True)
                mm.then_inc(g_SS, 1)

            def gla_O(h):
                pe.wait_ge(g_at, h + 1)
                pe.wait_ge(g_st, 2 * h + 2)
                for t in range(TOK):
                    o = ps[:, 5, t * DV:(t + 1) * DV]
                    pe.matmul(o, at_sb[:, t, :], z2[:, t, VG + h * DV:VG + (h + 1) * DV],
                              start=True, stop=False, skip_group_check=True)
                    parts = []
                    for half in range(2):
                        c = 2 * t + half
                        if c >= 1:
                            parts.append((half, 0, c, c - 1))
                        if c <= 2:
                            parts.append((half, 1, c, 2 - c))
                    for n, (half, d, c, i) in enumerate(parts):
                        mm = pe.matmul(ps[half * CHUNK:(half + 1) * CHUNK, 5, t * DV:(t + 1) * DV],
                                       fac[:, d, QI, h, c * CHUNK:(c + 1) * CHUNK], state[:, d, i, :],
                                       start=False, stop=(n == len(parts) - 1), skip_group_check=True)
                mm.then_inc(g_O, 1)

            def gated_fill(n):
                pe.wait_ge(mix2_ready, n + 1)
                if n == 3:
                    pe.wait_ge(kpe_ready, 5)
                fill(F_MIX2 + n, z2[:, :, QG:QG + 2 * NB], n)

            for g in range(50, 80):
                h, k = gla_slot(g)
                if k == 0 and 1 <= h <= GH:
                    gla_O(h - 1)
                if k == 0 and 0 <= h < GH:
                    gla_A(h)
                if k == 1 and 0 <= h < GH:
                    gla_KT(h)
                if k in (2, 4) and 0 <= h < GH:
                    gla_S(h, k // 2 - 1)
                if g == 74:
                    pe.wait_ge(rope_ready, 2)
                    pe.wait_ge(g_st, 2 * GH)
                    for q in range(KVH):
                        for t in range(TOK):
                            mm = pe.transpose(ps[:, 6, q * SEQ + t * P:q * SEQ + (t + 1) * P],
                                              z2[:, t, KA + q * HD:KA + (q + 1) * HD], ident[:])
                    mm.then_inc(kpe_ready, 1)
                if g >= MIX_FILL:
                    gated_fill(g - MIX_FILL)
                in2_tiles(g, g + 1)

            def attn2_T(p):
                if p < 2:
                    pe.wait_ge(rope_ready, 3)
                    pe.wait_ge(tp_free, F_MIX2 + 2)
                else:
                    pe.wait_ge(rope_ready, 2 + p)
                    pe.wait_ge(tp_free, F_MIX2 + 3 + p)
                if p == 1:
                    pe.wait_ge(at_qk, HEADS + 1)
                for k in range(2):
                    h = HEAD_ORDER[2 * p + k]
                    for t in range(TOK):
                        mm = pe.transpose(ps[:, 4, k * SEQ + t * P:k * SEQ + (t + 1) * P],
                                          z2[:, t, h * HD:(h + 1) * HD], ident[:])
                mm.then_inc(at_T, 1)

            def attn2_S(i):
                g = HEAD_ORDER[i] * KVH // HEADS
                pe.wait_ge(at_qk, HEADS + i // 2 + 1)
                if i == 0:
                    pe.wait_ge(kpe_ready, 5)
                    pe.wait_ge(tp_free, F_MIX2 + 3)
                else:
                    pe.wait_ge(at_exp, HEADS + i)
                for t in range(TOK):
                    mm = pe.matmul(ps[:, 5, t * SEQ:(t + 1) * SEQ], att2_q[:, i // 2 % 2, i % 2, t * P:(t + 1) * P],
                                   kaT[:, g, :], start=True, stop=True)
                mm.then_inc(at_S, 1)

            def attn2_PT(i):
                pe.wait_ge(at_exp, HEADS + i + 1)
                if i == 0:
                    pe.wait_ge(tp_free, F_MIX2 + 4)
                else:
                    pe.wait_ge(at_pT, HEADS + i)
                for k in range(4):
                    mm = pe.transpose(ps[:, 6, k * P:(k + 1) * P],
                                      att2_s[:, i % 2, k // 2, (k % 2) * P:(k % 2 + 1) * P], ident[:])
                mm.then_inc(at_PT, 1)

            def attn2_PV(i):
                g = HEAD_ORDER[i] * KVH // HEADS
                pe.wait_ge(at_pT, HEADS + i + 1)
                if i >= 1:
                    pe.wait_ge(at_out, HEADS + i)
                for t in range(TOK):
                    for k in range(TOK):
                        at = (i % 2) * SEQ + t * HD
                        mm = pe.matmul(ps[:, 7, at:at + HD], att2_p[:, i % 2, 2 * t + k, :],
                                       z2[:, k, VA + g * HD:VA + (g + 1) * HD], start=(k == 0), stop=(k == 1))
                mm.then_inc(at_PV, 1)

            def attn2_fill(p):
                pe.wait_ge(at_out, HEADS + 2 * p + 2)
                pe.wait_ge(at_qk, HEADS + min(p + 2, 4))
                pe.wait_ge(tp_free, F_MIX2 + 4 + p)
                for k in range(2):
                    h = HEAD_ORDER[2 * p + k]
                    for t in range(TOK):
                        mm = pe.transpose(ps[:, 4, k * SEQ + t * P:k * SEQ + (t + 1) * P],
                                          z2[:, t, h * HD:(h + 1) * HD], ident[:])
                mm.then_inc(tp_ready, 1)

            def x4_fill(n):
                pe.wait_ge(x_new, 16 + n // 2 + 1)
                if n == 0:
                    pe.wait_ge(tp_free, F_XT4)
                    pe.wait_ge(at_out, 2 * HEADS)
                fill(F_XT4 + n, x_sb, XT4_ORDER[n])

            pe.wait_ge(gemm_free[0], G_FF2)
            for g in range(32):
                if g < MIX_FILL + 4 - 80:
                    gated_fill(80 - MIX_FILL + g)
                if g % 4 == 0 and g // 4 < 4:
                    attn2_T(g // 4)
                if g % 2 == 1:
                    if 0 <= (g - 3) // 2 < HEADS:
                        attn2_PT((g - 3) // 2)
                    if 0 <= (g - 1) // 2 < HEADS:
                        attn2_S((g - 1) // 2)
                elif 0 <= (g - 4) // 2 < HEADS:
                    attn2_PV((g - 4) // 2)
                if g % 4 == 3 and 0 <= (g - 7) // 4 < 4:
                    attn2_fill((g - 7) // 4)
                if g < 16:
                    b, i = g // 4, g % 4
                    k0 = CC + 2 * i
                    if g < 4:
                        pe.wait_ge(tp_free, F_MIX2 + i + 1)
                    if i == 0 and b == 1:
                        pe.wait_ge(gemm_free[1], G_FF2)
                    if i == 0 and b >= 2:
                        pe.wait_ge(half_added, b - 1)
                else:
                    b, i = OUT2_TILES[g - 16]
                    k0 = 2 * PAIR_ORDER[i]
                    if b == 2:
                        pe.wait_ge(tp_free, F_MIX2 + 4 + i + 1)
                    if i == 0:
                        if b >= 2:
                            pe.wait_ge(half_added, b + 1)
                        else:
                            pe.wait_ge(x_new, 16 + b + 1)
                if 27 <= g < 31:
                    x4_fill(g - 27)
                gemm_tile(T_OUT2 + g, 0, H, k0, pair(b % 2), i == 0, i == 3)

            def ff2_turn(j, half):
                pe.wait_ge(gemm_free[half], G_FF2 + 1 + j)
                for c in range(4):
                    for t in range(TOK):
                        mm = pe.transpose(ps[:, 4 + 2 * half + c // 2, (c % 2) * SEQ + t * P:(c % 2) * SEQ + (t + 1) * P],
                                          raw_s[:, t, c * P:(c + 1) * P], ident[:])
                mm.then_inc(ct_ready, 1)

            for n in range(8):
                pe.wait_ge(tp_free, F_XT4 + n + 1)
                gemm_tile(T_FF2 + n, 0, H, 2 * XT4_ORDER[n], pair(0), n == 0, n == 7)
                if n < 4:
                    x4_fill(n + 4)
            ff_tiles(T_FF2 + 8, 0, 1, 0, 4)
            pe.wait_ge(tp_free, F_XT4 + 8)
            ff2_turn(0, 0)
            ff_tiles(T_FF2 + 8, 0, 1, 4, 8)
            with pe.Fori(1, FB) as j:
                pe.wait_ge(gemm_free[0], G_FF2 + j)
                ff_tiles(T_FF2, 16 * j, 0, 0, 4)
                pe.wait_ge(ct_free, 2 * j - 1)
                ff2_turn(j - 1, 1)
                ff_tiles(T_FF2, 16 * j, 0, 4, 8)
                pe.wait_ge(gemm_free[1], G_FF2 + j)
                ff_tiles(T_FF2 + 8, 16 * j, 1, 0, 4)
                pe.wait_ge(ct_free, 2 * j)
                ff2_turn(j, 0)
                ff_tiles(T_FF2 + 8, 16 * j, 1, 4, 8)
            pe.wait_ge(gemm_free[0], G_FF2 + FB)
            rows_tiles(T_DN2, 0, A, DN_TILES, 0, 4, pair(0))
            pe.wait_ge(ct_free, 2 * FB - 1)
            ff2_turn(FB - 1, 1)
            rows_tiles(T_DN2, 0, A, DN_TILES, 4, 20, pair(0))
            pe.wait_ge(aT_ready, FB)
            rows_tiles(T_DN2, 0, A, DN_TILES, 20, 24, pair(0))
            rows_rest(T_DN2, A, DN_TILES)

        @block.scalar
        def _(act):
            done = [0]

            def split_hi(c0, step):
                kc, width = SHAPES[c0]
                s = c0 % RING
                act.wait_ge(raw_landed[s], landed(c0, step))
                if c0 >= RING:
                    act.wait_ge(tile_used, c0 - RING + 1 + step)
                act.activation(w_hi[:, s, :kc, :width], raw[:, s, :kc, :width], ACT.Copy).then_inc(hi_ready, 1)

            def hi_upto(n):
                for g in range(done[0], n):
                    split_hi(g, 0)
                done[0] = max(done[0], n)

            def hi_tiles(c0, step, lo, hi):
                for g in range(c0 + lo, c0 + hi):
                    split_hi(g, step)

            count = [0]

            def step(ins):
                count[0] += 1
                ins.then_inc(act_step, 1)
                act.wait_ge(act_step, count[0])

            def fill_hi(F, dst, k, gain=None, bank=None):
                act.wait_ge(tp_ready, F + 1)
                b = 4 + F % 4
                for i in range(2):
                    at = G_AT[gain[0]] + gain[1] + i if gain else None
                    ins = act.activation(dst[:, k + i, :], ps[:, b, i * SEQ:(i + 1) * SEQ], ACT.Copy,
                                         **({"scale": gains[:, at:at + 1]} if gain else {}))
                ins.then_inc(tp_hi, 1)

            def squares(out, in_, name, at):
                return act.activation(out, in_, ACT.Square, accum_out=r_of(ss, name, at, 1))

            act.dma_start(rows[0:KD, 7, :], a["pre_mix_norm"].rearrange("o (c p) -> (o c) p", p=P)).then_inc(rows_landed, 16)
            act.wait_ge(rows_T, 1)
            act.activation(gains[:, 0:KD], ps[:, 0, 0:KD], ACT.Copy).then_inc(gains_ready, 1)
            act.wait_ge(gains_ready, 1)
            for n in range(8):
                fill_hi(F_XT1 + n, hT_hi, 2 * n, ("pre_mix_norm", 2 * n))
                if n == 6:
                    act.wait_ge(rows_T, 2)
                    act.activation(gains[:, KD:G_ROWS], ps[:, 2, NB - G_ROWS + KD:NB], ACT.Copy)
                    act.activation(convw[:], ps[:, 2, 0:TAPS * CC], ACT.Copy).then_inc(gains_ready, 1)
                    act.wait_ge(rows_T, 3)
                    act.activation(conv2[:].rearrange("p k c -> p (k c)"), ps[:, 3, 0:8 * FC], ACT.Copy).then_inc(gains_ready, 1)
                hi_upto(min(n + 3, 8))
            hi_upto(9)
            for n in range(4):
                act.wait_ge(x_landed[n], 16)
            for t in range(TOK):
                ins = squares(kv1[:, t, :], x_sb[:, t, :], "x0", t)
                if t == 0:
                    hi_upto(10)
            ins.then_inc(sq_done, 1)
            hi_upto(11)

            def scaled(B, gend, dst, name, at, width, func=ACT.Copy, free=True):
                act.wait_ge(tile_used, gend)
                for t in range(TOK):
                    ins = act.activation(dst(t), ps[:, 2 * (B % 2) + t, :width], func, scale=r_of(rstd, name, at + t, 1))
                ins.then_inc(gemm_free[B % 2], 1)

            act.wait_ge(rstd_ready, r_count("x0"))
            scaled(0, T_IN1 + 8, lambda t: a_s[:, t, :], "x0", 0, NB)
            hi_upto(19)
            scaled(1, T_IN1 + 16, lambda t: sg_s[:, t, :], "x0", 0, NB, ACT.Sigmoid)

            def cu_evac(g):
                for f in range(2):
                    act.wait_ge(cu_ready, 2 * g + f + 1)
                    c = 4 * g + 2 * f
                    act.activation(uT[:, c:c + 2, TAPS - 1:], ps[:, 6 + f, :].rearrange("p (c s) -> p c s", c=2),
                                   ACT.Copy).then_inc(cu_free, 1)

            hi_upto(23)
            cu_evac(0)
            act.wait_ge(trig_arg, 1)
            tt = [trig_t[:, i, :].rearrange("p (t n) -> p t n", t=TOK) for i in range(4)]
            act.activation(tt[1], tt[0], ACT.Abs).then_inc(trig_abs, 1)
            act.wait_ge(trig_arg, 2)
            act.activation(trig[:, :, 0, :], tt[2], ACT.Sin)
            act.activation(trig[:, :, 1, :], tt[0], ACT.Sin).then_inc(trig_done, 1)
            hi_upto(27)
            scaled(2, T_IN1 + 24, lambda t: a_s[:, t, :], "x0", 0, NB)
            hi_upto(35)
            scaled(3, T_IN1 + 32, lambda t: sg_s[:, t, :], "x0", 0, NB, ACT.Sigmoid)
            hi_upto(39)
            cu_evac(1)
            hi_upto(43)

            def z1_block(b):
                act.wait_ge(tile_used, T_IN1 + 8 * (b + 5))
                for t in range(TOK):
                    ins = act.activation(z1[:, t, b * 448:(b + 1) * 448], ps[:, 2 * (b % 2) + t, :448], ACT.Copy,
                                         scale=r_of(rstd, "x0", t, 1))
                ins.then_inc(gemm_free[b % 2], 1)

            z1_block(0)
            hi_upto(51)
            z1_block(1)
            in_sbuf(act, 5)
            for t in range(TOK):
                squares(q1[:, t, 0:QL], z1[:, t, 0:QL], "lat", t)
            hi_upto(55)
            for n in range(3):
                fill_hi(F_LAT + n, latT_hi, 2 * n, ("q_norm", 2 * n))
            hi_upto(59)
            z1_block(2)
            in_sbuf(act, 6)
            for t in range(TOK):
                ins = squares(q1[:, t, QL:QL + KVL], z1[:, t, QL:QL + KVL], "lat", 2 + t)
            ins.then_inc(sq_done, 1)
            hi_upto(62)
            for n in range(2):
                fill_hi(F_LAT + 3 + n, latT_hi, QC + 2 * n, ("kv_norm", 2 * n))
            act.wait_ge(rstd_ready, r_count("lat"))
            for b in range(3):
                scaled(7 + b, T_UQ + 3 * (b + 1), lambda t: q1[:, t, b * NB:(b + 1) * NB], "lat", 0, NB)
                hi_upto([65, 67, 69][b])
            def attn1_qk(h):
                b, e = 4 * ((h + 1) % 2), h % 2
                act.wait_ge(at_T, h + 1)
                if h >= 2:
                    act.wait_ge(at_S, h - 1)
                act.activation(qkT[:, e].rearrange("p i s -> p (i s)"), ps[:, b, :], ACT.Copy)
                act.activation(qpeT[:, e, :], ps[0:ROPE, b + 1, 0:SEQ], ACT.Copy).then_inc(at_qk, 1)

            def attn_exp(h, h0, src, scale):
                e = h % 2
                act.wait_ge(at_max, h0 + h + 1)
                for t in range(TOK):
                    ins = act.activation(src(e, t), src(e, t), ACT.Exp, bias=amax[:, e, t, 2:3], scale=scale,
                                         accum_out=asum[:, e, 0, t:t + 1])
                ins.then_inc(at_exp, 1)

            def attn_pT(h, h0, dst, n):
                b, e = 4 * ((h + 1) % 2), h % 2
                act.wait_ge(at_PT, h0 + h + 1)
                act.activation(dst(e), ps[:, b + 3, 0:n * P], ACT.Copy).then_inc(at_pT, 1)

            def s1(e, t):
                return att1_s[:, e, t * P:t * P + (t + 1) * P]

            for b in range(4):
                scaled(10 + b, T_UKV + 2 * (b + 1), lambda t: kv1[:, t, b * NB:(b + 1) * NB], "lat", 2, NB)
                hi_upto([71, 73, 75, 77][b])
                if b == 1:
                    act.wait_ge(kpe_ready, 2)
                    act.activation(kpeT[:, :], ps[0:ROPE, 5, 0:SEQ], ACT.Copy).then_inc(kpe_ready, 1)
            attn1_qk(0)
            for h in range(HEADS + 1):
                if h + 1 < HEADS:
                    attn1_qk(h + 1)
                if h >= 1:
                    attn_pT(h - 1, 0, lambda e: att1_p[:, e, :], 3)
                if h < HEADS:
                    attn_exp(h, 0, s1, float(QKH) ** -0.5)
            act.wait_ge(at_out, HEADS)
            for n in range(4):
                fill_hi(F_MIX1 + n, hT_hi, CC + 2 * n, ("attn_out_norm", 2 * n))
            for t in range(TOK):
                ins = squares(kv1[:, t, 0:CONV], attn1[:, t, :], "attn", t)
            ins.then_inc(sq_done, 1)
            hi_upto(T_OUT1 + 5)

            def attn_half(n):
                scaled(14 + n, T_OUT1 + 4 * (n + 1), lambda t: y_out[:, (2 * n + t) * NB:(2 * n + t + 1) * NB], "attn",
                       0, NB)

            act.wait_ge(ln_dve, 1)
            act.activation(lnsq[:], cv[:], ACT.Square).then_inc(ln_act, 1)
            act.wait_ge(rstd_ready, r_count("attn"))
            hi_upto(T_OUT1 + 8)
            attn_half(0)
            hi_upto(T_OUT1 + 11)
            act.wait_ge(ln_dve, 3)
            for c in range(CC):
                g, b = G_AT["conv_ln_g"] + c, G_AT["conv_ln_b"] + c
                ins = act.activation(cv[:, c, :], cv[:, c, :], ACT.Silu, scale=gains[:, g:g + 1], bias=gains[:, b:b + 1])
                if c == 3:
                    hi_upto(T_OUT1 + 12)
            ins.then_inc(ln_act, 1)
            attn_half(1)
            hi_upto(T_OUT1 + 13)
            act.wait_ge(ln_act, 2)
            act.activation(lnsq[:], cv[:], ACT.Square).then_inc(ln_act, 1)
            hi_upto(T_OUT1 + 14)
            for c in range(CC):
                g = G_AT["conv_out_norm"] + c
                if c == 4:
                    hi_upto(T_OUT1 + 15)
                ins = act.activation(hT_hi[:, c, :], cv[:, c, :], ACT.Copy, scale=gains[:, g:g + 1])
                if c % 2 == 1:
                    ins.then_inc(conv_hi, 1)
            hi_upto(T_OUT1 + 16)
            attn_half(2)
            hi_upto(T_OUT1 + 19)
            attn_half(3)

            def y_squares(n):
                for t in range(TOK):
                    act.wait_ge(y_ready, 2 * n + t + 1)
                    ins = act.activation(lnsq[:].rearrange("p c s -> p (c s)")[:, bass.ts(2 * (n % 2) + t, NB)],
                                         y_out[:, (2 * n + t) * NB:(2 * n + t + 1) * NB], ACT.Square,
                                         accum_out=ss4[:, 4 * t + n:4 * t + n + 1])
                ins.then_inc(row_sq, 1)

            for n in range(4):
                hi_upto(T_OUT1 + 16 + 4 * n + 7)
                y_squares(n)

            def row_squares(c_end, step, n, y):
                act.wait_ge(tile_used, c_end + step)
                for t in range(TOK):
                    ins = act.activation(y[:, bass.ts(2 * n + t, NB)], ps_flat[:, bass.ts(2 * n + t, NB)], ACT.Square,
                                         accum_out=ss4[:, bass.ts(4 * t + n, 1)])
                ins.then_inc(row_sq, 1)

            def x_squares(end, junk, name, c0):
                hi_upto(c0 + 9)
                act.wait_ge(x_new, end)
                for t in range(TOK):
                    ins = squares(junk(t), x_sb[:, t, :], name, t)
                    if t == 0:
                        hi_upto(c0 + 10)
                ins.then_inc(sq_done, 1)

            def with_fills(c0, F, gain):
                hi_upto(c0 + 3)
                for n in range(8):
                    fill_hi(F + n, hT_hi, 2 * n, (gain, 2 * n))
                    hi_upto(c0 + min(n + 3, 8))

            with_fills(T_FF1, F_XT2, "pre_ffn_norm")
            x_squares(8, lambda t: y_out[:, t * DM:(t + 1) * DM], "x1", T_FF1)
            act.wait_ge(rstd_ready, r_count("x1"))

            def silu1(j):
                act.wait_ge(tile_used, T_FF1 + 8 + 16 * j)
                for t in range(TOK):
                    ins = act.activation(gate_s[:, t, :], ps[:, t, :], ACT.Silu, scale=r_of(rstd, "x1", t, 1))
                ins.then_inc(gemm_free[0], 1)

            def turn_hi(j):
                for f in range(2):
                    act.wait_ge(tp_ready, F_FF1 + f + 1 + 2 * j)
                    act.activation(aT_hi_flat[:, bass.ts(2 * j + f, 2 * SEQ)], ps[:, 4 + f, :], ACT.Copy).then_inc(tp_hi, 1)

            aT_hi_flat = aT_hi[:].rearrange("p c s -> p (c s)")
            hi_upto(T_FF1 + 11)
            silu1(0)
            hi_upto(T_FF1 + 16)
            with act.Fori(1, FB) as j:
                hi_tiles(T_FF1, 16 * j, 0, 7)
                turn_hi(j - 1)
                hi_tiles(T_FF1, 16 * j, 7, 11)
                act.wait_ge(gemm_free[1], G_FF1 + j)
                silu1(j)
                hi_tiles(T_FF1, 16 * j, 11, 16)
            done[0] = T_DN1
            hi_upto(T_DN1 + 7)
            turn_hi(FB - 1)
            act.dma_start(grow_dn[:], a["post_ffn_norm"].to_broadcast([P, DM])).then_inc(grow_landed, 16)
            hi_upto(T_DN1 + 24)
            c0, T = T_DN1, 24
            with act.Fori(1, 4) as n:
                hi_tiles(c0, n * T, 0, 3)
                row_squares(c0, n * T, n - 1, y_dn)
                hi_tiles(c0, n * T, 3, T)
            done[0] = T_IN2
            hi_upto(T_IN2 + 3)
            row_squares(T_IN2, 0, 3, y_dn)

            with_fills(T_IN2, F_XT3, "norm1_g_2")
            x_squares(16, lambda t: fac[:, t].rearrange("p a h s -> p (a h s)")[:, 0:DM], "x2", T_IN2)
            act.wait_ge(rstd_ready, r_count("x2"))

            def z2_block(p):
                n = B2_ORDER[p]
                act.wait_ge(tile_used, T_IN2 + 8 * (p + 1))
                for t in range(TOK):
                    ins = act.activation(z2[:, t, n * W2:(n + 1) * W2], ps[:, 2 * (p % 2) + t, :W2], ACT.Copy,
                                         scale=r_of(rstd, "x2", t, 1))
                ins.then_inc(gemm_free[p % 2], 1)

            b_sum = [gb[:, 1, d, :].rearrange("p (h s) -> p h s", h=GH) for d in range(2)]
            hi_upto(T_IN2 + 11)
            z2_block(0)
            hi_upto(T_IN2 + 15)
            act.wait_ge(gl_mm, 1)
            act.wait_ge(consts_ready, 3)
            act.activation(lrT[0:RANK].rearrange("p d s -> p (d s)"), ps[0:RANK, 4, :], ACT.Copy).then_inc(gl_act, 1)
            hi_upto(T_IN2 + 19)
            z2_block(1)
            hi_upto(T_IN2 + 20)
            act.wait_ge(gl_dve, 1)
            for d in range(2):
                ins = act.activation(gb[:, 0, d], gb[:, 0, d], ACT.Exp)
                if d == 0:
                    hi_upto(T_IN2 + 21)
            ins.then_inc(gl_act, 1)
            hi_upto(T_IN2 + 22)
            act.wait_ge(gl_act, 2)
            for d in range(2):
                ins = act.activation(gb[:, 0, d], gb[:, 0, d], ACT.Ln, bias=1.0)
                if d == 0:
                    hi_upto(T_IN2 + 23)
            ins.then_inc(gl_act, 1)
            hi_upto(T_IN2 + 27)
            z2_block(2)
            hi_upto(T_IN2 + 31)
            act.wait_ge(gl_mm, 3)
            for d in range(2):
                for i in range(2):
                    ins = act.activation(gb[:, 1, d, i * NB:(i + 1) * NB], ps[:, 4 + 2 * d + i, :], ACT.Copy)
                if d == 0:
                    hi_upto(T_IN2 + 32)
            ins.then_inc(gl_act, 1)
            S16 = 1.0 / 16.0
            for d in range(2):
                hi_upto(T_IN2 + 33 + 3 * d)
                act.wait_ge(fac_diff, d + 1)
                step(act.activation(fac[:, d, 1], fac[:, d, 0], ACT.Exp, scale=-S16))
                act.activation(fac[:, d, 0], fac[:, d, 0], ACT.Exp, scale=S16)
                hi_upto(T_IN2 + 34 + 3 * d)
                act.activation(fac[:, d, 2], b_sum[d], ACT.Exp, scale=S16)
                act.activation(decay[:, d, :], last_of(b_sum[d], d), ACT.Exp, scale=S16)
                act.activation(fac[:, d, 3], fac[:, d, 3], ACT.Exp, scale=-S16).then_inc(fac_exp, 1)
                if d == 0:
                    hi_upto(T_IN2 + 35)
                    z2_block(3)
            hi_upto(T_IN2 + 39)
            act.wait_ge(gl_mm, 4)
            for i in range(2):
                act.activation(qT2[:, 2 * i:2 * i + 2, :], ps[:, 4 + i, :].rearrange("p (h s) -> p h s", h=2), ACT.Copy,
                               scale=float(DK) ** -0.5)
                ins = act.activation(kT2[:, 2 * i:2 * i + 2, :], ps[:, 6 + i, :].rearrange("p (h s) -> p h s", h=2), ACT.Copy)
            ins.then_inc(gl_act, 1)
            hi_upto(T_IN2 + 43)
            z2_block(4)

            def part_squares(part):
                name, h0, n, p, _ = QK_PARTS[part]
                in_sbuf(act, p, G_IN2)
                in_sbuf(act, p - 1, G_IN2)
                if part >= 2:
                    act.wait_ge(sq_done, 7)
                base = (0, 4, 0, 4)[part]
                for t in range(TOK):
                    for h in range(n):
                        i = t * n + h
                        ins = squares(gb_flat[:, (base + i) * HD:(base + i + 1) * HD],
                                      z2[:, t, (h0 + h) * HD:(h0 + h + 1) * HD], name, i)
                ins.then_inc(sq_done, 1)

            def k_copy(h):
                act.wait_ge(g_KT, h + 1)
                if h >= 1:
                    act.wait_ge(g_SS, 2 * h)
                act.activation(ktok[:].rearrange("p d t k -> p (d t k)"), ps[:, 5, :], ACT.Copy).then_inc(g_kt, 1)

            def gla_squares(h):
                act.wait_ge(g_o, h + 1)
                for t in range(TOK):
                    ins = act.activation(gb_flat[:, 3584 + t * DV:3584 + (t + 1) * DV],
                                         z2[:, t, QG + h * DV:QG + (h + 1) * DV], ACT.Square,
                                         accum_out=r_of(ss, "gla", t * GH + h, 1))
                    if h < GH - 1:
                        step(ins)
                if h == GH - 1:
                    ins.then_inc(sq_done, 1)

            def split_copy(F, pair_at, bank, after=None):
                act.wait_ge(tp_ready, F + 1)
                if after is not None:
                    act.wait_ge(tile_used, after)
                act.activation(hT_hi[:, 2 * pair_at:2 * pair_at + 2, :], ps[:, bank, :].rearrange("p (c s) -> p c s", c=2),
                               ACT.Copy).then_inc(tp_hi, 1)

            for g in range(43, 80):
                h, k = gla_slot(g - 2)
                if g % 8 == 3 and g > 43:
                    z2_block(g // 8 - 1)
                if k == 0 and 1 <= h <= GH:
                    gla_squares(h - 1)
                if k == 1 and 0 <= h < GH:
                    k_copy(h)
                if g == 60:
                    part_squares(0)
                if g == 68:
                    part_squares(1)
                if g == 76:
                    act.wait_ge(kpe_ready, 4)
                    act.activation(kaT[:].rearrange("p g s -> p (g s)"), ps[:, 6, :], ACT.Copy).then_inc(kpe_ready, 1)
                    for p in (0, 5, 8):
                        in_sbuf(act, p, G_IN2)
                    act.activation(z2[:, :, GG:GG + 2 * NB], z2[:, :, GG:GG + 2 * NB], ACT.Silu).then_inc(gate2_ready, 1)
                hi_upto(T_IN2 + g + 1)

            for g in range(32):
                if 0 <= g - 2 - (MIX_FILL - 80) < 4:
                    n = g - 2 - (MIX_FILL - 80)
                    split_copy(F_MIX2 + n, 4 + n, 4 + (F_MIX2 + n) % 4, T_IN2 + 77 + n)
                if g == 3:
                    z2_block(9)
                if g % 4 == 2 and g // 4 < 4:
                    p = g // 4
                    act.wait_ge(at_T, HEADS + p + 1)
                    if p >= 2:
                        act.wait_ge(at_S, HEADS + 2 * p - 2)
                    act.activation(att2_q[:, p % 2].rearrange("p k s -> p (k s)"), ps[:, 4, :], ACT.Copy).then_inc(at_qk, 1)
                if g == 3:
                    part_squares(2)
                    part_squares(3)
                if g % 2 == 1:
                    i = (g - 5) // 2
                    if 0 <= i < HEADS:
                        act.wait_ge(at_PT, HEADS + i + 1)
                        if i >= 2:
                            act.wait_ge(at_PV, HEADS + i - 1)
                        act.activation(att2_p[:, i % 2].rearrange("p k s -> p (k s)"), ps[:, 6, :], ACT.Copy).then_inc(at_pT, 1)
                    if g % 4 == 1 and 0 <= (g - 9) // 4 < 4:
                        p = (g - 9) // 4
                        split_copy(F_MIX2 + 4 + p, PAIR_ORDER[p], 4)
                    i = (g - 3) // 2
                    if 0 <= i < HEADS:
                        e, h = i % 2, HEAD_ORDER[i]
                        act.wait_ge(at_max, HEADS + i + 1)
                        if i >= 2:
                            act.wait_ge(at_PT, HEADS + i - 1)
                        for t in range(TOK):
                            act.activation(amax[:, e, t, 3:4], sinkb[:, h:h + 1], ACT.Exp, bias=amax[:, e, t, 2:3])
                        for t in range(TOK):
                            ins = act.activation(att2_s[:, e, t, :], ps[:, 5, t * SEQ:(t + 1) * SEQ], ACT.Exp,
                                                 bias=amax[:, e, t, 2:3], scale=float(HD) ** -0.5,
                                                 accum_out=asum[:, e, 0, t:t + 1])
                        ins.then_inc(at_exp, 1)
                i = (g - 6) // 2
                if g % 2 == 0 and 0 <= i < HEADS:
                    e, h = i % 2, HEAD_ORDER[i]
                    act.wait_ge(at_PV, HEADS + i + 1)
                    act.wait_ge(at_sum, HEADS + i + 1)
                    for t in range(TOK):
                        ins = act.activation(z2[:, t, h * HD:(h + 1) * HD],
                                             ps[:, 7, e * SEQ + t * HD:e * SEQ + (t + 1) * HD], ACT.Copy,
                                             scale=asum[:, e, 1, t:t + 1])
                    ins.then_inc(at_out, 1)
                if g >= 29:
                    fill_hi(F_XT4 + g - 29, hT_hi, 2 * XT4_ORDER[g - 29], ("norm2_g_2", 2 * XT4_ORDER[g - 29]))
                hi_upto(T_OUT2 + g + 1)

            for n in range(3, 8):
                if n >= 4:
                    act.wait_ge(tile_used, T_FF2)
                fill_hi(F_XT4 + n, hT_hi, 2 * XT4_ORDER[n], ("norm2_g_2", 2 * XT4_ORDER[n]))
                hi_upto(T_FF2 + n + 1)
            x_squares(20, lambda t: y_out[:, t * DM:(t + 1) * DM], "x3", T_FF2)
            act.wait_ge(rstd_ready, r_count("x3"))

            def copy2(j, half):
                act.wait_ge(tile_used, T_FF2 + 8 + 8 * half + 16 * j)
                for t in range(TOK):
                    ins = act.activation(raw_s[:, t, :], ps[:, 2 * half + t, :], ACT.Copy, scale=r_of(rstd, "x3", t, 1))
                ins.then_inc(gemm_free[half], 1)

            def center2(j, half):
                act.wait_ge(ct_ready, 2 * j + half + 1)
                dst = cg if half == 0 else cval
                for c in range(4):
                    k = 4 * j + c + FC * half
                    ins = act.activation(dst[:, c, :], ps[:, 4 + 2 * half + c // 2, (c % 2) * SEQ:(c % 2 + 1) * SEQ],
                                         ACT.Identity, scale=conv2[:, 1, bass.ts(k, 1)], bias=conv2[:, 3, bass.ts(k, 1)])
                    if c % 2:
                        ins.then_inc(ct_center, 1)

            def silu2(j):
                act.wait_ge(ct_free, 2 * j + 1)
                act.activation(cg[:], cg[:], ACT.Silu).then_inc(cg_silu, 1)

            def hidden_hi(j):
                act.wait_ge(prod_ready, j + 1)
                act.activation(aT_hi_flat[:, bass.ts(j, 4 * SEQ)], cg[:].rearrange("p c s -> p (c s)"), ACT.Copy)\
                   .then_inc(aT_hi_ready, 1)

            hi_upto(T_FF2 + 11)
            copy2(0, 0)
            hi_upto(T_FF2 + 15)
            center2(0, 0)
            hi_upto(T_FF2 + 16)
            with act.Fori(1, FB) as j:
                hi_tiles(T_FF2, 16 * j, 0, 2)
                silu2(j - 1)
                hi_tiles(T_FF2, 16 * j, 2, 3)
                act.wait_ge(ct_ready, 2 * j - 1)
                copy2(j - 1, 1)
                hi_tiles(T_FF2, 16 * j, 3, 7)
                center2(j - 1, 1)
                hi_tiles(T_FF2, 16 * j, 7, 11)
                act.wait_ge(ct_ready, 2 * j)
                copy2(j, 0)
                hidden_hi(j - 1)
                hi_tiles(T_FF2, 16 * j, 11, 15)
                act.wait_ge(aT_ready, j)
                center2(j, 0)
                hi_tiles(T_FF2, 16 * j, 15, 16)
            done[0] = T_DN2
            hi_upto(T_DN2 + 2)
            silu2(FB - 1)
            hi_upto(T_DN2 + 3)
            act.wait_ge(ct_ready, 2 * FB - 1)
            copy2(FB - 1, 1)
            hi_upto(T_DN2 + 7)
            center2(FB - 1, 1)
            hi_upto(T_DN2 + 11)
            hidden_hi(FB - 1)
            hi_upto(T_DN2 + 24)
            with act.Fori(1, 4) as n:
                hi_tiles(T_DN2, 24 * n, 0, 24)

        @block.vector
        def _(dve):
            done = [0]
            count = [0]

            def split_lo(c0, step):
                kc, width = SHAPES[c0]
                s = c0 % RING
                dve.wait_ge(hi_ready, c0 + 1 + step)
                dve.tensor_tensor(w_lo[:, s, :kc, :width], raw[:, s, :kc, :width],
                                  w_hi[:, s, :kc, :width].bitcast(F32), ALU.subtract).then_inc(lo_ready, 1)

            def lo_upto(n):
                for g in range(done[0], n):
                    split_lo(g, 0)
                done[0] = max(done[0], n)

            def lo_tiles(c0, step, lo, hi):
                for g in range(c0 + lo, c0 + hi):
                    split_lo(g, step)

            def step(ins):
                count[0] += 1
                ins.then_inc(dve_step, 1)
                dve.wait_ge(dve_step, count[0])

            def fill_lo(F, hi, lo, k, gain=None):
                dve.wait_ge(tp_hi, F + 1)
                b = 4 + F % 4
                for i in range(2):
                    src = ps[:, b, i * SEQ:(i + 1) * SEQ]
                    h = hi[:, k + i, :].bitcast(F32)
                    if gain:
                        at = G_AT[gain[0]] + gain[1] + i
                        ins = dve.scalar_tensor_tensor(out=lo[:, k + i, :], in0=src, scalar=gains[:, at:at + 1],
                                                       in1=h, op0=ALU.mult, op1=ALU.subtract)
                    else:
                        ins = dve.tensor_tensor(lo[:, k + i, :], src, h, ALU.subtract)
                ins.then_inc(tp_free, 1)

            def mean_sq(name, width, src=None):
                dve.tensor_scalar(r_of(ms, name), r_of(ss, name) if src is None else src, 1.0 / width, EPS, ALU.mult,
                                  ALU.add).then_inc(ms_ready, 1)

            dve.memset(ones[:], 1.0).then_inc(consts_ready, 1)
            dve.memset(minus_half[:], -0.5).then_inc(consts_ready, 1)
            step(dve.memset(uT[:, :, 0:TAPS - 1], 0.0))
            dve.wait_ge(gains_ready, 1)
            for n in range(8):
                fill_lo(F_XT1 + n, hT_hi, hT_lo, 2 * n, ("pre_mix_norm", 2 * n))
                lo_upto(min(n + 3, 8))
            lo_upto(10)
            dve.wait_ge(sq_done, 1)
            mean_sq("x0", DM)
            lo_upto(12)

            TWO_PI = 2.0 * np.pi
            C1 = 6.28125
            C2 = float(np.float32(np.round((TWO_PI - C1) * 2 ** 21) / 2 ** 21))
            C3 = float(np.float32(TWO_PI - C1 - C2))
            ROUND = 12582912.0
            PI_IN = 3.1415925
            dve.wait_ge(params_landed, 16 * SMALL)
            dve.wait_ge(masks_ready, 1)
            dve.wait_ge(gains_ready, 3)
            step(dve.tensor_copy(posf[:, 0, :], kpe[:, 0, 0:TOK].bitcast(I32)))
            tt = [trig_t[:, i, :].rearrange("p (t n) -> p t n", t=TOK) for i in range(4)]
            for t in range(TOK):
                dve.tensor_scalar(tt[0][:, t, 0:32], invf[:, 0:32], posf[:, 0, t:t + 1], None, ALU.mult)
                ins = dve.tensor_scalar(tt[0][:, t, 32:96], invf[:, 32:96], posf[:, 1, t:t + 1], None, ALU.mult)
            step(ins)
            step(dve.tensor_scalar(tt[1], tt[0], float(1.0 / TWO_PI), None, ALU.mult))
            step(dve.tensor_scalar(tt[1], tt[1], ROUND, None, ALU.add))
            step(dve.tensor_scalar(tt[1], tt[1], -ROUND, None, ALU.add))
            lo_upto(14)
            for c in (C1, C2, C3):
                step(dve.scalar_tensor_tensor(out=tt[0], in0=tt[1], scalar=-c, in1=tt[0], op0=ALU.mult, op1=ALU.add))
            dve.tensor_scalar(tt[0], tt[0], PI_IN, -PI_IN, ALU.min, ALU.max).then_inc(trig_arg, 1)
            lo_upto(16)
            lo_upto(19)

            def gate_u(g):
                dve.wait_ge(gemm_free[1], g + 1)
                dve.tensor_tensor(a_s, a_s, sg_s, ALU.mult).then_inc(u_ready, 1)

            gate_u(0)
            lo_upto(23)
            dve.wait_ge(trig_abs, 1)
            dve.tensor_scalar(tt[2], tt[1], -1.0, float(np.pi / 2), ALU.mult, ALU.add).then_inc(trig_arg, 1)

            tap = [0]

            def taps(n):
                for _ in range(n):
                    i = tap[0]
                    if i == DVE_TAPS:
                        return
                    g = int(i >= TAPS * len(CONV_DVE[0]))
                    k = len(CONV_DVE[g])
                    j, c = divmod(i - g * TAPS * len(CONV_DVE[0]), k)
                    if j == 0 and c == 0:
                        dve.wait_ge(cu_free, 2 * g + 2)
                    c = CONV_DVE[g][c]
                    w = convw[:, j * CC + c:j * CC + c + 1]
                    u = uT[:, c, j:j + SEQ]
                    if j == 0:
                        b = G_AT["conv_b"] + c
                        ins = dve.tensor_scalar(cv[:, c, :], u, w, gains[:, b:b + 1], ALU.mult, ALU.add)
                    else:
                        dve.wait_ge(conv_tap, i - k + 1)
                        ins = dve.scalar_tensor_tensor(out=cv[:, c, :], in0=u, scalar=w, in1=cv[:, c, :],
                                                       op0=ALU.mult, op1=ALU.add)
                    ins.then_inc(conv_tap, 1)
                    tap[0] += 1

            for g in range(24, 36):
                lo_upto(g)
                taps(TILE_TAPS)
            gate_u(1)
            for g in range(36, 56):
                lo_upto(g)
                taps(TILE_TAPS)
            for n in range(3):
                fill_lo(F_LAT + n, latT_hi, latT_lo, 2 * n, ("q_norm", 2 * n))
            for g in range(56, 60):
                lo_upto(g)
                taps(TILE_TAPS)
            lo_upto(60)
            dve.wait_ge(sq_done, 2)
            at = R["lat"][0]
            dve.tensor_scalar(ms[:, at:at + 2], ss[:, at:at + 2], 1.0 / QL, EPS, ALU.mult, ALU.add)
            dve.tensor_scalar(ms[:, at + 2:at + 4], ss[:, at + 2:at + 4], 1.0 / KVL, EPS, ALU.mult,
                              ALU.add).then_inc(ms_ready, 1)
            lo_upto(62)
            for n in range(2):
                fill_lo(F_LAT + 3 + n, latT_hi, latT_lo, QC + 2 * n, ("kv_norm", 2 * n))
            def rope(dst, src, half, heads, at, tmp, sem_done):
                x1, x2 = src[:, :, :, 0:half], src[:, :, :, half:2 * half]
                cos, sin = (trig[:, :, i, at:at + half].unsqueeze(2).to_broadcast([P, TOK, heads, half]) for i in range(2))
                t1, t2 = tmp
                dve.tensor_tensor(t1, x1, cos, ALU.mult)
                step(dve.tensor_tensor(t2, x2, sin, ALU.mult))
                if heads > 1:
                    lo_upto(done[0] + 1)
                dve.tensor_tensor(dst[:, :, :, 0:half], t1, t2, ALU.subtract)
                step(dve.tensor_tensor(dst[:, :, :, half:2 * half], x2, cos, ALU.mult))
                step(dve.tensor_tensor(t1, x1, sin, ALU.mult))
                dve.tensor_tensor(dst[:, :, :, half:2 * half], dst[:, :, :, half:2 * half], t1, ALU.add).then_inc(sem_done, 1)

            tmp = [z1[:, :, 512 + 256 * i:768 + 256 * i].rearrange("p t (h n) -> p t h n", h=HEADS) for i in range(2)]
            for g in range(63, 77):
                lo_upto(g)
                taps(TILE_TAPS)
                if g == 65:
                    dve.wait_ge(trig_done, 1)
                    in_sbuf(dve, 6)
                    dve.wait_ge(tp_free, F_LAT + 5)
                    rope(kpe[:].unsqueeze(2), z1[:, :, QL + KVL:Z1].unsqueeze(2), 32, 1, 0,
                         [t[:, :, 0:1, :] for t in tmp], kpe_ready)
                if g == 68:
                    in_sbuf(dve, 8)
                    in_sbuf(dve, 9)
                    dve.wait_ge(kpe_ready, 1)
                    rope(z1[:, :, 0:512].rearrange("p t (h n) -> p t h n", h=HEADS),
                         q1[:].rearrange("p t (h n) -> p t h n", h=HEADS)[:, :, :, NOPE:QKH], 32, HEADS, 0, tmp, rope_ready)
            lo_upto(77)

            def attn1_max(h):
                b, e = 4 * ((h + 1) % 2), h % 2
                dve.wait_ge(at_S, h + 1)
                if h >= 2:
                    dve.wait_ge(at_PT, h - 1)
                step(dve.tensor_tensor(att1_s[:, e, :], ps[:, b + 2, 0:3 * P], mask1[:], ALU.add))
                dve.tensor_reduce(amax[:, e, 0, 0:1], att1_s[:, e, 0:P], X, ALU.max)
                step(dve.tensor_reduce(amax[:, e, 1, 0:1], att1_s[:, e, P:3 * P], X, ALU.max))
                dve.tensor_scalar(amax[:, e, :, 2:3], amax[:, e, :, 0:1], -float(QKH) ** -0.5, None,
                                  ALU.mult).then_inc(at_max, 1)

            def attn_out(h, h0, dst):
                b, e = 4 * ((h + 1) % 2), h % 2
                dve.wait_ge(at_PV, h0 + h + 1)
                dve.wait_ge(at_sum, h0 + h + 1)
                for t in range(TOK):
                    ins = dve.tensor_scalar(dst(t), ps[:, b + 3, t * P:(t + 1) * P], asum[:, e, 1, t:t + 1], None, ALU.mult)
                ins.then_inc(at_out, 1)

            for h in range(HEADS + 2):
                if h < HEADS:
                    attn1_max(h)
                if h >= 2:
                    attn_out(h - 2, 0, lambda t: attn1[:, t, (h - 2) * VD:(h - 1) * VD])
                if 1 <= h <= HEADS:
                    e = (h - 1) % 2
                    dve.wait_ge(at_exp, h)
                    dve.reciprocal(asum[:, e, 1, :], asum[:, e, 0, :]).then_inc(at_sum, 1)
                    taps(ATTN_TAPS)
            taps(TAPS * CC)
            for n in range(4):
                fill_lo(F_MIX1 + n, hT_hi, hT_lo, CC + 2 * n, ("attn_out_norm", 2 * n))
            dve.wait_ge(sq_done, 3)
            mean_sq("attn", CONV)
            lo_upto(T_OUT1 + 5)

            dve.wait_ge(ln_mm, 1)
            dve.wait_ge(conv_tap, DVE_TAPS)
            sums = ps[:, 4, 0:SEQ].unsqueeze(1).to_broadcast([P, CC, SEQ])
            dve.scalar_tensor_tensor(out=cv[:], in0=sums, scalar=-1.0 / CONV, in1=cv[:], op0=ALU.mult,
                                     op1=ALU.add).then_inc(ln_dve, 1)
            lo_upto(T_OUT1 + 8)
            dve.wait_ge(ln_mm, 2)
            mean_sq("ln", CONV, ps[:, 5, 0:TOK])
            dve.wait_ge(rstd_ready, r_count("ln"))
            for t in range(TOK):
                ins = dve.tensor_scalar(lnsq[:, 0, t * P:(t + 1) * P], ident[:], r_of(rstd, "ln", t, 1), None, ALU.mult)
            ins.then_inc(ln_dve, 1)
            lo_upto(T_OUT1 + 9)
            dve.wait_ge(ln_mm, 3)
            spread = ps[:, 4, 0:SEQ].unsqueeze(1).to_broadcast([P, CC, SEQ])
            dve.tensor_tensor(cv[:], spread, cv[:], ALU.mult).then_inc(ln_dve, 1)
            lo_upto(T_OUT1 + 13)
            for c in range(CC):
                g = G_AT["conv_out_norm"] + c
                if c == 4:
                    lo_upto(T_OUT1 + 14)
                if c % 2 == 0:
                    dve.wait_ge(conv_hi, c // 2 + 1)
                ins = dve.scalar_tensor_tensor(out=hT_lo[:, c, :], in0=cv[:, c, :], scalar=gains[:, g:g + 1],
                                               in1=hT_hi[:, c, :].bitcast(F32), op0=ALU.mult, op1=ALU.subtract)
                if c % 2 == 1:
                    ins.then_inc(mix_conv, 1)
            lo_upto(T_OUT1 + 15)
            dve.wait_ge(ln_mm, 4)
            mean_sq("conv", CONV, ps[:, 5, 0:TOK])
            lo_upto(T_OUT1 + 19)
            dve.wait_ge(rstd_ready, r_count("conv"))

            def conv_half(n):
                dve.wait_ge(tile_used, T_OUT1 + 16 + 4 * (n + 1))
                in_sbuf(dve, 14 + n)
                for t in range(TOK):
                    y = y_out[:, (2 * n + t) * NB:(2 * n + t + 1) * NB]
                    dve.scalar_tensor_tensor(out=y, in0=ps[:, 2 * (n % 2) + t, :], scalar=r_of(rstd, "conv", t, 1),
                                             in1=y, op0=ALU.mult, op1=ALU.add).then_inc(y_ready, 1)

            def times_gain(n):
                dve.wait_ge(row_sq, n + 1)
                y = y_out[:, 2 * n * NB:(2 * n + 2) * NB].rearrange("p (t n) -> p t n", t=TOK)
                dve.tensor_tensor(y, y, grow_out[:, cols(n)].unsqueeze(1).to_broadcast([P, TOK, NB]),
                                  ALU.mult).then_inc(row_y, 1)

            dve.wait_ge(grow_landed, 16)
            for n in range(4):
                lo_upto(T_OUT1 + 16 + 4 * n + 7)
                conv_half(n)
                if n > 0:
                    times_gain(n - 1)


            def row_scale(base, n, y, grow):
                dve.wait_ge(row_sq, base + 1 + n)
                for t in range(TOK):
                    ins = dve.tensor_tensor(
                        y[:, bass.ts(n, 2 * NB)].rearrange("p (k t c) -> p k t c", k=2, t=TOK)[:, :, t, :],
                        ps_flat[:, bass.ts(2 * n + t, NB)].rearrange("p (k c) -> p k c", k=2),
                        grow[:, cols(n)].rearrange("p (k c) -> p k c", k=2), ALU.mult)
                ins.then_inc(row_y, 1)

            def new_x(name, y, c_next, F, gain, last_gain):
                step(dve.tensor_reduce(r_of(ss, name), ss4.rearrange("p (t n) -> p t n", t=TOK), X, ALU.add))
                mean_sq(name, DM)
                last_gain()
                dve.wait_ge(rstd_ready, r_count(name))
                for n in range(9):
                    if n < 8:
                        for t in range(TOK):
                            x = x_sb[:, t, n * 2 * P:(n + 1) * 2 * P]
                            ins = dve.scalar_tensor_tensor(out=x, in0=y(t, n), scalar=r_of(rstd, name, t, 1), in1=x,
                                                           op0=ALU.mult, op1=ALU.add)
                        ins.then_inc(x_new, 1)
                    if n >= 1:
                        fill_lo(F + n - 1, hT_hi, hT_lo, 2 * n - 2, (gain, 2 * n - 2))
                        lo_upto(c_next + min(n + 2, 8))

            def last_gain():
                times_gain(3)
                dve.wait_ge(row_y, 4)

            dve.wait_ge(row_sq, 4)
            new_x("out1", lambda t, n: y_out[:, (n - n % 2 + t) * NB + n % 2 * 2 * P:][:, 0:2 * P], T_FF1,
                  F_XT2, "pre_ffn_norm", last_gain)

            lo_upto(T_FF1 + 10)
            dve.wait_ge(sq_done, 4)
            mean_sq("x1", DM)
            lo_upto(T_FF1 + 16)
            dve.wait_ge(rstd_ready, r_count("x1"))

            def product(j):
                dve.wait_ge(gemm_free[0], G_FF1 + 1 + j)
                dve.wait_ge(tile_used, T_FF1 + 16 + 16 * j)
                for t in range(TOK):
                    ins = dve.scalar_tensor_tensor(out=prod_s[:, t, :], in0=ps[:, 2 + t, :], scalar=r_of(rstd, "x1", t, 1),
                                                   in1=gate_s[:, t, :], op0=ALU.mult, op1=ALU.mult)
                ins.then_inc(gemm_free[1], 1)

            aT_hi_flat = aT_hi[:].rearrange("p c s -> p (c s)")
            aT_lo_flat = aT_lo[:].rearrange("p c s -> p (c s)")

            def turn_lo(j):
                for f in range(2):
                    dve.wait_ge(tp_hi, F_FF1 + f + 1 + 2 * j)
                    dve.tensor_tensor(aT_lo_flat[:, bass.ts(2 * j + f, 2 * SEQ)], ps[:, 4 + f, :],
                                      aT_hi_flat[:, bass.ts(2 * j + f, 2 * SEQ)].bitcast(F32),
                                      ALU.subtract).then_inc(tp_free, 1)

            with dve.Fori(1, FB) as j:
                lo_tiles(T_FF1, 16 * j, 0, 3)
                product(j - 1)
                lo_tiles(T_FF1, 16 * j, 3, 7)
                turn_lo(j - 1)
                lo_tiles(T_FF1, 16 * j, 7, 16)
            done[0] = T_DN1
            lo_upto(T_DN1 + 3)
            product(FB - 1)
            lo_upto(T_DN1 + 7)
            turn_lo(FB - 1)
            lo_upto(T_DN1 + 24)
            dve.wait_ge(grow_landed, 32)
            with dve.Fori(1, 4) as n:
                lo_tiles(T_DN1, 24 * n, 0, 3)
                row_scale(4, n - 1, y_dn, grow_dn)
                lo_tiles(T_DN1, 24 * n, 3, 24)
            done[0] = T_IN2
            lo_upto(T_IN2 + 3)
            dve.wait_ge(row_sq, 8)

            def last_gain():
                row_scale(4, 3, y_dn, grow_dn)
                dve.wait_ge(row_y, 8)

            new_x("dn1", lambda t, n: y_dn[:, (2 * n + t) * 2 * P:(2 * n + t + 1) * 2 * P], T_IN2, F_XT3, "norm1_g_2",
                  last_gain)
            dve.memset(lrT[:], 1.0).then_inc(consts_ready, 1)

            lo_upto(T_IN2 + 10)
            dve.wait_ge(sq_done, 5)
            mean_sq("x2", DM)
            lo_upto(T_IN2 + 19)
            dve.wait_ge(gl_mm, 2)
            for d in range(2):
                for t in range(TOK):
                    g = gb[:, 0, d, t * NB:(t + 1) * NB]
                    ins = dve.tensor_scalar(g, ps[:, 4 + 2 * d + t, :], -1.0, None, ALU.mult)
            step(ins)
            lo_upto(T_IN2 + 20)
            for d in range(2):
                for t in range(TOK):
                    g = gb[:, 0, d, t * NB:(t + 1) * NB]
                    ins = dve.tensor_tensor(g, ps[:, 4 + 2 * d + t, :], g, ALU.min)
            ins.then_inc(gl_dve, 1)
            lo_upto(T_IN2 + 23)
            dve.wait_ge(gl_act, 3)
            for d in range(2):
                for t in range(TOK):
                    g = gb[:, 0, d, t * NB:(t + 1) * NB]
                    ins = dve.scalar_tensor_tensor(out=g, in0=ps[:, 4 + 2 * d + t, :], scalar=0.0, in1=g,
                                                   op0=ALU.min, op1=ALU.subtract)
            ins.then_inc(gl_dve, 1)
            lo_upto(T_IN2 + 32)
            dve.wait_ge(gl_act, 4)
            for d in range(2):
                b = gb[:, 1, d, :].rearrange("p (g s) -> p g s", s=CHUNK)
                ref, last = (CHUNK // 2, CHUNK - 1) if d == 0 else (CHUNK // 2 - 1, 0)
                for i, r in ((0, ref), (3, last)):
                    ins = dve.tensor_tensor(fac[:, d, i].rearrange("p h (c s) -> p (h c) s", s=CHUNK), b,
                                            b[:, :, r:r + 1].to_broadcast([P, GH * NCH, CHUNK]), ALU.subtract)
                ins.then_inc(fac_diff, 1)
                lo_upto(T_IN2 + 33 + d)
            lo_upto(T_IN2 + 38)
            dve.wait_ge(gl_act, 5)
            for d in range(2):
                dve.wait_ge(fac_exp, d + 1)
                for i, src in enumerate((qT2, kT2, qT2, kT2)):
                    ins = dve.tensor_tensor(fac[:, d, i], fac[:, d, i], src[:], ALU.mult)
                    if i % 2 == 0:
                        lo_upto(done[0] + 1)
                ins.then_inc(fac_ready, 1)

            def gla_mask(h):
                dve.wait_ge(g_AT, h + 1)
                if h >= 1:
                    dve.wait_ge(g_O, h)
                for d in range(2):
                    ins = dve.copy_predicated(at_sb[:], gmask[:, d, :].unsqueeze(1).to_broadcast([P, TOK, P]),
                                              ps[:, 4, 2 * d * P:2 * (d + 1) * P].rearrange("p (t s) -> p t s", t=TOK))
                    if d == 0:
                        step(ins)
                ins.then_inc(g_at, 1)

            def gla_states(h, d):
                dve.wait_ge(g_SS, 2 * h + d + 1)
                if h >= 1:
                    dve.wait_ge(g_O, h)
                for n in range(3):
                    c = n if d == 0 else 3 - n
                    new = gla_sum(d, c)
                    if n == 0:
                        ins = dve.tensor_copy(state[:, d, 0, :], new)
                    else:
                        ins = dve.scalar_tensor_tensor(out=state[:, d, n, :], in0=state[:, d, n - 1, :],
                                                       scalar=decay[:, d, h * NCH + c:h * NCH + c + 1], in1=new,
                                                       op0=ALU.mult, op1=ALU.add)
                    if n < 2:
                        step(ins)
                ins.then_inc(g_st, 1)

            def gla_out(h):
                dve.wait_ge(g_O, h + 1)
                dve.tensor_copy(z2[:, :, QG + h * DV:QG + (h + 1) * DV], ps[:, 5, :].rearrange("p (t n) -> p t n", t=TOK))\
                   .then_inc(g_o, 1)

            def part_norm(part):
                name, h0, n, _, gain = QK_PARTS[part]
                dve.wait_ge(late_landed, 16 * 7)
                dve.wait_ge(rstd_ready, r_count(name))
                for t in range(TOK):
                    for h in range(n):
                        q = z2[:, t, (h0 + h) * HD:(h0 + h + 1) * HD]
                        ins = dve.scalar_tensor_tensor(out=q, in0=q, scalar=r_of(rstd, name, t * n + h, 1),
                                                       in1=gqk[:, gain, :], op0=ALU.mult, op1=ALU.mult)
                ins.then_inc(qk_normed, 1)

            step(dve.memset(at_sb[:], 0.0))
            for g in range(42, 80):
                h, k = gla_slot(g - 2)
                if k == 0 and 1 <= h <= GH:
                    gla_out(h - 1)
                if k == 0 and 0 <= h < GH:
                    gla_mask(h)
                if k in (2, 4) and 0 <= h < GH:
                    gla_states(h, k // 2 - 1)
                if g == 62:
                    dve.wait_ge(sq_done, 6)
                    mean_sq("k", HD)
                if g == 63:
                    part_norm(0)
                if g == 70:
                    dve.wait_ge(sq_done, 7)
                    mean_sq("qa", HD)
                if g == 71:
                    part_norm(1)
                if g == 74:
                    dve.wait_ge(sq_done, 8)
                    mean_sq("gla", DV)
                if g == 75:
                    dve.wait_ge(rstd_ready, r_count("gla"))
                if g in (75, 76):
                    for h in range(2 * (g - 75), 2 * (g - 75) + 2):
                        for t in range(TOK):
                            o = z2[:, t, QG + h * DV:QG + (h + 1) * DV]
                            ins = dve.scalar_tensor_tensor(out=o, in0=o, scalar=r_of(rstd, "gla", t * GH + h, 1),
                                                           in1=gla_g[:], op0=ALU.mult, op1=ALU.mult)
                    step(ins)
                if g in (77, 78):
                    dve.wait_ge(gate2_ready, 1)
                    for h in range(2 * (g - 77), 2 * (g - 77) + 2):
                        o = z2[:, :, QG + h * DV:QG + (h + 1) * DV]
                        dve.tensor_tensor(o, o, z2[:, :, GG + h * DV:GG + (h + 1) * DV], ALU.mult).then_inc(mix2_ready, 1)
                lo_upto(T_IN2 + g + 1)

            def split_rest(F, pair_at, bank):
                dve.wait_ge(tp_hi, F + 1)
                dve.tensor_tensor(hT_lo[:, 2 * pair_at:2 * pair_at + 2, :], ps[:, bank, :].rearrange("p (c s) -> p c s", c=2),
                                  hT_hi[:, 2 * pair_at:2 * pair_at + 2, :].bitcast(F32), ALU.subtract).then_inc(tp_free, 1)

            def half_add(end, b, sem_done):
                dve.wait_ge(tile_used, end)
                x = x_sb[:, :, cols(b)]
                p = 2 * (b % 2)
                dve.tensor_tensor(x, ps[:, p:p + 2, :], x, ALU.add).then_inc(sem_done, 1)

            for g in range(32):
                if 0 <= g - 2 - (MIX_FILL - 80) < 4:
                    n = g - 2 - (MIX_FILL - 80)
                    split_rest(F_MIX2 + n, 4 + n, 4 + (F_MIX2 + n) % 4)
                i = (g - 3) // 2
                if g % 2 == 1 and 0 <= i < HEADS:
                    e, h = i % 2, HEAD_ORDER[i]
                    dve.wait_ge(at_S, HEADS + i + 1)
                    if i >= 2:
                        dve.wait_ge(at_out, HEADS + i - 1)
                    step(dve.tensor_tensor(ps[:, 5, P:3 * P], ps[:, 5, P:3 * P], mask2[:, P:3 * P], ALU.add))
                    step(dve.tensor_reduce(amax[:, e, :, 0:1], ps[:, 5, :].rearrange("p (t s) -> p t s", t=TOK), X, ALU.max))
                    step(dve.tensor_scalar(amax[:, e, :, 1:2], amax[:, e, :, 0:1], float(HD) ** -0.5, sinkb[:, h:h + 1],
                                           ALU.mult, ALU.max))
                    dve.tensor_scalar(amax[:, e, :, 2:3], amax[:, e, :, 1:2], -1.0, None, ALU.mult).then_inc(at_max, 1)
                i = (g - 4) // 2
                if g % 2 == 0 and 0 <= i < HEADS:
                    e = i % 2
                    dve.wait_ge(at_exp, HEADS + i + 1)
                    step(dve.tensor_tensor(asum[:, e, 1, :], asum[:, e, 0, :], amax[:, e, :, 3], ALU.add))
                    dve.reciprocal(asum[:, e, 1, :], asum[:, e, 1, :]).then_inc(at_sum, 1)
                if g in (4, 5):
                    dve.wait_ge(sq_done, 5 + g)
                    mean_sq("qb" if g == 4 else "qc", HD)
                if g in (5, 6):
                    part_norm(g - 3)
                if g % 4 == 1 and 0 <= (g - 9) // 4 < 4:
                    p = (g - 9) // 4
                    split_rest(F_MIX2 + 4 + p, PAIR_ORDER[p], 4)
                if g % 4 == 2 and 1 <= g // 4 <= 4:
                    half_add(T_OUT2 + 4 * (g // 4), g // 4 - 1, half_added)
                if g == 24:
                    half_add(T_OUT2 + 23, 2, x_new)
                if g == 26:
                    half_add(T_OUT2 + 24, 3, x_new)
                if g == 30:
                    half_add(T_OUT2 + 28, 0, x_new)
                if g >= 29:
                    fill_lo(F_XT4 + g - 29, hT_hi, hT_lo, 2 * XT4_ORDER[g - 29], ("norm2_g_2", 2 * XT4_ORDER[g - 29]))
                lo_upto(T_OUT2 + g + 1)
            fill_lo(F_XT4 + 3, hT_hi, hT_lo, 2 * XT4_ORDER[3], ("norm2_g_2", 2 * XT4_ORDER[3]))
            lo_upto(T_FF2 + 1)
            half_add(T_OUT2 + 32, 1, x_new)

            def row_add(c_end, step_, n, sem_done):
                dve.wait_ge(tile_used, c_end + step_)
                for t in range(TOK):
                    ins = dve.tensor_tensor(x_sb[:, t, cols(n)], ps_flat[:, bass.ts(2 * n + t, NB)], x_sb[:, t, cols(n)],
                                            ALU.add)
                ins.then_inc(sem_done, 1)

            for n in range(4, 8):
                lo_upto(T_FF2 + n - 1)
                fill_lo(F_XT4 + n, hT_hi, hT_lo, 2 * XT4_ORDER[n], ("norm2_g_2", 2 * XT4_ORDER[n]))
            lo_upto(T_FF2 + 10)
            dve.wait_ge(sq_done, 11)
            mean_sq("x3", DM)
            lo_upto(T_FF2 + 16)

            def taps2(j, half):
                dst = cg if half == 0 else cval
                n = 0
                for f in range(2):
                    dve.wait_ge(ct_center, 4 * j + 2 * half + f + 1)
                    for c in range(2 * f, 2 * f + 2):
                        k = 4 * j + c + FC * half
                        src = ps[:, 4 + 2 * half + f, (c % 2) * SEQ:(c % 2 + 1) * SEQ]
                        ins = dve.scalar_tensor_tensor(out=dst[:, c, 1:SEQ], in0=src[:, 0:SEQ - 1],
                                                       scalar=conv2[:, 0, bass.ts(k, 1)], in1=dst[:, c, 1:SEQ],
                                                       op0=ALU.mult, op1=ALU.add)
                        ins.then_inc(conv2_step, 1)
                    for c in range(2 * f, 2 * f + 2):
                        k = 4 * j + c + FC * half
                        src = ps[:, 4 + 2 * half + f, (c % 2) * SEQ:(c % 2 + 1) * SEQ]
                        dve.wait_ge(conv2_step, 8 * j + 4 * half + c + 1)
                        ins = dve.scalar_tensor_tensor(out=dst[:, c, 0:SEQ - 1], in0=src[:, 1:SEQ],
                                                       scalar=conv2[:, 2, bass.ts(k, 1)], in1=dst[:, c, 0:SEQ - 1],
                                                       op0=ALU.mult, op1=ALU.add)
                ins.then_inc(ct_free, 1)

            def product2(j):
                dve.wait_ge(cg_silu, j + 1)
                dve.wait_ge(ct_free, 2 * j + 2)
                dve.tensor_tensor(cg[:], cg[:], cval[:], ALU.mult).then_inc(prod_ready, 1)

            def hidden_lo(j):
                dve.wait_ge(aT_hi_ready, j + 1)
                dve.tensor_tensor(aT_lo_flat[:, bass.ts(j, 4 * SEQ)], cg[:].rearrange("p c s -> p (c s)"),
                                  aT_hi_flat[:, bass.ts(j, 4 * SEQ)].bitcast(F32), ALU.subtract).then_inc(aT_ready, 1)

            taps2(0, 0)
            with dve.Fori(1, FB) as j:
                lo_tiles(T_FF2, 16 * j, 0, 8)
                taps2(j - 1, 1)
                product2(j - 1)
                lo_tiles(T_FF2, 16 * j, 8, 12)
                hidden_lo(j - 1)
                lo_tiles(T_FF2, 16 * j, 12, 16)
                taps2(j, 0)
            done[0] = T_DN2
            lo_upto(T_DN2 + 8)
            taps2(FB - 1, 1)
            product2(FB - 1)
            lo_upto(T_DN2 + 12)
            hidden_lo(FB - 1)
            lo_upto(T_DN2 + 24)
            with dve.Fori(1, 4) as n:
                lo_tiles(T_DN2, 24 * n, 0, 3)
                row_add(T_DN2, 24 * n, n - 1, row_y)
                lo_tiles(T_DN2, 24 * n, 3, 24)
            row_add(T_END, 0, 3, row_y)


_INS = ["x", "positions", "pre_mix_norm", "w_in", "q_norm", "w_uq", "kv_norm", "w_ukv", "conv_w", "conv_b",
        "conv_ln_g", "conv_ln_b", "conv_out_norm", "attn_out_norm", "w_out", "post_mix_norm", "pre_ffn_norm",
        "w_gate", "w_up", "w_down", "post_ffn_norm", "norm1_g_2", "w_in_2", "attn_q_norm_g_2",
        "attn_k_norm_g_2", "attn_sink_2", "gla_wa2_fwd_2", "gla_ba_fwd_2", "gla_wa2_bwd_2", "gla_ba_bwd_2",
        "gla_out_norm_g_2", "w_out_2", "norm2_g_2", "w_up_2", "conv_w_2", "conv_b_2", "w_down_2"]


def inverse_frequencies():
    f = np.float32
    one = f(THETA) ** (-np.arange(0, ROPE, 2, dtype=f) / f(ROPE))
    two = f(1.0) / (f(THETA) ** (np.arange(HD // 2, dtype=f) / f(HD // 2)))
    return np.concatenate([one, two]).astype(f)[None, :]


def kernel(**inputs):
    import concourse.bacc as _bacc
    from concourse.bass_utils import run_bass_kernel_spmd as _run

    nc = _bacc.Bacc("TRN2", target_bir_lowering=False, num_devices=1)
    arrays = {f"in_{name}": np.ascontiguousarray(inputs[name]) for name in _INS}
    arrays["in_inv_freq"] = inverse_frequencies()
    aps = {name[3:]: nc.dram_tensor(name, v.shape, mybir.dt.from_np(v.dtype), kind="ExternalInput").ap()
           for name, v in arrays.items()}
    out = nc.dram_tensor("out_0", (1, SEQ, DM), F32, kind="ExternalOutput").ap()
    build(nc, aps, out)
    r = _run(nc, [arrays], core_ids=[0])
    return r.results[0]["out_0"]
```
